# Optimizing a Trainium2 kernel written in Bass

```python
import math
import jax, jax.numpy as jnp
from jax import lax
import numpy as np

D_MODEL = 1024
BATCH = 1
SEQ = 1024
DEPTH = 1
DEC_BATCH = 8
DEC_SEQ = 1
PAST_LEN = 8192
PAGE_SIZE = 128

MIX_WIDTH = D_MODEL
SSM_WIDTH = MIX_WIDTH // 2
CONV_WIDTH = MIX_WIDTH - SSM_WIDTH
SSM_GROUP = 16
N_SSM_GROUPS = SSM_WIDTH // SSM_GROUP
SSM_STATE = 64
CONV_K = 3
CONV_HEADS = 8
D_FF = 2816
IN_PROJ_WIDTH = SSM_WIDTH + 3 * CONV_WIDTH
EPS = 1e-6
DT_MIN = 1e-3
DT_MAX = 1e-1

kernel_name = "hymba_s5_shortconv_macaron_step"

def rmsnorm(x, g):
    xf = x.astype(jnp.float32)
    r = lax.rsqrt(jnp.mean(xf * xf, axis=-1, keepdims=True) + EPS)
    return (xf * r * g.astype(jnp.float32)).astype(x.dtype)

def swiglu(x, w_gate, w_up, w_down):
    return (jax.nn.silu(x @ w_gate) * (x @ w_up)) @ w_down

def s5_discretize(lam_re, lam_im, log_dt, b_re, b_im):
    f32 = jnp.float32
    dt = jnp.exp(log_dt.astype(f32))[:, None]
    lr = lam_re.astype(f32)
    li = lam_im.astype(f32)
    mag = jnp.exp(lr * dt)
    ab_re = mag * jnp.cos(li * dt)
    ab_im = mag * jnp.sin(li * dt)
    den = lr * lr + li * li
    nr = ab_re - 1.0
    ni = ab_im
    coef_re = ((nr * lr + ni * li) / den)[..., None]
    coef_im = ((ni * lr - nr * li) / den)[..., None]
    br = b_re.astype(f32)
    bi = b_im.astype(f32)
    bb_re = coef_re * br - coef_im * bi
    bb_im = coef_re * bi + coef_im * br
    return ab_re, ab_im, bb_re, bb_im

def _complex_affine_combine(e1, e2):
    a1r, a1i, b1r, b1i = e1
    a2r, a2i, b2r, b2i = e2
    return (a1r * a2r - a1i * a2i,
            a1r * a2i + a1i * a2r,
            a2r * b1r - a2i * b1i + b2r,
            a2r * b1i + a2i * b1r + b2i)

def s5_mixer(u, h0_re, h0_im, lam_re, lam_im, log_dt, b_re, b_im, c_re, c_im, d_skip, w_glu, b_glu):
    f32 = jnp.float32
    bsz, seq_len, _ = u.shape
    uf = u.astype(f32)
    ug = uf.reshape(bsz, seq_len, N_SSM_GROUPS, SSM_GROUP)
    ab_re, ab_im, bb_re, bb_im = s5_discretize(lam_re, lam_im, log_dt, b_re, b_im)
    bu_re = jnp.einsum('blgc,gpc->blgp', ug, bb_re)
    bu_im = jnp.einsum('blgc,gpc->blgp', ug, bb_im)
    h0r = h0_re.astype(f32)
    h0i = h0_im.astype(f32)
    bu_re = bu_re.at[:, 0].add(ab_re * h0r - ab_im * h0i)
    bu_im = bu_im.at[:, 0].add(ab_re * h0i + ab_im * h0r)
    a_re = jnp.broadcast_to(ab_re, bu_re.shape)
    a_im = jnp.broadcast_to(ab_im, bu_im.shape)
    _, _, x_re, x_im = lax.associative_scan(_complex_affine_combine, (a_re, a_im, bu_re, bu_im), axis=1)
    y = (jnp.einsum('blgp,gcp->blgc', x_re, c_re.astype(f32))
         - jnp.einsum('blgp,gcp->blgc', x_im, c_im.astype(f32)))
    y = y.reshape(bsz, seq_len, SSM_WIDTH) + d_skip.astype(f32) * uf
    z = jax.nn.gelu(y)
    out = z * jax.nn.sigmoid(z @ w_glu.astype(f32) + b_glu.astype(f32))
    return out.astype(u.dtype), x_re[:, -1], x_im[:, -1]

def short_conv_mixer(x_in, gate_b, gate_c, buf, conv_w):
    seq_len = x_in.shape[1]
    v = gate_c * x_in
    vp = jnp.concatenate([buf.astype(v.dtype), v], axis=1)
    z = conv_w[0] * vp[:, 0:seq_len]
    for k in range(1, CONV_K):
        z = z + conv_w[k] * vp[:, k:k + seq_len]
    return gate_b * z, vp[:, -(CONV_K - 1):]

def decoder_layer(x, h_re, h_im, conv_buf,
                  ffn1_norm, ffn1_w_gate, ffn1_w_up, ffn1_w_down,
                  mix_norm, w_in,
                  ssm_lambda_re, ssm_lambda_im, ssm_log_dt, ssm_b_re, ssm_b_im,
                  ssm_c_re, ssm_c_im, ssm_d, ssm_w_glu, ssm_b_glu,
                  conv_w, w_out,
                  ffn2_norm, ffn2_w_gate, ffn2_w_up, ffn2_w_down):
    h = x + 0.5 * swiglu(rmsnorm(x, ffn1_norm), ffn1_w_gate, ffn1_w_up, ffn1_w_down)
    p = rmsnorm(h, mix_norm) @ w_in
    u = p[..., :SSM_WIDTH]
    x_conv = p[..., SSM_WIDTH:SSM_WIDTH + CONV_WIDTH]
    gate_b = p[..., SSM_WIDTH + CONV_WIDTH:SSM_WIDTH + 2 * CONV_WIDTH]
    gate_c = p[..., SSM_WIDTH + 2 * CONV_WIDTH:]
    s_out, new_re, new_im = s5_mixer(u, h_re, h_im, ssm_lambda_re, ssm_lambda_im, ssm_log_dt,
                                     ssm_b_re, ssm_b_im, ssm_c_re, ssm_c_im, ssm_d, ssm_w_glu, ssm_b_glu)
    c_out, new_buf = short_conv_mixer(x_conv, gate_b, gate_c, conv_buf, conv_w)
    h = h + jnp.concatenate([s_out, c_out.astype(s_out.dtype)], axis=-1) @ w_out
    h = h + 0.5 * swiglu(rmsnorm(h, ffn2_norm), ffn2_w_gate, ffn2_w_up, ffn2_w_down)
    return h, new_re, new_im, new_buf

def setup_inputs(seed: int = 0) -> dict:
    key = jax.random.key(seed)
    ks = jax.random.split(key, 40)
    f32 = jnp.float32

    def nrm(k, shape, scale):
        return scale * jax.random.normal(k, shape, f32)

    n_idx = jnp.arange(SSM_STATE, dtype=f32)
    gp = (DEPTH, N_SSM_GROUPS, SSM_STATE)
    return {
        "x_prompt": nrm(ks[0], (BATCH, SEQ, D_MODEL), 1.0),
        "x_sample": nrm(ks[1], (DEC_BATCH, DEC_SEQ, D_MODEL), 1.0),
        "state_ssm_re": nrm(ks[2], (DEPTH, DEC_BATCH, N_SSM_GROUPS, SSM_STATE), 0.1),
        "state_ssm_im": nrm(ks[3], (DEPTH, DEC_BATCH, N_SSM_GROUPS, SSM_STATE), 0.1),
        "state_conv": nrm(ks[4], (DEPTH, DEC_BATCH, CONV_K - 1, CONV_WIDTH), 1.0),
        "ffn1_norm": 1.0 + nrm(ks[5], (DEPTH, D_MODEL), 0.02),
        "ffn1_w_gate": nrm(ks[6], (DEPTH, D_MODEL, D_FF), D_MODEL ** -0.5),
        "ffn1_w_up": nrm(ks[7], (DEPTH, D_MODEL, D_FF), D_MODEL ** -0.5),
        "ffn1_w_down": nrm(ks[8], (DEPTH, D_FF, D_MODEL), D_FF ** -0.5),
        "mix_norm": 1.0 + nrm(ks[9], (DEPTH, D_MODEL), 0.02),
        "w_in": nrm(ks[10], (DEPTH, D_MODEL, IN_PROJ_WIDTH), D_MODEL ** -0.5),
        "ssm_lambda_re": -0.5 + nrm(ks[11], gp, 0.01),
        "ssm_lambda_im": math.pi * n_idx + nrm(ks[12], gp, 0.01),
        "ssm_log_dt": jax.random.uniform(ks[13], (DEPTH, N_SSM_GROUPS), f32,
                                         minval=math.log(DT_MIN), maxval=math.log(DT_MAX)),
        "ssm_b_re": nrm(ks[14], (DEPTH, N_SSM_GROUPS, SSM_STATE, SSM_GROUP), (2 * SSM_GROUP) ** -0.5),
        "ssm_b_im": nrm(ks[15], (DEPTH, N_SSM_GROUPS, SSM_STATE, SSM_GROUP), (2 * SSM_GROUP) ** -0.5),
        "ssm_c_re": nrm(ks[16], (DEPTH, N_SSM_GROUPS, SSM_GROUP, SSM_STATE), SSM_STATE ** -0.5),
        "ssm_c_im": nrm(ks[17], (DEPTH, N_SSM_GROUPS, SSM_GROUP, SSM_STATE), SSM_STATE ** -0.5),
        "ssm_d": nrm(ks[18], (DEPTH, SSM_WIDTH), 1.0),
        "ssm_w_glu": nrm(ks[19], (DEPTH, SSM_WIDTH, SSM_WIDTH), SSM_WIDTH ** -0.5),
        "ssm_b_glu": nrm(ks[20], (DEPTH, SSM_WIDTH), 0.02),
        "conv_w": nrm(ks[21], (DEPTH, CONV_K, CONV_WIDTH), CONV_K ** -0.5),
        "w_out": nrm(ks[22], (DEPTH, MIX_WIDTH, D_MODEL), MIX_WIDTH ** -0.5),
        "ffn2_norm": 1.0 + nrm(ks[23], (DEPTH, D_MODEL), 0.02),
        "ffn2_w_gate": nrm(ks[24], (DEPTH, D_MODEL, D_FF), D_MODEL ** -0.5),
        "ffn2_w_up": nrm(ks[25], (DEPTH, D_MODEL, D_FF), D_MODEL ** -0.5),
        "ffn2_w_down": nrm(ks[26], (DEPTH, D_FF, D_MODEL), D_FF ** -0.5),
        "final_norm": 1.0 + nrm(ks[27], (D_MODEL,), 0.02),
    }

def reference(x_prompt, x_sample, state_ssm_re, state_ssm_im, state_conv,
              ffn1_norm, ffn1_w_gate, ffn1_w_up, ffn1_w_down,
              mix_norm, w_in,
              ssm_lambda_re, ssm_lambda_im, ssm_log_dt, ssm_b_re, ssm_b_im,
              ssm_c_re, ssm_c_im, ssm_d, ssm_w_glu, ssm_b_glu,
              conv_w, w_out,
              ffn2_norm, ffn2_w_gate, ffn2_w_up, ffn2_w_down,
              final_norm):
    n_prompt = x_prompt.shape[0]
    hp = x_prompt
    hs = x_sample
    p_re, p_im, p_conv, s_re, s_im, s_conv = [], [], [], [], [], []
    for l in range(DEPTH):
        lw = (ffn1_norm[l], ffn1_w_gate[l], ffn1_w_up[l], ffn1_w_down[l],
              mix_norm[l], w_in[l],
              ssm_lambda_re[l], ssm_lambda_im[l], ssm_log_dt[l], ssm_b_re[l], ssm_b_im[l],
              ssm_c_re[l], ssm_c_im[l], ssm_d[l], ssm_w_glu[l], ssm_b_glu[l],
              conv_w[l], w_out[l],
              ffn2_norm[l], ffn2_w_gate[l], ffn2_w_up[l], ffn2_w_down[l])
        zero_h = jnp.zeros((n_prompt, N_SSM_GROUPS, SSM_STATE), jnp.float32)
        zero_buf = jnp.zeros((n_prompt, CONV_K - 1, CONV_WIDTH), x_prompt.dtype)
        hp, r_p, i_p, b_p = decoder_layer(hp, zero_h, zero_h, zero_buf, *lw)
        hs, r_s, i_s, b_s = decoder_layer(hs, state_ssm_re[l], state_ssm_im[l], state_conv[l], *lw)
        p_re.append(r_p); p_im.append(i_p); p_conv.append(b_p)
        s_re.append(r_s); s_im.append(i_s); s_conv.append(b_s)
    y_prompt = rmsnorm(hp, final_norm)
    y_sample = rmsnorm(hs, final_norm)
    new_ssm_re_prompt = jnp.stack(p_re, axis=0)
    new_ssm_im_prompt = jnp.stack(p_im, axis=0)
    new_conv_prompt = jnp.stack(p_conv, axis=0)
    new_ssm_re_sample = jnp.stack(s_re, axis=0)
    new_ssm_im_sample = jnp.stack(s_im, axis=0)
    new_conv_sample = jnp.stack(s_conv, axis=0)
    return (y_prompt, y_sample, new_ssm_re_prompt, new_ssm_im_prompt, new_conv_prompt,
            new_ssm_re_sample, new_ssm_im_sample, new_conv_sample)


_drawn_inputs = setup_inputs


def setup_inputs(seed=0):
    import zlib

    import numpy as np

    out = dict(_drawn_inputs(seed))
    spreads = {}
    factors = {'ffn1_norm': 4.713,
     'ssm_lambda_re': 67.532,
     'ssm_c_re': 13.606,
     'ssm_c_im': 13.796,
     'ssm_b_glu': 171.934,
     'ffn2_norm': 8.0,
     'final_norm': 30.046,
     'ssm_w_glu': 4.26}
    for name, (base, spread) in spreads.items():
        noise = np.random.default_rng([zlib.crc32(name.encode()), seed]).standard_normal(out[name].shape)
        drawn = base * np.exp(spread * noise) if base else spread * noise
        out[name] = __import__('jax').numpy.asarray(drawn.astype(out[name].dtype))
    for name, factor in factors.items():
        out[name] = (out[name] * factor).astype(out[name].dtype)
    return out
```

```python
from contextlib import ExitStack

import numpy as np

import concourse.bass as bass
from concourse import mybir

F32 = mybir.dt.float32
F32R = mybir.dt.float32r
ALU = mybir.AluOpType
ACT = mybir.ActivationFunctionType

P = 128
D = 1024
DC = D // P
SEQ = 1024
DEC = 8
S8 = 8
NK = SEQ // S8
NT = SEQ + DEC
TB = 3
TW = NT // TB
FF = 2816
NF = FF // P
W = 512
WC = W // P
G = 32
GP = G // 2
C16 = 16
NS = 64
EPS = 1e-6
UC = DEC + NK + DEC
XC = DEC + 1 + NK + DEC
YC = DEC + NK
MAGIC = 12582912.0
TWO_PI = 2 * np.pi
PI_A = 6.28125
PI_B = round((TWO_PI - PI_A) * 2**19) / 2**19
PI_C = TWO_PI - PI_A - PI_B


class Unit:

    def __init__(self, slot, before):
        self.slot, self.before = slot, before

    def full(self, bank):
        return 3 * self.before + bank + 1

    def at(self, step):
        return Unit(self.slot, self.before + step)


def plan():
    units, used, weights, loaded = {}, [0, 0], {}, [0, 0, 0]

    def add(name, slot, weighted=False, times=1):
        units[name] = Unit(slot, used[slot])
        used[slot] += times
        if weighted:
            weights[name] = loaded[slot]
            loaded[slot] += times

    for n in range(12):
        add(("x", n), n % 2)
    add("params", 0)
    add("gate1", 0, True, NF)
    add("up1", 1, True, NF)
    add("norm2", 1)
    for j in range(WC):
        add(("u", j), j % 2, True)
    for n in range(4):
        add(("tab", n), n % 2)
    add("carried", 0)
    add("buffer", 1)
    n = 0
    for c in range(WC):
        for what in ("xc", "gc", "gb"):
            add((what, c), n % 2, True)
            n += 1
        if c == 0:
            for v in range(4):
                add(("v", v), (n + v) % 2)
    for j in range(4):
        add(("y", j), j % 2)
    add("states", 0)
    add("vout", 1)
    for j in range(WC):
        add(("glu", j), j % 2, True)
    add("norm3", 0)
    add("gate2", 0, True, NF)
    add("up2", 1, True, NF)
    for s in range(S8 + 1):
        add(("out", s), s % 2)
    return units, weights


UNITS, WEIGHTS = plan()
WEIGHTED = [("u", j) for j in range(WC)]
for _c in range(WC):
    WEIGHTED += [("xc", _c), ("gc", _c), ("gb", _c)]
WEIGHTED += [("glu", j) for j in range(WC)]

DOWN1, DOWNC, DOWNS, DOWN2 = 0, NF, NF + WC, NF + 2 * WC
ND = 2 * NF + 2 * WC
TILES = TB * DC

V_ITEMS = 2 * GP
V_BANKS = [list(range(b, min(b + 3, V_ITEMS))) for b in range(0, V_ITEMS, 3)]
Y_BANKS = [[0, 1, 2], [3, 4, 5], [6, 7]]


def hybrid_trunk(nc, a, o):
    ctx = ExitStack()

    def sb(name, shape, dt=F32, stack=ctx):
        return stack.enter_context(nc.sbuf_tensor(name, shape, dt))

    def sem(name):
        return ctx.enter_context(nc.semaphore(name))

    def dram(name, shape):
        return nc.dram_tensor(name, shape, F32, kind="Internal").ap()

    with ctx:
        HT = sb("HT", [P, DC, NT])
        RAW = sb("RAW", [P, 3, D])
        WH = sb("WH", [P, 3, D], F32R)
        WL = sb("WL", [P, 3, D], F32R)
        IDENT = sb("IDENT", [P, P])
        ONES = sb("ONES", [P, P])
        S = sb("S", [P, NT])
        T = sb("T", [P, NT])
        GAIN = sb("GAIN", [P, 3, DC])
        EPSC = sb("EPSC", [P, 1])
        CW = sb("CW", [P, 3, WC])
        BG = sb("BG", [P, WC])
        CBT = sb("CBT", [P, WC, 2 * DEC])
        VOUT = sb("VOUT", [P, WC, 16])
        SS = sb("SS", [P, S8 + 1, 2])
        RS = sb("RS", [P, S8 + 1])
        LRI = sb("LRI", [P, 3, GP])
        TMP = sb("TMP", [P, 14, GP])
        AP8 = sb("AP8", [P, S8, 3, GP])
        DT = sb("DT", [32, GP])
        DM = sb("DM", [32, C16])
        st = ExitStack()
        DR = sb("DR", [P, S8 + 1, P], F32, st)
        st.close()
        WT = sb("WT", [P, GP, 2, P], F32, st)
        st.close()
        HH = sb("HH", [P, 2, NT], F32R)
        HL = sb("HL", [P, 2, NT], F32R)
        st = ExitStack()
        CL = sb("CL", [P, 2, 4, P], F32, st)
        st.close()
        PROD = sb("PROD", [P, 2, GP, C16], F32, st)
        st.close()
        CARR = sb("CARR", [P, 2, P], F32, st)
        CBUF = sb("CBUF", [16, W], F32, st)
        st.close()
        R = sb("R", [P, NT])
        V = R
        st = ExitStack()
        BRAW = sb("BRAW", [P, 2, GP, C16], F32, st)
        PAR = sb("PAR", [96, P], F32, st)
        st.close()
        ST1 = sb("ST1", [P, 2, GP, GP], F32, st)
        ST2 = sb("ST2", [P, 2, GP, GP], F32, st)
        st.close()
        SQ = sb("SQ", [P, NT])
        st = ExitStack()
        T0 = sb("T0", [P, GP, 2, P], F32, st)
        CB = sb("CB", [P, GP, 2, 2, P], F32, st)
        Z = sb("Z", [P, 2, 8, YC], F32, st)
        st.close()
        ZH = sb("ZH", [P, WC, NT], F32R, st)
        ZL = sb("ZL", [P, WC, NT], F32R, st)
        st.close()
        XH = sb("XH", [P, DC, NT], F32R)
        XL = sb("XL", [P, DC, NT], F32R)
        st = ExitStack()
        X = sb("X", [P, S8, D], F32, st)
        st.close()
        CA = sb("CA", [P, GP, 2, 9 * C16], F32, st)
        BD = sb("BD", [P, GP, 2, 2 * C16], F32, st)
        BS = sb("BS", [P, GP, 2, P], F32, st)
        st.close()
        sb("over_CA", [P, GP, 2, 9 * C16], F32, st)
        sb("over_BD", [P, GP, 2, 2 * C16], F32, st)
        KT = sb("KT", [32, GP, 15 * C16], F32, st)
        DTM = sb("DTM", [32, C16], F32, st)
        st.close()
        U = sb("U", [P, G, UC], F32, st)
        XS = sb("XS", [P, 2 * GP, XC], F32, st)
        VPRE = sb("VPRE", [P, 2, NK], F32, st)
        DNEW = sb("DNEW", [P, 2, P], F32, st)
        st.close()
        ZT = sb("ZT", [P, WC, NT], F32, st)
        STO = sb("STO", [P, 4, P], F32, st)
        VO = sb("VO", [16, W], F32, st)
        st.close()
        OUT = sb("OUT", [P, 2, D], F32, st)
        GF = sb("GF", [P, D], F32, st)
        st.close()

        AB = [[ctx.enter_context(nc.psum_tensor(f"bank{s}{b}", [P, 512], F32)) for b in range(3)] for s in range(2)]
        DB = [ctx.enter_context(nc.psum_tensor(f"bank_down{b}", [P, 512], F32)) for b in range(2)]

        UD = dram("u_scratch", [W, NT])
        ZD = dram("z_scratch", [W, NT])
        CAD = dram("ca_scratch", [P, GP * 2, 9 * C16])
        T0D = dram("t0_scratch", [P, GP, 2, P])

        banks_full = [sem("banks_full_0"), sem("banks_full_1")]
        banks_free = [sem("banks_free_0"), sem("banks_free_1")]
        raw_full = [sem(f"raw_full_{s}") for s in range(3)]
        w_hi = [sem(f"w_hi_{s}") for s in range(3)]
        w_split = [sem(f"w_split_{s}") for s in range(3)]
        hi_done = sem("hi_done")
        h_ready = sem("h_ready")
        down_full = sem("down_full")
        down_free = sem("down_free")
        gate_done = sem("gate_done")
        x_in = [sem(f"x_in_{s}") for s in range(S8 + 1)]
        sq_x = sem("sq_x")
        sqrt_x = sem("sqrt_x")
        ss_sum = sem("ss_sum")
        rcp_x = sem("rcp_x")
        diag_x = sem("diag_x")
        ht_ready = sem("ht_ready")
        xn_hi = sem("xn_hi")
        xn_ready = sem("xn_ready")
        xn_tmp = sem("xn_tmp")
        sq_done = sem("sq_done")
        sums_done = sem("sums_done")
        rt_done = sem("rt_done")
        r_done = sem("r_done")
        const_done = sem("const_done")
        consts_in = sem("consts_in")
        c_in = sem("c_in")
        b_in = sem("b_in")
        par_in = sem("par_in")
        dt_in = sem("dt_in")
        par_set = sem("par_set")
        lri_done = sem("lri_done")
        c_done = sem("c_done")
        disc_a = sem("disc_a")
        disc_p = sem("disc_p")
        den_inv = sem("den_inv")
        pool_step = sem("pool_step")
        ca_out = sem("ca_out")
        kt_done = sem("kt_done")
        dt_k = sem("dt_k")
        t0_out = sem("t0_out")
        u_out = [sem(f"u_out_{j}") for j in range(WC)]
        u_zero = sem("u_zero")
        u_in = sem("u_in")
        carr_in = sem("carr_in")
        cbt_done = sem("cbt_done")
        xs_zero = sem("xs_zero")
        scanned = sem("scanned")
        conv_step = sem("conv_step")
        cb_zero = sem("cb_zero")
        y_tab = [sem(f"y_tab_{j}") for j in range(WC)]
        z_out = [sem(f"z_out_{j}") for j in range(WC)]
        zt_in = [sem(f"zt_in_{j}") for j in range(WC)]
        z_hi = sem("z_hi")
        z_ready = sem("z_ready")
        small_out = sem("small_out")
        st_out = sem("st_out")
        gf_in = sem("gf_in")
        out_done = sem("out_done")
        y_out = [sem("y_out_0"), sem("y_out_1")]

        block = ctx.enter_context(nc.Block())

        def cols(tb):
            return slice(tb * TW, (tb + 1) * TW)

        def take(eng, unit, bank=0):
            eng.wait_ge(banks_free[unit.slot], 3 * unit.before + bank)

        def last_tile(d):
            return TILES * (d + 1)

        x_rows = a["x_prompt"].rearrange("b (k s) d -> (b k) s d", s=S8)
        xs_rows = a["x_sample"].rearrange("b t d -> (b t) d")
        w_in = a["w_in"][0]

        def columns(w, n, k=DC):
            return w.rearrange("(c p) m -> p c m", p=P)[:, 0:k, n * P:(n + 1) * P] if isinstance(n, int) \
                else w.rearrange("(c p) m -> p c m", p=P)[:, 0:k, bass.ds(n * P, P)]

        def weights_of(name):
            what, j = name
            if what == "glu":
                return columns(a["ssm_w_glu"][0], j, WC)
            first = {"u": 0, "xc": W, "gb": 2 * W, "gc": 3 * W}[what] // P
            return columns(w_in, first + j)

        def down_rows(w, f):
            return w[f * P:(f + 1) * P, :] if isinstance(f, int) else w[bass.ds(f * P, P), :]

        @block.sync
        def _(sp):
            def load(slot, n, src):
                if not (isinstance(n, int) and n == 0):
                    sp.wait_ge(w_split[slot], n)
                k = src.shape[1] if slot < 2 else DC
                dst = RAW[:, slot, 0:k * P]
                if slot < 2:
                    dst = dst.rearrange("p (c m) -> p c m", m=P)
                sp.dma_start(dst, src).then_inc(raw_full[slot], 16)

            def load_named(name):
                load(UNITS[name].slot, WEIGHTS[name], weights_of(name))

            for s in range(4):
                sp.dma_start(X[:, s, :], x_rows[:, s, :]).then_inc(x_in[s], 16)
            load(0, 0, columns(a["ffn1_w_gate"][0], 0))
            for s in range(4, S8):
                sp.dma_start(X[:, s, :], x_rows[:, s, :]).then_inc(x_in[s], 16)
            sp.dma_start(T[0:DEC, 0:D], xs_rows).then_inc(x_in[S8], 16)
            load(1, 0, columns(a["ffn1_w_up"][0], 0))
            sp.dma_start(o["conv_sample"][0, :, 0, :], a["state_conv"][0, :, 1, :]).then_inc(small_out, 16)
            load(2, 0, down_rows(a["ffn1_w_down"][0], 0))

            def ffn_rest(which, wg, wu, wd, down):
                with sp.Fori(1, NF) as f:
                    load(0, f + WEIGHTS["gate" + which], columns(wg, f))
                    load(1, f + WEIGHTS["up" + which], columns(wu, f))
                    load(2, f + down, down_rows(wd, f))

            ffn_rest("1", a["ffn1_w_gate"][0], a["ffn1_w_up"][0], a["ffn1_w_down"][0], DOWN1)

            for j in range(2):
                load_named(("u", j))
            sp.wait_ge(xn_ready, 17 + 24)
            for ri, name in enumerate(("state_ssm_re", "state_ssm_im")):
                sp.dma_start(CARR[:, ri, :], a[name][0].rearrange("b (g e) p -> (b g) (e p)", e=2)).then_inc(carr_in, 16)
            sp.dma_start(CBUF[:, :], a["state_conv"][0].rearrange("b r c -> (b r) c")).then_inc(carr_in, 16)
            def store_u(j):
                unit = UNITS[("u", j)]
                sp.wait_ge(banks_free[unit.slot], unit.full(2))
                sp.dma_start(UD[j * P:(j + 1) * P, :], (S, T)[j % 2][:, :]).then_inc(u_out[j], 16)

            load_named(("u", 2))
            load(2, DOWNC, down_rows(a["w_out"][0], WC))
            load_named(("u", 3))
            store_u(0)
            load_named(("xc", 0))
            store_u(1)
            load_named(("gc", 0))
            store_u(2)
            load_named(("gb", 0))
            store_u(3)
            sp.wait_ge(dt_k, 2)
            for s in range(S8):
                for g2 in range(2):
                    sp.dma_start(T0D[s * C16:(s + 1) * C16, :, g2, :],
                                 KT[g2 * C16:(g2 + 1) * C16, :, (7 - s) * C16:(7 - s) * C16 + P]).then_inc(t0_out, 16)

            for j in range(WC):
                sp.wait_ge(u_out[j], 16)
            sp.wait_ge(u_zero, 1)
            ug = UD.rearrange("(g c) n -> c g n", c=C16)
            for s in range(S8):
                sp.dma_start(U[s * C16:(s + 1) * C16, :, DEC:DEC + NK], ug[:, :, s * NK:(s + 1) * NK]).then_inc(u_in, 16)
            with nc.allow_non_contiguous_dma(reason="32 bytes a row, small"):
                sp.dma_start(U[0:C16, :, 0:DEC], ug[:, :, SEQ:NT]).then_inc(u_in, 16)
                sp.dma_start(U[P - C16:P, :, DEC + NK:UC], ug[:, :, SEQ:NT]).then_inc(u_in, 16)

            for c in range(1, WC):
                for what in ("xc", "gc", "gb"):
                    load_named((what, c))
                load(2, DOWNC + c, down_rows(a["w_out"][0], WC + c))
            load_named(("glu", 0))
            sp.wait_ge(cb_zero, 1)
            sp.wait_ge(t0_out, 16 * 16)
            sp.wait_ge(ca_out, 16)
            for j in range(WC):
                q = slice(4 * j, 4 * j + 4)
                sp.dma_start(T0[:, q], T0D[:, q]).then_inc(y_tab[j], 16)
                for g2 in range(2):
                    half = slice(g2 * NS, (g2 + 1) * NS)
                    sp.dma_start(CB[half, q, :, g2, :].rearrange("p g r n -> p (g r) n"),
                                 CAD[half, 8 * j:8 * j + 8, C16:]).then_inc(y_tab[j], 16)
            load_named(("glu", 1))
            for j in range(WC):
                unit = UNITS[("y", j)]
                sp.wait_ge(banks_free[unit.slot], unit.full(2))
                zg = ZD[j * P:(j + 1) * P, :].rearrange("(g c) n -> c g n", c=C16)
                for t in range(S8):
                    sp.dma_start(zg[:, :, t * NK:(t + 1) * NK],
                                 Z[t * C16:(t + 1) * C16, j % 2, :, DEC:YC]).then_inc(z_out[j], 16)
                with nc.allow_non_contiguous_dma(reason="32 bytes a row, small"):
                    sp.dma_start(zg[:, :, SEQ:NT], Z[0:C16, j % 2, :, 0:DEC]).then_inc(z_out[j], 16)
            unit = UNITS["states"]
            sp.wait_ge(banks_full[unit.slot], unit.full(2))
            for j in range(WC):
                sp.wait_ge(z_out[j], 16 * 9)
                sp.dma_start(ZT[:, j, :], ZD[j * P:(j + 1) * P, :]).then_inc(zt_in[j], 16)
            load(2, DOWNS, down_rows(a["w_out"][0], 0))
            sp.wait_ge(st_out, 2)
            for ri, (ps, ss) in enumerate((("re_prompt", "re_sample"), ("im_prompt", "im_sample"))):
                sp.dma_start(o[ps][0, 0].rearrange("(g e) p -> g (e p)", e=2), STO[0:GP, 2 + ri, :]).then_inc(small_out, 16)
                sp.dma_start(o[ss][0].rearrange("b (g e) p -> (b g) (e p)", e=2), STO[:, ri, :]).then_inc(small_out, 16)
            sp.dma_start(o["conv_sample"][0, :, 1, :], VO[0:DEC, :]).then_inc(small_out, 16)
            sp.dma_start(o["conv_prompt"][0, 0], VO[DEC:DEC + 2, :]).then_inc(small_out, 16)
            for j in range(2, WC):
                load_named(("glu", j))
                load(2, DOWNS + j - 1, down_rows(a["w_out"][0], j - 1))
            load(0, WEIGHTS["gate2"], columns(a["ffn2_w_gate"][0], 0))
            load(2, DOWNS + 3, down_rows(a["w_out"][0], 3))
            load(1, WEIGHTS["up2"], columns(a["ffn2_w_up"][0], 0))
            load(2, DOWN2, down_rows(a["ffn2_w_down"][0], 0))
            ffn_rest("2", a["ffn2_w_gate"][0], a["ffn2_w_up"][0], a["ffn2_w_down"][0], DOWN2)
            sp.wait_ge(small_out, 16 * 7)
            sp.dma_start(GF[:, :], a["final_norm"].rearrange("(o d) -> o d", o=1).to_broadcast([P, D])).then_inc(gf_in, 16)
            y_rows = o["y_prompt"].rearrange("b (k s) d -> (b k) s d", s=S8)
            for s in range(S8 + 1):
                sp.wait_ge(out_done, 2 * s + 2)
                if s < S8:
                    sp.dma_start(y_rows[:, s, :], OUT[:, s % 2, :]).then_inc(y_out[s % 2], 16)
                else:
                    sp.dma_start(o["y_sample"].rearrange("b t d -> (b t) d"), OUT[0:DEC, s % 2, :]).then_inc(y_out[s % 2], 16)
            sp.wait_ge(y_out[0], 16 * 5)
            sp.wait_ge(y_out[1], 16 * 4)

        @block.tensor
        def _(pe):
            def product3(out, wh, wl, xh, xl, first, last):
                pe.matmul(out, wh, xh, start=first, stop=False)
                pe.matmul(out, wh, xl, start=False, stop=False)
                return pe.matmul(out, wl, xh, start=False, stop=last)

            def bank_wait(unit, b):
                if isinstance(unit.before, int) and unit.before == 0:
                    return
                pe.wait_ge(banks_free[unit.slot], 3 * unit.before + b - 2)

            def down_tile(d, par, tb, j):
                tile = TILES * d + DC * tb + j
                if not (isinstance(d, int) and d == 0 and tb == 0 and j < 2):
                    pe.wait_ge(down_free, tile - 1)
                out = DB[(DC * tb + j) % 2][:, 0:TW]
                m = slice(j * P, (j + 1) * P)
                product3(out, WH[:, 2, m], WL[:, 2, m], HH[:, par, cols(tb)], HL[:, par, cols(tb)], True, True
                         ).then_inc(down_full, 1)

            def down_start(d):
                pe.wait_ge(w_split[2], d + 1)

            def down_block(d, par, tb):
                pe.wait_ge(h_ready, 3 * d + tb + 1)
                for j in range(DC):
                    down_tile(d, par, tb, j)

            def project(unit, weight, xh=XH, xl=XL, k=DC, x_wait=None, down=None):
                pe.wait_ge(w_split[unit.slot], weight + 1)
                if down is not None:
                    down_start(down[0])
                for tb in range(TB):
                    if x_wait is not None:
                        pe.wait_ge(*x_wait[tb])
                    bank_wait(unit, tb)
                    if down is not None:
                        pe.wait_ge(h_ready, 3 * down[0] + tb + 1)
                    out = AB[unit.slot][tb][:, 0:TW]
                    for c in range(k):
                        m = slice(c * P, (c + 1) * P)
                        last = product3(out, WH[:, unit.slot, m], WL[:, unit.slot, m], xh[:, c, cols(tb)],
                                        xl[:, c, cols(tb)], c == 0, c == k - 1)
                        if c == k - 1:
                            last.then_inc(banks_full[unit.slot], 1)
                        if down is not None:
                            down_tile(down[0], down[1], tb, c)

            def norm_sums(unit, n, tb):
                bank_wait(unit, tb)
                for c in range(DC):
                    i = n + DC * tb + c
                    pe.wait_ge(sq_done, i + 1)
                    last = pe.matmul(AB[unit.slot][tb][:, 0:TW], ONES[:, :], SQ[:, (i % 3) * TW:(i % 3 + 1) * TW],
                                     start=c == 0, stop=c == DC - 1)
                    last.then_inc(*((sums_done, 1) if c < DC - 1 else (banks_full[unit.slot], 1)))

            def ffn(which, down, x_waits):
                ug, uu = UNITS["gate" + which], UNITS["up" + which]
                wg, wu = WEIGHTS["gate" + which], WEIGHTS["up" + which]
                project(ug, wg, x_wait=x_waits)
                project(uu, wu)

                def step(f, par):
                    project(ug.at(f), f + wg)
                    project(uu.at(f), f + wu, down=(f + (down - 1), par))
                step(1, 0)
                step(2, 1)
                with pe.Fori(1, (NF - 2) // 2) as i:
                    step(i * 2 + 1, 0)
                    step(i * 2 + 2, 1)
                step(NF - 1, 0)

            pe.wait_ge(const_done, 3)
            n = 0
            for half in range(2):
                for what in range(2):
                    for c in range(DC):
                        unit, b = UNITS[("x", n // 3)], n % 3
                        bank_wait(unit, b)
                        for q in range(4):
                            s = 4 * half + q
                            if c == 0:
                                pe.wait_ge(*((x_in[s], 16) if what == 0 else (diag_x, s + 1)))
                            rhs = IDENT[:, :] if what == 0 else DR[:, s, :]
                            last = pe.matmul(AB[unit.slot][b][:, q * P:(q + 1) * P], X[:, s, c * P:(c + 1) * P], rhs,
                                             start=True, stop=True)
                        last.then_inc(banks_full[unit.slot], 1)
                        n += 1
            for what in range(2):
                unit, b = UNITS[("x", n // 3)], n % 3
                bank_wait(unit, b)
                pe.wait_ge(*((x_in[S8], 16) if what == 0 else (diag_x, S8 + 1)))
                for c in range(DC):
                    rhs = IDENT[0:DEC, 0:DEC] if what == 0 else DR[0:DEC, S8, 0:DEC]
                    last = pe.matmul(AB[unit.slot][b][:, c * DEC:(c + 1) * DEC], T[0:DEC, c * P:(c + 1) * P], rhs,
                                     start=True, stop=True)
                last.then_inc(banks_full[unit.slot], 1 if what == 0 else 3)
                n += 1
            unit = UNITS["params"]
            bank_wait(unit, 0)
            pe.wait_ge(par_set, 3)
            pe.transpose(AB[unit.slot][0][:, 0:96], PAR[:, :], IDENT[0:96, 0:96]).then_inc(banks_full[unit.slot], 1)
            pe.wait_ge(c_in, 64)
            for ri in range(2):
                bank_wait(unit, 1 + ri)
                for q in range(4):
                    last = pe.transpose(AB[unit.slot][1 + ri][:, q * P:(q + 1) * P], CL[:, ri, q, :], IDENT[:, :])
                last.then_inc(banks_full[unit.slot], 1)

            ffn("1", DOWN1, [(xn_ready, 8), (xn_ready, 16), (xn_ready, 17)])

            d = DOWN1 + NF - 1
            down_start(d)
            down_block(d, d % 2, 0)
            down_block(d, d % 2, 1)
            norm_sums(UNITS["norm2"], 0, 0)
            down_block(d, d % 2, 2)
            norm_sums(UNITS["norm2"], 0, 1)
            norm_sums(UNITS["norm2"], 0, 2)
            xw = [(xn_ready, 17 + 8), (xn_ready, 17 + 16), (xn_ready, 17 + 24)]
            for j in range(WC):
                project(UNITS[("u", j)], WEIGHTS[("u", j)], x_wait=xw if j == 0 else None)
            pe.wait_ge(disc_p, 4)
            for n in range(8):
                unit, b = UNITS[("tab", n // 3)], n % 3
                bank_wait(unit, b)
                for q in range(4):
                    i = 4 * n + q
                    last = pe.transpose(AB[unit.slot][b][:, q * P:(q + 1) * P], BS[:, i // 2, i % 2, :], IDENT[:, :])
                last.then_inc(banks_full[unit.slot], 1)
            for n in range(8, 12):
                unit, b = UNITS[("tab", n // 3)], n % 3
                bank_wait(unit, b)
                for q in range(4):
                    i = 4 * (n - 8) + q
                    for ri in range(2):
                        last = pe.matmul(AB[unit.slot][b][0:32, q * P:(q + 1) * P], BD[:, i, ri, :], CA[:, i, ri, 0:P],
                                         start=ri == 0, stop=ri == 1)
                last.then_inc(banks_full[unit.slot], 1)
            unit = UNITS["carried"]
            pe.wait_ge(carr_in, 48)
            bank_wait(unit, 2)
            for ri in range(2):
                last = pe.transpose(AB[unit.slot][0][:, ri * P:(ri + 1) * P], CARR[:, ri, :], IDENT[:, :])
            last.then_inc(banks_full[unit.slot], 3)
            unit = UNITS["buffer"]
            bank_wait(unit, 2)
            for j in range(WC):
                last = pe.transpose(AB[unit.slot][0][:, j * 16:(j + 1) * 16], CBUF[:, j * P:(j + 1) * P],
                                    IDENT[0:16, 0:16])
            last.then_inc(banks_full[unit.slot], 3)

            for c in range(WC):
                project(UNITS[("xc", c)], WEIGHTS[("xc", c)])
                project(UNITS[("gc", c)], WEIGHTS[("gc", c)], down=None if c == 0 else (DOWNC + c - 1, (c - 1) % 2))
                project(UNITS[("gb", c)], WEIGHTS[("gb", c)])
                if c == 0:
                    pe.wait_ge(u_in, 16 * 10)
                    for n, items in enumerate(V_BANKS):
                        unit, b = UNITS[("v", n // 3)], n % 3
                        bank_wait(unit, b)
                        for q, i in enumerate(items):
                            ri, g = divmod(i, GP)
                            for g2 in range(2):
                                half = slice(g2 * NS, (g2 + 1) * NS)
                                last = pe.matmul(AB[unit.slot][b][half, q * YC:(q + 1) * YC], WT[:, g, ri, half],
                                                 U[:, 2 * g + g2, DEC:UC], start=True, stop=True)
                        last.then_inc(banks_full[unit.slot], 2 if n == len(V_BANKS) - 1 else 1)

            pe.wait_ge(scanned, 1)
            for j in range(WC):
                unit = UNITS[("y", j)]
                pe.wait_ge(y_tab[j], 48)
                for b, items in enumerate(Y_BANKS):
                    bank_wait(unit, b)
                    for q, i in enumerate(items):
                        g = 8 * j + i
                        out = AB[unit.slot][b][:, q * YC:(q + 1) * YC]
                        pe.matmul(out, T0[:, g // 2, g % 2, :], U[:, g, 0:YC], start=True, stop=False)
                        pe.matmul(out, CB[:, g // 2, 0, g % 2, :], XS[:, g // 2, 0:YC], start=False, stop=False)
                        last = pe.matmul(out, CB[:, g // 2, 1, g % 2, :], XS[:, GP + g // 2, 0:YC], start=False, stop=True)
                    last.then_inc(banks_full[unit.slot], 1)
            unit = UNITS["states"]
            bank_wait(unit, 2)
            for ri in range(2):
                pe.transpose(AB[unit.slot][0][:, ri * P:(ri + 1) * P], DNEW[:, ri, :], IDENT[:, :])
                last = pe.transpose(AB[unit.slot][0][0:GP, (2 + ri) * P:(3 + ri) * P],
                                    XS[:, ri * GP:(ri + 1) * GP, DEC + NK], IDENT[:, :])
            last.then_inc(banks_full[unit.slot], 3)
            unit = UNITS["vout"]
            bank_wait(unit, 2)
            pe.wait_ge(conv_step, 10 * WC)
            for j in range(WC):
                last = pe.transpose(AB[unit.slot][0][0:16, j * P:(j + 1) * P], VOUT[:, j, :], IDENT[:, :])
            last.then_inc(banks_full[unit.slot], 3)
            d = DOWNC + 3
            down_start(d)
            for tb in range(TB):
                down_block(d, d % 2, tb)

            zw = [(z_ready, 4), (z_ready, 8), (z_ready, 12)]
            for j in range(WC):
                project(UNITS[("glu", j)], WEIGHTS[("glu", j)], ZH, ZL, WC, x_wait=zw if j == 0 else None)
                if j >= 1:
                    down_start(DOWNS + j - 1)
                    for tb in range(TB):
                        down_block(DOWNS + j - 1, (j - 1) % 2, tb)
            d = DOWNS + 3
            down_start(d)
            down_block(d, d % 2, 0)
            down_block(d, d % 2, 1)
            norm_sums(UNITS["norm3"], 24, 0)
            down_block(d, d % 2, 2)
            norm_sums(UNITS["norm3"], 24, 1)
            norm_sums(UNITS["norm3"], 24, 2)

            ffn("2", DOWN2, [(xn_ready, 41 + 8), (xn_ready, 41 + 16), (xn_ready, 41 + 24)])
            d = DOWN2 + NF - 1
            down_start(d)
            for tb in range(TB):
                down_block(d, d % 2, tb)
            for s in range(S8 + 1):
                unit = UNITS[("out", s)]
                bank_wait(unit, 2)
                last_col = (s + 1) * NK if s < S8 else NT
                pe.wait_ge(down_free, TILES * d + DC * -(-last_col // TW))
                m = NK if s < S8 else DEC
                for c in range(DC):
                    last = pe.transpose(AB[unit.slot][c // 4][0:m, (c % 4) * P:(c % 4 + 1) * P],
                                        HT[:, c, s * NK:s * NK + m], IDENT[:, :])
                last.then_inc(banks_full[unit.slot], 3)

        @block.scalar
        def _(act):
            def split_hi(slot, n, k=DC, unit=None, down=None):
                act.wait_ge(raw_full[slot], (n + 1) * 16)
                if unit is not None:
                    act.wait_ge(banks_full[slot], unit.full(2))
                if down is not None:
                    act.wait_ge(down_full, last_tile(down))
                act.activation(WH[:, slot, 0:k * P], RAW[:, slot, 0:k * P], ACT.Copy).then_inc(w_hi[slot], 1)

            def h_hi(d, par, tb, wait):
                act.wait_ge(*wait)
                if not (isinstance(d, int) and d < 2):
                    act.wait_ge(down_full, TILES * (d - 1))
                act.activation(HH[:, par, cols(tb)], T[:, cols(tb)], ACT.Copy).then_inc(hi_done, 1)

            def norm(unit, n, base, d, xn_base, free_unit, free_down):
                def squares(tb):
                    for c in range(DC):
                        i = n + DC * tb + c
                        act.wait_ge(down_free, TILES * d + DC * tb + c + 1)
                        if i - 3 >= n:
                            block, q = divmod(i - 3, DC)
                            if q < DC - 1:
                                act.wait_ge(sums_done, (DC - 1) * block + q + 1)
                            else:
                                act.wait_ge(banks_full[unit.slot], unit.full(block - n // DC))
                        act.activation(SQ[:, (i % 3) * TW:(i % 3 + 1) * TW], HT[:, c, cols(tb)], ACT.Square
                                       ).then_inc(sq_done, 1)

                def root(tb):
                    act.wait_ge(banks_full[unit.slot], unit.full(tb))
                    take(act, unit, tb)
                    act.activation(R[:, cols(tb)], AB[unit.slot][tb][:, 0:TW], ACT.Sqrt, bias=EPSC[:, :], scale=1.0 / D
                                   ).then_inc(banks_free[unit.slot], 1)

                def upper(tb):
                    for c in range(DC):
                        i = DC * tb + c
                        act.wait_ge(xn_tmp, base + i + 1)
                        if i == 0:
                            for u in free_unit:
                                act.wait_ge(banks_full[u.slot], u.full(2))
                        act.activation(XH[:, c, cols(tb)], ring(i), ACT.Copy).then_inc(xn_hi, 1)
                return squares, root, upper

            def ffn(which, down, last_next):
                ug, uu = UNITS["gate" + which], UNITS["up" + which]
                wg, wu = WEIGHTS["gate" + which], WEIGHTS["up" + which]

                def silu(f, d):
                    if isinstance(f, int) and f == 0:
                        take(act, ug)
                    for tb in range(TB):
                        act.wait_ge(banks_full[0], ug.at(f).full(tb))
                        if not (isinstance(f, int) and f == 0):
                            act.wait_ge(banks_free[1], uu.at(f - 1).full(tb))
                        act.activation(S[:, cols(tb)], AB[0][tb][:, 0:TW], ACT.Silu).then_inc(banks_free[0], 1)

                def uppers(f, par):
                    for tb in range(TB):
                        h_hi(f + down, par, tb, (banks_free[1], uu.at(f).full(tb)))

                def step(f, par):
                    split_hi(1, f + wu, unit=uu.at(f - 1))
                    if isinstance(f, int) and f == 1:
                        split_hi(2, down) if down == 0 else split_hi(2, down, down=down - 1)
                    else:
                        split_hi(2, f + (down - 1), down=f + (down - 2))
                    silu(f, f + down)
                    split_hi(0, f + (wg + 1), unit=ug.at(f))
                    uppers(f, par)

                silu(0, down)
                split_hi(0, wg + 1, unit=ug)
                uppers(0, 0)
                step(1, 1)
                step(2, 0)
                with act.Fori(1, (NF - 2) // 2) as i:
                    step(i * 2 + 1, 1)
                    step(i * 2 + 2, 0)
                f = NF - 1
                split_hi(1, f + wu, unit=uu.at(f - 1))
                split_hi(2, f + (down - 1), down=f + (down - 2))
                silu(f, f + down)
                if last_next is not None:
                    split_hi(0, last_next, unit=ug.at(f))
                uppers(f, 1)
                split_hi(2, f + down, down=f + down - 1)

            def ring(i):
                return (S, T)[i % 6 // 3][:, (i % 3) * TW:(i % 3 + 1) * TW]

            act.wait_ge(const_done, 3)
            for half in range(2):
                for s in range(4 * half, 4 * half + 4):
                    act.wait_ge(x_in[s], 16)
                    if s > 0:
                        act.wait_ge(sq_x, s)
                    act.activation(S[:, 0:D], X[:, s, :], ACT.Square, accum_out=SS[:, s, 0:1]).then_inc(sq_x, 1)
                act.wait_ge(sq_x, 4 * half + 4)
                act.activation(RS[:, 4 * half:4 * half + 4], SS[:, 4 * half:4 * half + 4, 0], ACT.Sqrt, bias=EPSC[:, :],
                               scale=1.0 / D).then_inc(sqrt_x, 1)
                if half == 0:
                    split_hi(0, 0)
                if half == 1:
                    act.wait_ge(x_in[S8], 16)
                    act.activation(S[0:DEC, 0:D], T[0:DEC, 0:D], ACT.Square, accum_out=SS[0:DEC, S8, 0:1]).then_inc(sq_x, 1)
                    act.wait_ge(sq_x, 9)
                    act.activation(RS[0:DEC, S8:S8 + 1], SS[0:DEC, S8, 0:1], ACT.Sqrt, bias=EPSC[0:DEC, :], scale=1.0 / D
                                   ).then_inc(sqrt_x, 1)
                if half == 0:
                    act.wait_ge(consts_in, 16 * 6)
                for c in range(DC):
                    n = 16 * half + 8 + c
                    unit, b = UNITS[("x", n // 3)], n % 3
                    act.wait_ge(banks_full[unit.slot], unit.full(b))
                    act.activation(XH[:, c, half * 512:(half + 1) * 512], AB[unit.slot][b][:, :], ACT.Copy,
                                   scale=GAIN[:, 0, c:c + 1]).then_inc(xn_hi, 1)
            unit = UNITS[("x", 11)]
            act.wait_ge(banks_full[unit.slot], unit.full(0))
            for c in range(DC):
                last = act.activation(XH[:, c, SEQ:NT], AB[unit.slot][0][:, c * DEC:(c + 1) * DEC], ACT.Copy,
                                      scale=GAIN[:, 0, c:c + 1])
            last.then_inc(xn_hi, 1)
            split_hi(1, 0)
            act.wait_ge(lri_done, 3)
            act.activation(TMP[:, 0, :], LRI[:, 2, :], ACT.Exp).then_inc(disc_a, 1)
            act.wait_ge(disc_p, 1)
            act.activation(TMP[:, 3, :], TMP[:, 1, :], ACT.Exp).then_inc(disc_a, 1)
            act.activation(TMP[:, 4, :], TMP[:, 2, :], ACT.Sin).then_inc(disc_a, 1)
            act.activation(TMP[:, 5, :], TMP[:, 6, :], ACT.Sin).then_inc(disc_a, 1)

            ffn("1", DOWN1, WEIGHTS[("u", 0)])
            split_hi(1, WEIGHTS[("u", 1)], unit=UNITS["up1"].at(NF - 1))

            act.wait_ge(disc_p, 4)
            squares, root, upper = norm(UNITS["norm2"], 0, 0, NF - 1, 17,
                                        [UNITS["gate1"].at(NF - 1), UNITS["up1"].at(NF - 1)], None)
            act.wait_ge(h_ready, 3 * NF)
            squares(0)
            root(0)
            squares(1)
            upper(0)
            squares(2)
            root(1)
            upper(1)
            root(2)
            upper(2)

            def evict(unit, tb, dst):
                act.wait_ge(banks_full[unit.slot], unit.full(tb))
                take(act, unit, tb)
                act.activation(dst[:, cols(tb)], AB[unit.slot][tb][:, 0:TW], ACT.Copy).then_inc(banks_free[unit.slot], 1)

            def next_split(name):
                i = WEIGHTED.index(name)
                slot = UNITS[name].slot
                before = [w for w in WEIGHTED[:i] if UNITS[w].slot == slot]
                k = WC if name[0] == "glu" else DC
                split_hi(slot, WEIGHTS[name], k, unit=UNITS[before[-1]])

            for j in range(WC):
                unit = UNITS[("u", j)]
                dst = (S, T)[j % 2]
                if j >= 2:
                    act.wait_ge(u_out[j - 2], 16)
                if j == 0:
                    act.wait_ge(xn_ready, 17 + 24)
                for tb in range(TB):
                    evict(unit, tb, dst)
                next_split(WEIGHTED[j + 2])
                if j == 0:
                    split_hi(2, DOWNC, down=DOWNC - 1)
            act.wait_ge(down_full, last_tile(DOWN1 + NF - 1))
            for n in range(12):
                unit, b = UNITS[("tab", n // 3)], n % 3
                act.wait_ge(banks_full[unit.slot], unit.full(b))
                take(act, unit, b)
                if n < 8:
                    act.activation(WT[:, 2 * n:2 * n + 2, :, :].rearrange("p g r n -> p (g r n)"), AB[unit.slot][b][:, :],
                                   ACT.Copy).then_inc(banks_free[unit.slot], 1)
                else:
                    if n == 8:
                        act.wait_ge(disc_p, 5)
                    src = AB[unit.slot][b][0:32, :].rearrange("p (g n) -> p g n", n=P)
                    act.activation(KT[:, 4 * (n - 8):4 * (n - 7), 7 * C16:], src, ACT.Copy
                                   ).then_inc(banks_free[unit.slot], 1)
            unit = UNITS["carried"]
            act.wait_ge(banks_full[unit.slot], unit.full(2))
            take(act, unit)
            act.wait_ge(xs_zero, 1)
            for ri in range(2):
                last = act.activation(XS[:, ri * GP:(ri + 1) * GP, 0:DEC].rearrange("p g t -> p t g"),
                                      AB[unit.slot][0][:, ri * P:(ri + 1) * P].rearrange("p (t g) -> p t g", g=GP), ACT.Copy)
            last.then_inc(banks_free[unit.slot], 3)
            unit = UNITS["buffer"]
            act.wait_ge(banks_full[unit.slot], unit.full(2))
            take(act, unit)
            act.activation(CBT[:, :, :].rearrange("p j n -> p (j n)"), AB[unit.slot][0][:, 0:64], ACT.Copy
                           ).then_inc(banks_free[unit.slot], 3)

            for c in range(WC):
                names = [("xc", c), ("gc", c), ("gb", c)]
                i = WEIGHTED.index(names[0])
                unit = UNITS[names[0]]
                if c == 0:
                    act.wait_ge(u_out[2], 16)
                    act.wait_ge(u_out[3], 16)
                else:
                    act.wait_ge(banks_free[UNITS[("gc", c - 1)].slot], UNITS[("gc", c - 1)].full(2))
                for tb in range(TB):
                    evict(unit, tb, S)
                next_split(WEIGHTED[i + 2])
                next_split(WEIGHTED[i + 3])
                unit = UNITS[("gb", c)]
                if c == 0:
                    for n, items in enumerate(V_BANKS):
                        vu, b = UNITS[("v", n // 3)], n % 3
                        act.wait_ge(banks_full[vu.slot], vu.full(b))
                        take(act, vu, b)
                        src = AB[vu.slot][b][:, 0:len(items) * YC].rearrange("p (q n) -> p q n", n=YC)
                        act.activation(XS[:, items[0]:items[-1] + 1, DEC + 1:XC], src, ACT.Copy
                                       ).then_inc(banks_free[vu.slot], 2 if n == len(V_BANKS) - 1 else 1)
                for tb in range(TB):
                    h_hi(DOWNC + c, c % 2, tb, (banks_free[unit.slot], unit.full(tb)))
                next_split(WEIGHTED[i + 4])
                if c >= 1:
                    split_hi(2, DOWNC + c, down=DOWNC + c - 1)
            for j in range(WC):
                unit = UNITS[("y", j)]
                if j >= 2:
                    act.wait_ge(z_out[j - 2], 16 * 9)
                for b, items in enumerate(Y_BANKS):
                    act.wait_ge(banks_full[unit.slot], unit.full(b))
                    take(act, unit, b)
                    act.activation(Z[:, j % 2, items[0]:items[-1] + 1, :].rearrange("p g n -> p (g n)"),
                                   AB[unit.slot][b][:, 0:len(items) * YC], ACT.Gelu_apprx_tanh
                                   ).then_inc(banks_free[unit.slot], 1)
            unit = UNITS["states"]
            act.wait_ge(banks_full[unit.slot], unit.full(2))
            take(act, unit)
            act.activation(STO[:, 0:2, :].rearrange("p r n -> p (r n)"), AB[unit.slot][0][:, 0:2 * P], ACT.Copy)
            act.activation(STO[0:GP, 2:4, :].rearrange("p r n -> p (r n)"), AB[unit.slot][0][0:GP, 2 * P:4 * P], ACT.Copy
                           ).then_inc(banks_free[unit.slot], 3)
            act.wait_ge(banks_free[unit.slot], unit.full(2))
            act.nop().then_inc(st_out, 1)
            unit = UNITS["vout"]
            act.wait_ge(banks_full[unit.slot], unit.full(2))
            take(act, unit)
            act.activation(VO[:, :], AB[unit.slot][0][0:16, :], ACT.Copy).then_inc(banks_free[unit.slot], 3)
            act.wait_ge(banks_free[unit.slot], unit.full(2))
            act.nop().then_inc(st_out, 1)
            y3 = UNITS[("y", 3)]
            for tb in range(TB):
                for j in range(WC):
                    if tb == 0:
                        act.wait_ge(zt_in[j], 16)
                        act.wait_ge(z_out[j], 16 * 9)
                    act.activation(ZH[:, j, cols(tb)], ZT[:, j, cols(tb)], ACT.Copy).then_inc(z_hi, 1)
            split_hi(2, DOWNS, down=DOWNS - 1)
            for j in range(WC):
                unit = UNITS[("glu", j)]
                for tb in range(TB):
                    act.wait_ge(banks_full[unit.slot], unit.full(tb))
                    if j > 0:
                        act.wait_ge(gate_done, 3 * (j - 1) + tb + 1)
                    take(act, unit, tb)
                    act.activation(S[:, cols(tb)], AB[unit.slot][tb][:, 0:TW], ACT.Sigmoid, bias=BG[:, j:j + 1]
                                   ).then_inc(banks_free[unit.slot], 1)
                for tb in range(TB):
                    h_hi(DOWNS + j, j % 2, tb, (gate_done, 3 * j + tb + 1))
                if j < 2:
                    next_split(("glu", j + 2))
                if j >= 1:
                    split_hi(2, DOWNS + j, down=DOWNS + j - 1)
                if j == 2:
                    split_hi(0, WEIGHTS["gate2"], unit=UNITS[("glu", 2)])
                if j == 3:
                    split_hi(1, WEIGHTS["up2"], unit=UNITS[("glu", 3)])
            squares, root, upper = norm(UNITS["norm3"], 24, 24, DOWNS + 3, 41, [UNITS[("glu", 3)]], None)
            act.wait_ge(h_ready, 3 * DOWN2)
            squares(0)
            root(0)
            squares(1)
            upper(0)
            squares(2)
            root(1)
            upper(1)
            root(2)
            upper(2)
            act.wait_ge(xn_ready, 41 + 24)
            ffn("2", DOWN2, None)

            act.wait_ge(h_ready, 3 * ND)
            for s in range(S8 + 1):
                unit = UNITS[("out", s)]
                m = NK if s < S8 else DEC
                act.wait_ge(banks_full[unit.slot], unit.full(2))
                for h in range(2):
                    if s > 0 or h > 0:
                        act.wait_ge(sq_x, 9 + 2 * s + h)
                    act.activation(S[0:m, 0:512], AB[unit.slot][h][0:m, :], ACT.Square, accum_out=SS[0:m, s, h:h + 1]
                                   ).then_inc(sq_x, 1)
                act.wait_ge(ss_sum, s + 1)
                act.activation(RS[0:m, s:s + 1], SS[0:m, s, 0:1], ACT.Sqrt, bias=EPSC[0:m, :], scale=1.0 / D
                               ).then_inc(sqrt_x, 1)

        @block.vector
        def _(dve):
            def f(t):
                return t.bitcast(F32)

            def split_lo(slot, n, k=DC):
                dve.wait_ge(w_hi[slot], n + 1)
                dve.tensor_tensor(WL[:, slot, 0:k * P], RAW[:, slot, 0:k * P], f(WH[:, slot, 0:k * P]), ALU.subtract
                                  ).then_inc(w_split[slot], 1)

            def h_lo(d, par, tb):
                dve.wait_ge(hi_done, 3 * d + tb + 1)
                dve.tensor_tensor(HL[:, par, cols(tb)], T[:, cols(tb)], f(HH[:, par, cols(tb)]), ALU.subtract
                                  ).then_inc(h_ready, 1)

            def add_tile(d, tb, j, scale):
                dve.wait_ge(down_full, TILES * d + DC * tb + j + 1)
                ht = HT[:, j, cols(tb)]
                if scale == 1.0:
                    ins = dve.tensor_tensor(ht, DB[(DC * tb + j) % 2][:, 0:TW], ht, ALU.add)
                else:
                    ins = dve.scalar_tensor_tensor(ht, DB[(DC * tb + j) % 2][:, 0:TW], scale, ht, ALU.mult, ALU.add)
                ins.then_inc(down_free, 1)

            def add_block(d, tb, scale=0.5):
                for j in range(DC):
                    add_tile(d, tb, j, scale)

            def ring(i):
                return (S, T)[i % 6 // 3][:, (i % 3) * TW:(i % 3 + 1) * TW]

            def norm(unit, k, base, xn_base, add):
                def invert(tb):
                    dve.wait_ge(banks_free[unit.slot], unit.full(tb))
                    dve.reciprocal(R[:, cols(tb)], R[:, cols(tb)]).then_inc(r_done, 1)

                def scaled(i, n0):
                    tb, c = divmod(i, DC)
                    if c == 0:
                        dve.wait_ge(r_done, n0 + tb + 1)
                    if i >= 6:
                        dve.wait_ge(xn_ready, xn_base + i - 5)
                    dve.scalar_tensor_tensor(ring(i), HT[:, c, cols(tb)], GAIN[:, k, c:c + 1], R[:, cols(tb)], ALU.mult,
                                             ALU.mult).then_inc(xn_tmp, 1)

                def lower(i):
                    tb, c = divmod(i, DC)
                    dve.wait_ge(xn_hi, xn_base + i + 1)
                    dve.tensor_tensor(XL[:, c, cols(tb)], ring(i), f(XH[:, c, cols(tb)]), ALU.subtract
                                      ).then_inc(xn_ready, 1)

                def apply(tb, n0):
                    for c in range(DC + 2):
                        if c < DC:
                            scaled(DC * tb + c, n0)
                        if c >= 2:
                            lower(DC * tb + c - 2)

                n0 = 3 * (k - 1)
                dve.wait_ge(h_ready, 3 * NF if k == 1 else 3 * DOWN2)
                for tb in range(TB):
                    add(tb)
                invert(0)
                apply(0, n0)
                invert(1)
                apply(1, n0)
                invert(2)
                apply(2, n0)

            def ffn(which, down, last_next):
                ug, uu = UNITS["gate" + which], UNITS["up" + which]
                wg, wu = WEIGHTS["gate" + which], WEIGHTS["up" + which]

                def mul(n, tb):
                    if isinstance(n, int) and n == 0:
                        take(dve, uu, tb)
                    dve.wait_ge(banks_full[1], uu.at(n).full(tb))
                    dve.wait_ge(banks_free[0], ug.at(n).full(tb))
                    if not (isinstance(n, int) and n == 0):
                        dve.wait_ge(h_ready, 3 * (n + (down - 1)) + tb + 1)
                    else:
                        dve.wait_ge(xn_ready, 17 if down == 0 else 41 + 24)
                    dve.tensor_tensor(T[:, cols(tb)], AB[1][tb][:, 0:TW], S[:, cols(tb)], ALU.mult
                                      ).then_inc(banks_free[1], 1)

                def step(n, par):
                    split_lo(1, n + wu)
                    split_lo(2, n + (down - 1))
                    split_lo(0, n + (wg + 1))
                    for tb in range(TB):
                        add_block(n + (down - 1), tb)
                        mul(n, tb)
                    for tb in range(TB):
                        h_lo(n + down, par, tb)

                split_lo(0, wg + 1)
                for tb in range(TB):
                    mul(0, tb)
                for tb in range(TB):
                    h_lo(down, 0, tb)
                if down == 0:
                    dve.wait_ge(disc_p, 2)
                    dve.reciprocal(TMP[:, 12, :], TMP[:, 7, :]).then_inc(den_inv, 1)
                with dve.Fori(0, (NF - 2) // 2) as i:
                    step(i * 2 + 1, 1)
                    step(i * 2 + 2, 0)
                n = NF - 1
                split_lo(1, n + wu)
                split_lo(2, n + down - 1)
                if last_next is not None:
                    split_lo(0, last_next)
                for tb in range(TB):
                    add_block(n + down - 1, tb)
                    mul(n, tb)
                for tb in range(TB):
                    h_lo(n + down, 1, tb)
                split_lo(2, n + down)

            dve.wait_ge(const_done, 3)

            def diagonals(half):
                span = slice(4 * half, 4 * half + 4)
                dve.wait_ge(sqrt_x, half + 1)
                dve.reciprocal(RS[:, span], RS[:, span]).then_inc(rcp_x, 1)
                dve.wait_ge(rcp_x, half + 1)
                for s in range(4 * half, 4 * half + 4):
                    dve.tensor_scalar(DR[:, s, :], IDENT[:, :], RS[:, s:s + 1], None, ALU.mult).then_inc(diag_x, 1)

            for half in range(2):
                span = slice(half * 512, (half + 1) * 512)
                for c in range(DC):
                    n = 16 * half + c
                    unit, b = UNITS[("x", n // 3)], n % 3
                    dve.wait_ge(banks_full[unit.slot], unit.full(b))
                    dve.tensor_copy(HT[:, c, span], AB[unit.slot][b][:, :]).then_inc(banks_free[unit.slot], 1)
                    if c == 1:
                        diagonals(half)
                    if c == 3 and half == 1:
                        dve.wait_ge(sqrt_x, 3)
                        dve.reciprocal(RS[0:DEC, S8:S8 + 1], RS[0:DEC, S8:S8 + 1]).then_inc(rcp_x, 1)
                        dve.wait_ge(rcp_x, 3)
                        dve.tensor_scalar(DR[0:DEC, S8, 0:DEC], IDENT[0:DEC, 0:DEC], RS[0:DEC, S8:S8 + 1], None, ALU.mult
                                          ).then_inc(diag_x, 1)
                if half == 0:
                    split_lo(0, 0)
                for c in range(DC):
                    n = 16 * half + 8 + c
                    unit, b = UNITS[("x", n // 3)], n % 3
                    dve.wait_ge(xn_hi, 8 * half + c + 1)
                    dve.scalar_tensor_tensor(XL[:, c, span], AB[unit.slot][b][:, :], GAIN[:, 0, c:c + 1],
                                             f(XH[:, c, span]), ALU.mult, ALU.subtract).then_inc(xn_ready, 1)
                    dve.wait_ge(xn_ready, 8 * half + c + 1)
                    dve.nop().then_inc(banks_free[unit.slot], 1)
            unit = UNITS[("x", 10)]
            dve.wait_ge(banks_full[unit.slot], unit.full(2))
            dve.tensor_copy(HT[:, :, SEQ:NT], AB[unit.slot][2][:, 0:DC * DEC].rearrange("p (c n) -> p c n", n=DEC)
                            ).then_inc(banks_free[unit.slot], 1)
            unit = UNITS[("x", 11)]
            dve.wait_ge(xn_hi, 17)
            for c in range(DC):
                last = dve.scalar_tensor_tensor(XL[:, c, SEQ:NT], AB[unit.slot][0][:, c * DEC:(c + 1) * DEC],
                                                GAIN[:, 0, c:c + 1], f(XH[:, c, SEQ:NT]), ALU.mult, ALU.subtract)
            last.then_inc(xn_ready, 1)
            dve.wait_ge(xn_ready, 17)
            dve.nop().then_inc(banks_free[unit.slot], 3)
            split_lo(1, 0)
            unit = UNITS["params"]
            dve.wait_ge(banks_full[unit.slot], unit.full(0))
            for n in range(3):
                last = dve.tensor_copy(LRI[:, n, :], AB[unit.slot][0][:, 32 * n:32 * n + GP])
                last.then_inc(lri_done, 1)
            dve.wait_ge(lri_done, 3)
            dve.nop().then_inc(banks_free[unit.slot], 1)
            for ri in range(2):
                dve.wait_ge(banks_full[unit.slot], unit.full(1 + ri))
                for g2 in range(2):
                    half = slice(g2 * NS, (g2 + 1) * NS)
                    src = AB[unit.slot][1 + ri][half, :].rearrange("p (g e c) -> p g e c", e=2, c=C16)[:, :, g2, :]
                    dve.tensor_scalar(CA[half, :, ri, 0:C16], src, (1.0, -1.0)[ri], None, ALU.mult).then_inc(c_done, 1)
                dve.wait_ge(c_done, 2 * ri + 2)
                dve.nop().then_inc(banks_free[unit.slot], 1)

            ffn("1", DOWN1, WEIGHTS[("u", 0)])
            split_lo(1, WEIGHTS[("u", 1)])
            norm(UNITS["norm2"], 1, 0, 17, lambda tb: add_block(DOWN1 + NF - 1, tb))

            def next_lo(name):
                split_lo(UNITS[name].slot, WEIGHTS[name], WC if name[0] == "glu" else DC)

            for j in range(WC):
                next_lo(WEIGHTED[j + 2])
                if j == 0:
                    split_lo(2, DOWNC)

            unit = UNITS[("tab", 3)]
            dve.wait_ge(banks_free[unit.slot], unit.full(2))
            for g in range(GP):
                dve.tensor_scalar(DTM[:, :], DM[:, :], DT[:, g:g + 1], None, ALU.mult).then_inc(kt_done, 1)
                dve.wait_ge(kt_done, 2 * g + 1)
                dve.tensor_tensor(KT[:, g, 7 * C16:8 * C16], KT[:, g, 7 * C16:8 * C16], DTM[:, :], ALU.add
                                  ).then_inc(kt_done, 1)
                dve.wait_ge(kt_done, 2 * g + 2)
            dve.nop().then_inc(dt_k, 2)

            vb = UNITS["buffer"]
            steps = [0]

            def step_done(ins):
                steps[0] += 1
                ins.then_inc(conv_step, 1)
                dve.wait_ge(conv_step, steps[0])

            def taps(k):
                return CW[:, k, c:c + 1]

            for c in range(WC):
                i = WEIGHTED.index(("xc", c))
                next_lo(WEIGHTED[i + 2])
                xu, gu, bu = UNITS[("xc", c)], UNITS[("gc", c)], UNITS[("gb", c)]
                if c == 0:
                    dve.wait_ge(banks_full[vb.slot], vb.full(2))
                for tb in range(TB):
                    if c > 0:
                        add_block(DOWNC + c - 1, tb, 1.0)
                    dve.wait_ge(banks_full[gu.slot], gu.full(tb))
                    dve.wait_ge(banks_free[xu.slot], xu.full(tb))
                    if c > 0:
                        dve.wait_ge(h_ready, 3 * (DOWNC + c - 1) + 3)
                    take(dve, gu, tb)
                    dve.tensor_tensor(V[:, cols(tb)], AB[gu.slot][tb][:, 0:TW], S[:, cols(tb)], ALU.mult
                                      ).then_inc(banks_free[gu.slot], 1)
                next_lo(WEIGHTED[i + 3])
                dve.wait_ge(banks_free[gu.slot], gu.full(2))
                if c == 0:
                    dve.wait_ge(u_out[3], 16)
                    dve.wait_ge(banks_free[vb.slot], vb.full(2))
                    dve.wait_ge(xs_zero, 1)
                step_done(dve.tensor_copy(VPRE[:, :, 1:NK],
                                          V[:, 6 * NK:SEQ].rearrange("p (s k) -> p s k", k=NK)[:, :, 0:NK - 1]))
                step_done(dve.tensor_copy(VOUT[:, c, 0:DEC], V[:, SEQ:NT]))
                step_done(dve.tensor_copy(VOUT[:, c, DEC:DEC + 2],
                                          V[:, 6 * NK:SEQ].rearrange("p (s k) -> p s k", k=NK)[:, :, NK - 1]))
                step_done(dve.tensor_scalar(T[:, :], V[:, :], taps(2), None, ALU.mult))

                def tap(dst, src, k):
                    step_done(dve.scalar_tensor_tensor(dst, src, taps(k), dst, ALU.mult, ALU.add))
                tap(T[:, NK:SEQ], V[:, 0:SEQ - NK], 1)
                tap(T[:, 0:NK], VPRE[:, 1, :], 1)
                tap(T[:, 2 * NK:SEQ], V[:, 0:SEQ - 2 * NK], 0)
                tap(T[:, 0:2 * NK], VPRE[:, :, :].rearrange("p s k -> p (s k)"), 0)
                buf = CBT[:, c, :].rearrange("p (b r) -> p b r", r=2)
                tap(T[:, SEQ:NT], buf[:, :, 1], 1)
                tap(T[:, SEQ:NT], buf[:, :, 0], 0)
                for tb in range(TB):
                    dve.wait_ge(banks_full[bu.slot], bu.full(tb))
                    take(dve, bu, tb)
                    dve.tensor_tensor(T[:, cols(tb)], AB[bu.slot][tb][:, 0:TW], T[:, cols(tb)], ALU.mult
                                      ).then_inc(banks_free[bu.slot], 1)
                for tb in range(TB):
                    h_lo(DOWNC + c, c % 2, tb)
                next_lo(WEIGHTED[i + 4])
                if c >= 1:
                    split_lo(2, DOWNC + c)
            for tb in range(TB):
                add_block(DOWNC + 3, tb, 1.0)
            for tb in range(TB):
                for j in range(WC):
                    dve.wait_ge(z_hi, WC * tb + j + 1)
                    dve.tensor_tensor(ZL[:, j, cols(tb)], ZT[:, j, cols(tb)], f(ZH[:, j, cols(tb)]), ALU.subtract
                                      ).then_inc(z_ready, 1)
            split_lo(2, DOWNS)
            for j in range(WC):
                unit = UNITS[("glu", j)]
                for tb in range(TB):
                    dve.wait_ge(banks_free[unit.slot], unit.full(tb))
                    dve.wait_ge(h_ready, 3 * (DOWNS + j - 1) + tb + 1)
                    dve.tensor_tensor(T[:, cols(tb)], S[:, cols(tb)], ZT[:, j, cols(tb)], ALU.mult
                                      ).then_inc(gate_done, 1)
                for tb in range(TB):
                    h_lo(DOWNS + j, j % 2, tb)
                if j < 2:
                    next_lo(("glu", j + 2))
                if j >= 1:
                    for tb in range(TB):
                        add_block(DOWNS + j - 1, tb, 1.0)
                    split_lo(2, DOWNS + j)
                if j == 2:
                    split_lo(0, WEIGHTS["gate2"])
                if j == 3:
                    split_lo(1, WEIGHTS["up2"])
            norm(UNITS["norm3"], 2, 24, 41, lambda tb: add_block(DOWNS + 3, tb, 1.0))
            ffn("2", DOWN2, None)
            for tb in range(TB):
                add_block(DOWN2 + NF - 1, tb)
            dve.wait_ge(gf_in, 16)
            for s in range(S8 + 1):
                unit = UNITS[("out", s)]
                m = NK if s < S8 else DEC
                dve.wait_ge(sq_x, 9 + 2 * s + 2)
                take(dve, unit)
                dve.tensor_tensor(SS[0:m, s, 0:1], SS[0:m, s, 0:1], SS[0:m, s, 1:2], ALU.add).then_inc(ss_sum, 1)
                dve.wait_ge(sqrt_x, 3 + s + 1)
                dve.reciprocal(RS[0:m, s:s + 1], RS[0:m, s:s + 1]).then_inc(rcp_x, 1)
                dve.wait_ge(rcp_x, 3 + s + 1)
                if s >= 2:
                    dve.wait_ge(y_out[s % 2], 16 * (s // 2))
                for h in range(2):
                    span = slice(512 * h, 512 * (h + 1))
                    dve.scalar_tensor_tensor(OUT[0:m, s % 2, span], AB[unit.slot][h][0:m, :], RS[0:m, s:s + 1],
                                             GF[0:m, span], ALU.mult, ALU.mult).then_inc(out_done, 1)
                dve.wait_ge(out_done, 2 * s + 2)
                dve.nop().then_inc(banks_free[unit.slot], 3)

        @block.gpsimd
        def _(pool):
            count = [0]

            def chain(ins):
                count[0] += 1
                ins.then_inc(pool_step, 1)
                pool.wait_ge(pool_step, count[0])

            chain(pool.memset(IDENT[:, :], 0.0))
            pool.affine_select(out=IDENT[:, :], in_=IDENT[:, :], compare_op=ALU.not_equal, fill=1.0, base=0,
                               pattern=[[-1, P]], channel_multiplier=1).then_inc(const_done, 1)
            pool.memset(ONES[:, :], 1.0).then_inc(const_done, 1)
            pool.memset(EPSC[:, :], EPS).then_inc(const_done, 1)
            pool.memset(VOUT[:, :, :], 0.0)
            with nc.allow_non_contiguous_dma(reason="small parameters, channels to partitions"):
                for n, name in enumerate(("ffn1_norm", "mix_norm", "ffn2_norm")):
                    pool.dma_start(GAIN[:, n, :], a[name][0].rearrange("(c p) -> p c", p=P)).then_inc(consts_in, 16)
                pool.dma_start(CW[:, :, :], a["conv_w"][0].rearrange("k (c p) -> p k c", p=P)).then_inc(consts_in, 16)
                pool.dma_start(BG[:, :], a["ssm_b_glu"][0].rearrange("(c p) -> p c", p=P)).then_inc(consts_in, 16)
                pool.dma_start(DT[:, :], a["ssm_d"][0].rearrange("(g n) -> n g", n=32)).then_inc(consts_in, 16)
            chain(pool.memset(PAR[:, :], 0.0))
            pool.dma_start(PAR[0:GP, :], a["ssm_lambda_re"][0].rearrange("(g e) p -> g (e p)", e=2)).then_inc(par_in, 16)
            pool.dma_start(PAR[32:32 + GP, :], a["ssm_lambda_im"][0].rearrange("(g e) p -> g (e p)", e=2)
                           ).then_inc(par_in, 16)
            pool.dma_start(TMP[64:64 + GP, 0, 0:2], a["ssm_log_dt"][0].rearrange("(g e) -> g e", e=2)).then_inc(dt_in, 16)
            for ri, name in enumerate(("ssm_c_re", "ssm_c_im")):
                src = a[name][0].rearrange("(q g) c p -> (g c) q p", q=4)
                for twice in range(2):
                    pool.dma_start(CL[:, ri, :, twice * NS:(twice + 1) * NS], src).then_inc(c_in, 16)
            for ri, name in enumerate(("ssm_b_re", "ssm_b_im")):
                pool.dma_start(BRAW[:, ri, :, :], a[name][0].rearrange("(g e) p c -> (e p) g c", e=2)).then_inc(b_in, 16)
            pool.wait_ge(par_in, 32)
            pool.nop().then_inc(par_set, 1)
            pool.wait_ge(dt_in, 16)
            for e in range(2):
                pool.tensor_copy(PAR[64:64 + GP, e * NS:(e + 1) * NS],
                                 TMP[64:64 + GP, 0, e:e + 1].broadcast_to([GP, NS])).then_inc(par_set, 1)

            t = lambda n: TMP[:, n, :]

            def tt(out, x, y, op):
                chain(pool.tensor_tensor(out, x, y, op))

            def ts(out, x, s1, op1, s2=None, op2=None):
                if op2 is None:
                    chain(pool.tensor_scalar(out, x, s1, None, op1))
                else:
                    chain(pool.tensor_scalar(out, x, s1, s2, op1, op2))

            lr, li = LRI[:, 0, :], LRI[:, 1, :]
            pool.wait_ge(disc_a, 1)
            tt(t(1), lr, t(0), ALU.mult)
            tt(t(2), li, t(0), ALU.mult)
            ts(t(7), t(2), 1.0 / TWO_PI, ALU.mult)
            ts(t(7), t(7), MAGIC, ALU.add)
            ts(t(7), t(7), MAGIC, ALU.subtract)
            for part in (PI_A, PI_B, PI_C):
                ts(t(8), t(7), part, ALU.mult)
                tt(t(2), t(2), t(8), ALU.subtract)
            ts(t(2), t(2), 3.1415925, ALU.min, -3.1415925, ALU.max)
            ts(t(8), t(2), -1.0, ALU.mult)
            chain(pool.tensor_scalar(t(9), t(2), 0.0, None, ALU.max))
            chain(pool.tensor_scalar(t(8), t(8), 0.0, None, ALU.max))
            tt(t(6), t(9), t(8), ALU.add)
            ts(t(6), t(6), -1.0, ALU.mult, float(np.pi / 2), ALU.add)
            pool.nop().then_inc(disc_p, 1)
            pool.wait_ge(disc_a, 4)
            ar, ai, nai = AP8[:, 7, 0, :], AP8[:, 7, 1, :], AP8[:, 7, 2, :]
            tt(ar, t(3), t(5), ALU.mult)
            tt(ai, t(3), t(4), ALU.mult)
            tt(t(7), lr, lr, ALU.mult)
            tt(t(8), li, li, ALU.mult)
            tt(t(7), t(7), t(8), ALU.add)
            pool.nop().then_inc(disc_p, 1)
            ts(t(8), ar, -1.0, ALU.add)
            tt(t(9), t(8), lr, ALU.mult)
            tt(t(10), ai, li, ALU.mult)
            tt(t(9), t(9), t(10), ALU.add)
            tt(t(10), ai, lr, ALU.mult)
            tt(t(11), t(8), li, ALU.mult)
            tt(t(10), t(10), t(11), ALU.subtract)
            pool.wait_ge(den_inv, 1)
            tt(t(9), t(9), t(12), ALU.mult)
            tt(t(10), t(10), t(12), ALU.mult)
            pool.wait_ge(b_in, 32)
            pool.wait_ge(c_done, 4)

            def over(x, n=C16):
                return x.rearrange("p (g o) -> p g o", o=1).broadcast_to([P, GP, n])

            D1 = PROD[:, 0]
            D2 = PROD[:, 1]
            br, bi = BRAW[:, 0], BRAW[:, 1]

            def bs(ri, s):
                return BS[:, :, ri, s * C16:(s + 1) * C16]

            def ca(ri, j):
                return CA[:, :, ri, j * C16:(j + 1) * C16]

            def rotate(out_r, out_i, in_r, in_i, cr, ci, sign):
                tt(D1, in_r, over(cr), ALU.mult)
                tt(D2, in_i, over(ci), ALU.mult)
                tt(out_r, D1, D2, ALU.subtract if sign == 1 else ALU.add)
                tt(D1, in_i, over(cr), ALU.mult)
                tt(D2, in_r, over(ci), ALU.mult)
                tt(out_i, D1, D2, ALU.add if sign == 1 else ALU.subtract)

            rotate(bs(0, 7), bs(1, 7), br, bi, t(9), t(10), 1)
            for s in range(6, -1, -1):
                rotate(bs(0, s), bs(1, s), bs(0, s + 1), bs(1, s + 1), ar, ai, 1)
            for j in range(1, 9):
                rotate(ca(0, j), ca(1, j), ca(0, j - 1), ca(1, j - 1), ar, ai, -1)
            chain(pool.memset(BD[:, :, :, :], 0.0))
            for ri in range(2):
                chain(pool.tensor_copy(BD[0:NS, :, ri, 0:C16], BS[0:NS, :, ri, 7 * C16:]))
                chain(pool.tensor_copy(BD[NS:P, :, ri, C16:], BS[NS:P, :, ri, 7 * C16:]))
            pool.dma_start(CAD, CA[:, :, :, :].rearrange("p g r n -> p (g r) n")).then_inc(ca_out, 16)

            def square_of(x, out_r, out_i):
                tt(t(0), x[0], x[0], ALU.mult)
                tt(t(1), x[1], x[1], ALU.mult)
                tt(t(2), x[0], x[1], ALU.mult)
                tt(out_r, t(0), t(1), ALU.subtract)
                tt(out_i, t(2), t(2), ALU.add)
            chain(pool.tensor_copy(t(12), ar))
            chain(pool.tensor_copy(t(13), ai))
            square_of((ar, ai), t(3), t(4))
            square_of((t(3), t(4)), t(5), t(6))
            square_of((t(5), t(6)), AP8[:, 0, 0, :], AP8[:, 0, 1, :])
            for i in range(1, 8):
                x, y = (AP8[:, i - 1, 0, :], AP8[:, i - 1, 1, :]), (AP8[:, 0, 0, :], AP8[:, 0, 1, :])
                tt(t(0), x[0], y[0], ALU.mult)
                tt(t(1), x[1], y[1], ALU.mult)
                tt(AP8[:, i, 0, :], t(0), t(1), ALU.subtract)
                tt(t(0), x[0], y[1], ALU.mult)
                tt(t(1), x[1], y[0], ALU.mult)
                tt(AP8[:, i, 1, :], t(0), t(1), ALU.add)
            chain(pool.tensor_scalar(AP8[:, :, 2, :], AP8[:, :, 1, :], -1.0, None, ALU.mult))
            ts(t(11), t(13), -1.0, ALU.mult)
            tt(DM[:, :], IDENT[0:32, 0:C16], IDENT[0:32, C16:32], ALU.add)
            pool.wait_ge(consts_in, 16 * 6)
            pool.nop().then_inc(disc_p, 2)
            tab = UNITS[("tab", 2)]
            pool.wait_ge(banks_full[tab.slot], tab.full(1))
            pool.wait_ge(ca_out, 16)
            chain(pool.memset(KT[:, :, 0:7 * C16], 0.0))
            pool.nop().then_inc(disc_p, 1)
            tab = UNITS[("tab", 3)]
            pool.wait_ge(banks_full[tab.slot], tab.full(2))
            pool.wait_ge(t0_out, 16 * 16)
            pool.memset(XS[:, :, DEC:DEC + 1], 0.0)
            chain(pool.memset(VPRE[:, :, 0:1], 0.0))
            pool.nop().then_inc(xs_zero, 1)
            pool.memset(U[:, :, 0:DEC], 0.0)
            chain(pool.memset(U[:, :, DEC + NK:UC], 0.0))
            pool.nop().then_inc(u_zero, 1)

            v3 = UNITS[("v", 3)]
            pool.wait_ge(banks_free[v3.slot], v3.full(2))
            v2 = UNITS[("v", 2)]
            pool.wait_ge(banks_free[v2.slot], v2.full(2))
            main = XS[:, :, DEC + 1:DEC + 1 + NK].rearrange("p g (b i) -> p g b i", i=8)

            def power(i, what, n, both):
                x = (AP8[:, i, what, :] if i >= 0 else t({0: 12, 1: 13, 2: 11}[what]))
                x = x.rearrange("p (r g o) -> p r g o", r=1, o=1)
                return x.broadcast_to([P, 2, GP, n]) if both else x[:, 0].broadcast_to([P, GP, n])

            def advance(dst, src, i, n):
                t1, t2 = ST1[:, :, :, 0:n], ST2[:, :, :, 0:n]
                halves = (slice(0, GP), slice(GP, 2 * GP))
                src4 = src.rearrange("p (r g) n -> p r g n", r=2)
                dst4 = dst.rearrange("p (r g) n -> p r g n", r=2)
                pool.tensor_tensor(t1, src4, power(i, 0, n, True), ALU.mult).then_inc(pool_step, 1)
                pool.tensor_tensor(t2[:, 0], src[:, halves[1], :], power(i, 2, n, False), ALU.mult).then_inc(pool_step, 1)
                count[0] += 2
                tt(t2[:, 1], src[:, halves[0], :], power(i, 1, n, False), ALU.mult)
                tt(dst4, dst4, t1, ALU.add)
                tt(dst4, dst4, t2, ALU.add)

            for i in range(1, 8):
                advance(main[:, :, :, i], main[:, :, :, i - 1], 0, 16)
            for b in range(1, 16):
                advance(main[:, :, b, 7:8], main[:, :, b - 1, 7:8], 7, 1)
            for i in range(7):
                advance(main[:, :, 1:16, i], main[:, :, 0:15, 7], i, 15)
            advance(XS[:, :, XC - DEC:XC], XS[:, :, 0:DEC], -1, DEC)
            for ri in range(2):
                chain(pool.tensor_copy(DNEW[:, ri, :].rearrange("p (t g) -> p g t", g=GP),
                                       XS[:, ri * GP:(ri + 1) * GP, XC - DEC:XC]))
            pool.nop().then_inc(scanned, 1)
            last = UNITS[("gb", 3)]
            pool.wait_ge(banks_full[last.slot], last.full(2))
            for g2 in range(2):
                half = slice(g2 * NS, (g2 + 1) * NS)
                chain(pool.memset(CB[half, :, :, 1 - g2, :], 0.0))
            pool.nop().then_inc(cb_zero, 1)


_OUTS = [("y_prompt", (1, SEQ, D)), ("y_sample", (DEC, 1, D)), ("re_prompt", (1, 1, G, NS)), ("im_prompt", (1, 1, G, NS)),
         ("conv_prompt", (1, 1, 2, W)), ("re_sample", (1, DEC, G, NS)), ("im_sample", (1, DEC, G, NS)),
         ("conv_sample", (1, DEC, 2, W))]


def kernel(**inputs):
    import concourse.bacc as bacc
    from concourse.bass_utils import run_bass_kernel_spmd

    nc = bacc.Bacc("TRN2", target_bir_lowering=False, num_devices=1)
    arrays, ins, outs = {}, {}, {}
    for name, value in inputs.items():
        arrays["in_" + name] = np.ascontiguousarray(value)
        ins[name] = nc.dram_tensor("in_" + name, arrays["in_" + name].shape, F32, kind="ExternalInput").ap()
    for name, shape in _OUTS:
        outs[name] = nc.dram_tensor("out_" + name, shape, F32, kind="ExternalOutput").ap()
    hybrid_trunk(nc, ins, outs)
    result = run_bass_kernel_spmd(nc, [arrays], core_ids=[0]).results[0]
    return tuple(result["out_" + name] for name, _ in _OUTS)
```

```python
from contextlib import ExitStack

import numpy as np

import concourse.bass as bass
from concourse import mybir

F32 = mybir.dt.float32
F32R = mybir.dt.float32r
ALU = mybir.AluOpType
ACT = mybir.ActivationFunctionType

P = 128
D = 1024
DC = D // P
SEQ = 1024
DEC = 8
S8 = 8
NK = SEQ // S8
NT = SEQ + DEC
TB = 3
TW = NT // TB
QW = TW // 4
XN = TB * DC
FF = 2816
NF = FF // P
W = 512
WC = W // P
G = 32
GP = G // 2
C16 = 16
NS = 64
EPS = 1e-6
UC = DEC + NK + DEC
XC = DEC + 1 + NK + DEC
YC = DEC + NK
MAGIC = 12582912.0
TWO_PI = 2 * np.pi
PI_A = 6.28125
PI_B = round((TWO_PI - PI_A) * 2**19) / 2**19
PI_C = TWO_PI - PI_A - PI_B


class Unit:

    def __init__(self, slot, before):
        self.slot, self.before = slot, before

    def full(self, bank):
        return 3 * self.before + bank + 1

    def at(self, step):
        return Unit(self.slot, self.before + step)


def plan():
    units, used, weights, loaded = {}, [0, 0], {}, [0, 0, 0]

    def add(name, slot, weighted=False, times=1):
        units[name] = Unit(slot, used[slot])
        used[slot] += times
        if weighted:
            weights[name] = loaded[slot]
            loaded[slot] += times

    for n in range(3):
        add(("rms", n), 1)
    add("gate1", 0, True, NF)
    add("up1", 1, True, NF)
    add("norm2", 1)
    for j in range(WC):
        add(("u", j), j % 2, True)
    for n in range(4):
        add(("tab", n), n % 2)
    add("carried", 0)
    add("buffer", 1)
    n = 0
    for c in range(WC):
        for what in ("xc", "gc", "gb"):
            add((what, c), n % 2, True)
            n += 1
        if c == 0:
            for v in range(4):
                add(("v", v), (n + v) % 2)
    for j in range(4):
        add(("y", j), j % 2)
    add("states", 0)
    add("vout", 1)
    for j in range(WC):
        add(("glu", j), j % 2, True)
    add("norm3", 1)
    add("gate2", 0, True, NF)
    add("up2", 1, True, NF)
    for s in range(S8 + 1):
        add(("out", s), s % 2)
    return units, weights


UNITS, WEIGHTS = plan()
WEIGHTED = [("u", j) for j in range(WC)]
for _c in range(WC):
    WEIGHTED += [("xc", _c), ("gc", _c), ("gb", _c)]
WEIGHTED += [("glu", j) for j in range(WC)]

DOWN1, DOWNC, DOWNS, DOWN2 = 0, NF, NF + WC, NF + 2 * WC
ND = 2 * NF + 2 * WC
TILES = TB * DC

V_ITEMS = 2 * GP
V_BANKS = [list(range(b, min(b + 3, V_ITEMS))) for b in range(0, V_ITEMS, 3)]
Y_BANKS = [[0, 1, 2], [3, 4, 5], [6, 7]]


def hybrid_trunk(nc, a, o):
    ctx = ExitStack()

    def sb(name, shape, dt=F32, stack=ctx):
        return stack.enter_context(nc.sbuf_tensor(name, shape, dt))

    def sem(name):
        return ctx.enter_context(nc.semaphore(name))

    def dram(name, shape):
        return nc.dram_tensor(name, shape, F32, kind="Internal").ap()

    with ctx:
        HT = sb("HT", [P, DC, NT])
        RAW = sb("RAW", [P, 3, D])
        WH = sb("WH", [P, 3, D], F32R)
        WL = sb("WL", [P, 3, D], F32R)
        IDENT = sb("IDENT", [P, P])
        ONES = sb("ONES", [P, P])
        S = sb("S", [P, NT])
        T = sb("T", [P, NT])
        GAIN = sb("GAIN", [P, 3, DC])
        EPSC = sb("EPSC", [P, 1])
        CW = sb("CW", [P, 3, WC])
        BG = sb("BG", [P, WC])
        CBT = sb("CBT", [P, WC, 2 * DEC])
        VOUT = sb("VOUT", [P, WC, 16])
        SS = sb("SS", [P, S8 + 1, 2])
        RS = sb("RS", [P, S8 + 1])
        RQ = sb("RQ", [QW, 2 * TB, 4])
        LRI = sb("LRI", [P, 3, GP])
        TMP = sb("TMP", [P, 14, GP])
        AP8 = sb("AP8", [P, S8, 3, GP])
        DT = sb("DT", [32, GP])
        DM = sb("DM", [32, C16])
        st = ExitStack()
        XD = sb("XD", [DEC, D], F32, st)
        JUNK = sb("JUNK", [P, D], F32, st)
        st.close()
        WT = sb("WT", [P, GP, 2, P], F32, st)
        st.close()
        HH = sb("HH", [P, 2, NT], F32R)
        HL = sb("HL", [P, 2, NT], F32R)
        st = ExitStack()
        PROD = sb("PROD", [P, 2, GP, C16], F32, st)
        st.close()
        CARR = sb("CARR", [P, 2, P], F32, st)
        CBUF = sb("CBUF", [16, W], F32, st)
        st.close()
        R = sb("R", [P, NT])
        V = R
        st = ExitStack()
        BRAW = sb("BRAW", [P, 2, GP, C16], F32, st)
        PAR = sb("PAR", [96, P], F32, st)
        st.close()
        ST1 = sb("ST1", [P, 2, GP, GP], F32, st)
        ST2 = sb("ST2", [P, 2, GP, GP], F32, st)
        st.close()
        SQ = sb("SQ", [P, NT])
        st = ExitStack()
        T0 = sb("T0", [P, GP, 2, P], F32, st)
        CB = sb("CB", [P, GP, 2, 2, P], F32, st)
        Z = sb("Z", [P, 2, 8, YC], F32, st)
        st.close()
        ZH = sb("ZH", [P, WC, NT], F32R, st)
        ZL = sb("ZL", [P, WC, NT], F32R, st)
        st.close()
        XH = sb("XH", [P, DC, NT], F32R)
        XL = sb("XL", [P, DC, NT], F32R)
        st = ExitStack()
        X = sb("X", [P, S8, D], F32, st)
        st.close()
        CA = sb("CA", [P, GP, 2, 9 * C16], F32, st)
        BD = sb("BD", [P, GP, 2, 2 * C16], F32, st)
        st2 = ExitStack()
        CL = sb("CL", [P, 2, 4, P], F32, st2)
        st2.close()
        BS = sb("BS", [P, GP, 2, P], F32, st)
        st.close()
        sb("over_CA", [P, GP, 2, 9 * C16], F32, st)
        sb("over_BD", [P, GP, 2, 2 * C16], F32, st)
        KT = sb("KT", [32, GP, 15 * C16], F32, st)
        DTM = sb("DTM", [32, C16], F32, st)
        st.close()
        U = sb("U", [P, G, UC], F32, st)
        XS = sb("XS", [P, 2 * GP, XC], F32, st)
        VPRE = sb("VPRE", [P, 2, NK], F32, st)
        DNEW = sb("DNEW", [P, 2, P], F32, st)
        st.close()
        ZT = sb("ZT", [P, WC, NT], F32, st)
        STO = sb("STO", [P, 4, P], F32, st)
        VO = sb("VO", [16, W], F32, st)
        st.close()
        OUT = sb("OUT", [P, 2, D], F32, st)
        GF = sb("GF", [P, D], F32, st)
        st.close()

        AB = [[ctx.enter_context(nc.psum_tensor(f"bank{s}{b}", [P, 512], F32)) for b in range(3)] for s in range(2)]
        DB = [ctx.enter_context(nc.psum_tensor(f"bank_down{b}", [P, 512], F32)) for b in range(2)]

        UD = dram("u_scratch", [W, NT])
        ZD = dram("z_scratch", [W, NT])
        CAD = dram("ca_scratch", [P, GP * 2, 9 * C16])
        T0D = dram("t0_scratch", [P, GP, 2, P])

        banks_full = [sem("banks_full_0"), sem("banks_full_1")]
        banks_free = [sem("banks_free_0"), sem("banks_free_1")]
        raw_full = [sem(f"raw_full_{s}") for s in range(3)]
        w_hi = [sem(f"w_hi_{s}") for s in range(3)]
        w_split = [sem(f"w_split_{s}") for s in range(3)]
        hi_done = sem("hi_done")
        h_ready = sem("h_ready")
        down_full = sem("down_full")
        down_free = sem("down_free")
        gate_done = sem("gate_done")
        x_in = [sem(f"x_in_{s}") for s in range(S8 + 1)]
        sq_x = sem("sq_x")
        sqrt_x = sem("sqrt_x")
        ss_sum = sem("ss_sum")
        rcp_x = sem("rcp_x")
        diag_x = sem("diag_x")
        xt_full = sem("xt_full")
        xt_free = sem("xt_free")
        par_full = sem("par_full")
        par_free = sem("par_free")
        xn_hi = sem("xn_hi")
        xn_ready = sem("xn_ready")
        xn_tmp = sem("xn_tmp")
        sq_done = sem("sq_done")
        acc_done = sem("acc_done")
        sums_done = sem("sums_done")
        rt_done = sem("rt_done")
        rcp_done = sem("rcp_done")
        diag_done = sem("diag_done")
        const_done = sem("const_done")
        gain_in = sem("gain_in")
        consts_in = sem("consts_in")
        c_in = sem("c_in")
        b_in = sem("b_in")
        par_in = sem("par_in")
        dt_in = sem("dt_in")
        par_set = sem("par_set")
        lri_done = sem("lri_done")
        c_done = sem("c_done")
        disc_a = sem("disc_a")
        disc_p = sem("disc_p")
        den_inv = sem("den_inv")
        pool_step = sem("pool_step")
        ca_out = sem("ca_out")
        kt_done = sem("kt_done")
        dt_k = sem("dt_k")
        t0_out = sem("t0_out")
        u_out = [sem(f"u_out_{j}") for j in range(WC)]
        u_zero = sem("u_zero")
        u_in = sem("u_in")
        carr_in = sem("carr_in")
        cbt_done = sem("cbt_done")
        xs_zero = sem("xs_zero")
        scanned = sem("scanned")
        conv_step = sem("conv_step")
        cb_zero = sem("cb_zero")
        y_tab = [sem(f"y_tab_{j}") for j in range(WC)]
        z_out = [sem(f"z_out_{j}") for j in range(WC)]
        zt_in = [sem(f"zt_in_{j}") for j in range(WC)]
        z_hi = sem("z_hi")
        z_ready = sem("z_ready")
        small_out = sem("small_out")
        st_out = sem("st_out")
        gf_in = sem("gf_in")
        out_done = sem("out_done")
        y_out = [sem("y_out_0"), sem("y_out_1")]

        block = ctx.enter_context(nc.Block())

        def cols(tb):
            return slice(tb * TW, (tb + 1) * TW)

        def ring(i):
            return (S, T)[i % 6 // 3][:, (i % 3) * TW:(i % 3 + 1) * TW]

        def take(eng, unit, bank=0):
            eng.wait_ge(banks_free[unit.slot], 3 * unit.before + bank)

        def last_tile(d):
            return TILES * (d + 1)

        x_rows = a["x_prompt"].rearrange("b (k s) d -> (b k) s d", s=S8)
        xs_rows = a["x_sample"].rearrange("b t d -> (b t) d")
        w_in = a["w_in"][0]

        def columns(w, n, k=DC):
            return w.rearrange("(c p) m -> p c m", p=P)[:, 0:k, n * P:(n + 1) * P] if isinstance(n, int) \
                else w.rearrange("(c p) m -> p c m", p=P)[:, 0:k, bass.ds(n * P, P)]

        def weights_of(name):
            what, j = name
            if what == "glu":
                return columns(a["ssm_w_glu"][0], j, WC)
            first = {"u": 0, "xc": W, "gb": 2 * W, "gc": 3 * W}[what] // P
            return columns(w_in, first + j)

        def down_rows(w, f):
            return w[f * P:(f + 1) * P, :] if isinstance(f, int) else w[bass.ds(f * P, P), :]

        @block.sync
        def _(sp):
            def load(slot, n, src):
                if not (isinstance(n, int) and n == 0):
                    sp.wait_ge(w_split[slot], n)
                k = src.shape[1] if slot < 2 else DC
                dst = RAW[:, slot, 0:k * P]
                if slot < 2:
                    dst = dst.rearrange("p (c m) -> p c m", m=P)
                sp.dma_start(dst, src).then_inc(raw_full[slot], 16)

            def load_named(name):
                load(UNITS[name].slot, WEIGHTS[name], weights_of(name))

            for s in range(2):
                sp.dma_start(X[:, s, :], x_rows[:, s, :]).then_inc(x_in[s], 16)
            load(0, 0, columns(a["ffn1_w_gate"][0], 0))
            for s in range(2, S8):
                sp.dma_start(X[:, s, :], x_rows[:, s, :]).then_inc(x_in[s], 16)
            sp.dma_start(XD[:, :], xs_rows).then_inc(x_in[S8], 16)
            load(1, 0, columns(a["ffn1_w_up"][0], 0))
            sp.dma_start(o["conv_sample"][0, :, 0, :], a["state_conv"][0, :, 1, :]).then_inc(small_out, 16)
            load(2, 0, down_rows(a["ffn1_w_down"][0], 0))

            def ffn_rest(which, wg, wu, wd, down):
                with sp.Fori(1, NF) as f:
                    load(0, f + WEIGHTS["gate" + which], columns(wg, f))
                    load(1, f + WEIGHTS["up" + which], columns(wu, f))
                    load(2, f + down, down_rows(wd, f))

            ffn_rest("1", a["ffn1_w_gate"][0], a["ffn1_w_up"][0], a["ffn1_w_down"][0], DOWN1)

            for j in range(2):
                load_named(("u", j))
            sp.wait_ge(xn_ready, 2 * XN)
            for ri, name in enumerate(("state_ssm_re", "state_ssm_im")):
                sp.dma_start(CARR[:, ri, :], a[name][0].rearrange("b (g e) p -> (b g) (e p)", e=2)).then_inc(carr_in, 16)
            sp.dma_start(CBUF[:, :], a["state_conv"][0].rearrange("b r c -> (b r) c")).then_inc(carr_in, 16)
            def store_u(j):
                unit = UNITS[("u", j)]
                sp.wait_ge(banks_free[unit.slot], unit.full(2))
                sp.dma_start(UD[j * P:(j + 1) * P, :], (S, T)[j % 2][:, :]).then_inc(u_out[j], 16)

            load_named(("u", 2))
            load(2, DOWNC, down_rows(a["w_out"][0], WC))
            load_named(("u", 3))
            store_u(0)
            load_named(("xc", 0))
            store_u(1)
            load_named(("gc", 0))
            store_u(2)
            load_named(("gb", 0))
            store_u(3)
            sp.wait_ge(dt_k, 2)
            for s in range(S8):
                for g2 in range(2):
                    sp.dma_start(T0D[s * C16:(s + 1) * C16, :, g2, :],
                                 KT[g2 * C16:(g2 + 1) * C16, :, (7 - s) * C16:(7 - s) * C16 + P]).then_inc(t0_out, 16)

            for j in range(WC):
                sp.wait_ge(u_out[j], 16)
            sp.wait_ge(u_zero, 1)
            ug = UD.rearrange("(g c) n -> c g n", c=C16)
            for s in range(S8):
                sp.dma_start(U[s * C16:(s + 1) * C16, :, DEC:DEC + NK], ug[:, :, s * NK:(s + 1) * NK]).then_inc(u_in, 16)
            with nc.allow_non_contiguous_dma(reason="32 bytes a row, small"):
                sp.dma_start(U[0:C16, :, 0:DEC], ug[:, :, SEQ:NT]).then_inc(u_in, 16)
                sp.dma_start(U[P - C16:P, :, DEC + NK:UC], ug[:, :, SEQ:NT]).then_inc(u_in, 16)

            for c in range(1, WC):
                for what in ("xc", "gc", "gb"):
                    load_named((what, c))
                load(2, DOWNC + c, down_rows(a["w_out"][0], WC + c))
            load_named(("glu", 0))
            sp.wait_ge(cb_zero, 1)
            sp.wait_ge(t0_out, 16 * 16)
            sp.wait_ge(ca_out, 16)
            for j in range(WC):
                q = slice(4 * j, 4 * j + 4)
                sp.dma_start(T0[:, q], T0D[:, q]).then_inc(y_tab[j], 16)
                for g2 in range(2):
                    half = slice(g2 * NS, (g2 + 1) * NS)
                    sp.dma_start(CB[half, q, :, g2, :].rearrange("p g r n -> p (g r) n"),
                                 CAD[half, 8 * j:8 * j + 8, C16:]).then_inc(y_tab[j], 16)
            load_named(("glu", 1))
            for j in range(WC):
                unit = UNITS[("y", j)]
                sp.wait_ge(banks_free[unit.slot], unit.full(2))
                zg = ZD[j * P:(j + 1) * P, :].rearrange("(g c) n -> c g n", c=C16)
                for t in range(S8):
                    sp.dma_start(zg[:, :, t * NK:(t + 1) * NK],
                                 Z[t * C16:(t + 1) * C16, j % 2, :, DEC:YC]).then_inc(z_out[j], 16)
                with nc.allow_non_contiguous_dma(reason="32 bytes a row, small"):
                    sp.dma_start(zg[:, :, SEQ:NT], Z[0:C16, j % 2, :, 0:DEC]).then_inc(z_out[j], 16)
            unit = UNITS["states"]
            sp.wait_ge(banks_full[unit.slot], unit.full(2))
            for j in range(WC):
                sp.wait_ge(z_out[j], 16 * 9)
                sp.dma_start(ZT[:, j, :], ZD[j * P:(j + 1) * P, :]).then_inc(zt_in[j], 16)
            load(2, DOWNS, down_rows(a["w_out"][0], 0))
            sp.wait_ge(st_out, 2)
            for ri, (ps, ss) in enumerate((("re_prompt", "re_sample"), ("im_prompt", "im_sample"))):
                sp.dma_start(o[ps][0, 0].rearrange("(g e) p -> g (e p)", e=2), STO[0:GP, 2 + ri, :]).then_inc(small_out, 16)
                sp.dma_start(o[ss][0].rearrange("b (g e) p -> (b g) (e p)", e=2), STO[:, ri, :]).then_inc(small_out, 16)
            sp.dma_start(o["conv_sample"][0, :, 1, :], VO[0:DEC, :]).then_inc(small_out, 16)
            sp.dma_start(o["conv_prompt"][0, 0], VO[DEC:DEC + 2, :]).then_inc(small_out, 16)
            for j in range(2, WC):
                load_named(("glu", j))
                load(2, DOWNS + j - 1, down_rows(a["w_out"][0], j - 1))
            load(0, WEIGHTS["gate2"], columns(a["ffn2_w_gate"][0], 0))
            load(2, DOWNS + 3, down_rows(a["w_out"][0], 3))
            load(1, WEIGHTS["up2"], columns(a["ffn2_w_up"][0], 0))
            load(2, DOWN2, down_rows(a["ffn2_w_down"][0], 0))
            ffn_rest("2", a["ffn2_w_gate"][0], a["ffn2_w_up"][0], a["ffn2_w_down"][0], DOWN2)
            sp.wait_ge(small_out, 16 * 7)
            sp.dma_start(GF[:, :], a["final_norm"].rearrange("(o d) -> o d", o=1).to_broadcast([P, D])).then_inc(gf_in, 16)
            y_rows = o["y_prompt"].rearrange("b (k s) d -> (b k) s d", s=S8)
            for s in range(S8 + 1):
                sp.wait_ge(out_done, 2 * s + 2)
                if s < S8:
                    sp.dma_start(y_rows[:, s, :], OUT[:, s % 2, :]).then_inc(y_out[s % 2], 16)
                else:
                    sp.dma_start(o["y_sample"].rearrange("b t d -> (b t) d"), OUT[0:DEC, s % 2, :]).then_inc(y_out[s % 2], 16)
            sp.wait_ge(y_out[0], 16 * 5)
            sp.wait_ge(y_out[1], 16 * 4)

        @block.tensor
        def _(pe):
            def product3(out, wh, wl, xh, xl, first, last):
                pe.matmul(out, wh, xh, start=first, stop=False)
                pe.matmul(out, wh, xl, start=False, stop=False)
                return pe.matmul(out, wl, xh, start=False, stop=last)

            def bank_wait(unit, b):
                if isinstance(unit.before, int) and unit.before == 0:
                    return
                pe.wait_ge(banks_free[unit.slot], 3 * unit.before + b - 2)

            def down_tile(d, par, tb, j):
                tile = TILES * d + DC * tb + j
                if isinstance(d, int) and d == 0 and tb == 0 and j < 2:
                    pe.wait_ge(par_free, 3)
                else:
                    pe.wait_ge(down_free, tile - 1)
                out = DB[(DC * tb + j) % 2][:, 0:TW]
                m = slice(j * P, (j + 1) * P)
                product3(out, WH[:, 2, m], WL[:, 2, m], HH[:, par, cols(tb)], HL[:, par, cols(tb)], True, True
                         ).then_inc(down_full, 1)

            def down_start(d):
                pe.wait_ge(w_split[2], d + 1)

            def down_block(d, par, tb):
                pe.wait_ge(h_ready, 3 * d + tb + 1)
                for j in range(DC):
                    down_tile(d, par, tb, j)

            def project(unit, weight, xh=XH, xl=XL, k=DC, x_wait=None, xn=None, down=None, after={}):
                pe.wait_ge(w_split[unit.slot], weight + 1)
                if down is not None:
                    down_start(down[0])
                for tb in range(TB):
                    if x_wait is not None:
                        pe.wait_ge(*x_wait[tb])
                    bank_wait(unit, tb)
                    if down is not None:
                        pe.wait_ge(h_ready, 3 * down[0] + tb + 1)
                    out = AB[unit.slot][tb][:, 0:TW]
                    for c in range(k):
                        m = slice(c * P, (c + 1) * P)
                        if xn is not None:
                            pe.wait_ge(xn_ready, XN * xn + DC * tb + c + 1)
                        last = product3(out, WH[:, unit.slot, m], WL[:, unit.slot, m], xh[:, c, cols(tb)],
                                        xl[:, c, cols(tb)], c == 0, c == k - 1)
                        if c == k - 1:
                            last.then_inc(banks_full[unit.slot], 1)
                        if down is not None:
                            down_tile(down[0], down[1], tb, c)
                        if (tb, c) in after:
                            after[tb, c]()

            def norm_sums(unit, k, tb):
                bank_wait(unit, tb)
                pe.wait_ge(acc_done, (DC - 1) * (TB * (k - 1) + tb + 1))
                for q in range(4):
                    at = tb * TW + q * QW
                    last = pe.matmul(AB[unit.slot][tb][0:QW, TW + q:TW + q + 1], R[:, at:at + QW], ONES[:, 0:1],
                                     start=True, stop=True)
                last.then_inc(sums_done, 1)

            def norm_spread(unit, k, tb):
                for q in range(4):
                    at = tb * TW + q * QW
                    pe.wait_ge(diag_done, 4 * (TB * (k - 1) + tb) + q + 1)
                    last = pe.matmul(AB[unit.slot][tb][:, q * QW:(q + 1) * QW], ONES[0:QW, :], R[0:QW, at:at + QW],
                                     start=True, stop=True)
                last.then_inc(banks_full[unit.slot], 1)

            def last_down(d, unit, k):
                down_start(d)
                for tb in range(TB):
                    pe.wait_ge(h_ready, 3 * d + tb + 1)
                    for j in range(DC):
                        down_tile(d, d % 2, tb, j)
                        if tb > 0 and j == 4:
                            norm_sums(unit, k, tb - 1)
                        if tb > 0 and j == DC - 1:
                            norm_spread(unit, k, tb - 1)
                return {(0, 3): lambda: norm_sums(unit, k, TB - 1), (1, 0): lambda: norm_spread(unit, k, TB - 1)}

            def ffn(which, down, xn, after, between):
                ug, uu = UNITS["gate" + which], UNITS["up" + which]
                wg, wu = WEIGHTS["gate" + which], WEIGHTS["up" + which]
                project(ug, wg, xn=xn, after=after)
                project(uu, wu)
                if between is not None:
                    between()

                def step(f, par):
                    project(ug.at(f), f + wg)
                    project(uu.at(f), f + wu, down=(f + (down - 1), par))
                step(1, 0)
                step(2, 1)
                with pe.Fori(1, (NF - 2) // 2) as i:
                    step(i * 2 + 1, 0)
                    step(i * 2 + 2, 1)
                step(NF - 1, 0)

            pe.wait_ge(const_done, 3)

            def x_transpose(s):
                pe.wait_ge(x_in[s], 16)
                for h in range(2):
                    if s > 0:
                        pe.wait_ge(xt_free, 2 * s + h - 1)
                    for c in range(4 * h, 4 * h + 4):
                        m = slice(c * P, (c + 1) * P)
                        if s < S8:
                            last = pe.transpose(DB[h][:, (c % 4) * P:(c % 4 + 1) * P], X[:, s, m], IDENT[:, :])
                        else:
                            last = pe.transpose(DB[h][:, (c % 4) * DEC:(c % 4 + 1) * DEC], XD[:, m], IDENT[0:DEC, 0:DEC])
                    last.then_inc(xt_full, 1)

            def x_spread(s):
                unit, b = UNITS[("rms", s // 3)], s % 3
                m = P if s < S8 else DEC
                bank_wait(unit, b)
                pe.wait_ge(diag_x, s + 1)
                pe.matmul(AB[unit.slot][b][:, 0:m], ONES[0:m, :], R[0:m, s * P:s * P + m], start=True, stop=True
                          ).then_inc(banks_full[unit.slot], 1)

            def x_next(transposes, spreads):
                for s in transposes:
                    x_transpose(s)
                for s in spreads:
                    x_spread(s)

            def parameters():
                pe.wait_ge(par_set, 3)
                pe.wait_ge(xt_free, 2 * (S8 + 1))
                pe.transpose(DB[0][:, 0:96], PAR[:, :], IDENT[0:96, 0:96]).then_inc(par_full, 1)
                pe.wait_ge(c_in, 64)
                for ri in range(2):
                    if ri == 1:
                        pe.wait_ge(par_free, 1)
                    for q in range(4):
                        last = pe.transpose(DB[1 - ri][:, q * P:(q + 1) * P], CL[:, ri, q, :], IDENT[:, :])
                    last.then_inc(par_full, 1)

            x_next((0, 1), (0,))
            x_next((2,), (1,))
            x_next((3,), (2,))
            x_next((4,), (3,))
            ffn("1", DOWN1, 0, {(0, DC - 1): lambda: x_next((5, 6), (4, 5)), (1, DC - 1): lambda: x_next((7, 8), (6, 7, 8))},
                parameters)

            after = last_down(DOWN1 + NF - 1, UNITS["norm2"], 1)
            for j in range(WC):
                project(UNITS[("u", j)], WEIGHTS[("u", j)], xn=1 if j == 0 else None, after=after if j == 0 else {})
            pe.wait_ge(disc_p, 4)
            for n in range(8):
                unit, b = UNITS[("tab", n // 3)], n % 3
                bank_wait(unit, b)
                for q in range(4):
                    i = 4 * n + q
                    last = pe.transpose(AB[unit.slot][b][:, q * P:(q + 1) * P], BS[:, i // 2, i % 2, :], IDENT[:, :])
                last.then_inc(banks_full[unit.slot], 1)
            for n in range(8, 12):
                unit, b = UNITS[("tab", n // 3)], n % 3
                bank_wait(unit, b)
                for q in range(4):
                    i = 4 * (n - 8) + q
                    for ri in range(2):
                        last = pe.matmul(AB[unit.slot][b][0:32, q * P:(q + 1) * P], BD[:, i, ri, :], CA[:, i, ri, 0:P],
                                         start=ri == 0, stop=ri == 1)
                last.then_inc(banks_full[unit.slot], 1)
            unit = UNITS["carried"]
            pe.wait_ge(carr_in, 48)
            bank_wait(unit, 2)
            for ri in range(2):
                last = pe.transpose(AB[unit.slot][0][:, ri * P:(ri + 1) * P], CARR[:, ri, :], IDENT[:, :])
            last.then_inc(banks_full[unit.slot], 3)
            unit = UNITS["buffer"]
            bank_wait(unit, 2)
            for j in range(WC):
                last = pe.transpose(AB[unit.slot][0][:, j * 16:(j + 1) * 16], CBUF[:, j * P:(j + 1) * P],
                                    IDENT[0:16, 0:16])
            last.then_inc(banks_full[unit.slot], 3)

            for c in range(WC):
                project(UNITS[("xc", c)], WEIGHTS[("xc", c)])
                project(UNITS[("gc", c)], WEIGHTS[("gc", c)], down=None if c == 0 else (DOWNC + c - 1, (c - 1) % 2))
                project(UNITS[("gb", c)], WEIGHTS[("gb", c)])
                if c == 0:
                    pe.wait_ge(u_in, 16 * 10)
                    for n, items in enumerate(V_BANKS):
                        unit, b = UNITS[("v", n // 3)], n % 3
                        bank_wait(unit, b)
                        for q, i in enumerate(items):
                            ri, g = divmod(i, GP)
                            for g2 in range(2):
                                half = slice(g2 * NS, (g2 + 1) * NS)
                                last = pe.matmul(AB[unit.slot][b][half, q * YC:(q + 1) * YC], WT[:, g, ri, half],
                                                 U[:, 2 * g + g2, DEC:UC], start=True, stop=True)
                        last.then_inc(banks_full[unit.slot], 2 if n == len(V_BANKS) - 1 else 1)

            pe.wait_ge(scanned, 1)
            for j in range(WC):
                unit = UNITS[("y", j)]
                pe.wait_ge(y_tab[j], 48)
                for b, items in enumerate(Y_BANKS):
                    bank_wait(unit, b)
                    for q, i in enumerate(items):
                        g = 8 * j + i
                        out = AB[unit.slot][b][:, q * YC:(q + 1) * YC]
                        pe.matmul(out, T0[:, g // 2, g % 2, :], U[:, g, 0:YC], start=True, stop=False)
                        pe.matmul(out, CB[:, g // 2, 0, g % 2, :], XS[:, g // 2, 0:YC], start=False, stop=False)
                        last = pe.matmul(out, CB[:, g // 2, 1, g % 2, :], XS[:, GP + g // 2, 0:YC], start=False, stop=True)
                    last.then_inc(banks_full[unit.slot], 1)
            unit = UNITS["states"]
            bank_wait(unit, 2)
            for ri in range(2):
                pe.transpose(AB[unit.slot][0][:, ri * P:(ri + 1) * P], DNEW[:, ri, :], IDENT[:, :])
                last = pe.transpose(AB[unit.slot][0][0:GP, (2 + ri) * P:(3 + ri) * P],
                                    XS[:, ri * GP:(ri + 1) * GP, DEC + NK], IDENT[:, :])
            last.then_inc(banks_full[unit.slot], 3)
            unit = UNITS["vout"]
            bank_wait(unit, 2)
            pe.wait_ge(conv_step, 10 * WC)
            for j in range(WC):
                last = pe.transpose(AB[unit.slot][0][0:16, j * P:(j + 1) * P], VOUT[:, j, :], IDENT[:, :])
            last.then_inc(banks_full[unit.slot], 3)
            d = DOWNC + 3
            down_start(d)
            for tb in range(TB):
                down_block(d, d % 2, tb)

            zw = [(z_ready, 4), (z_ready, 8), (z_ready, 12)]
            for j in range(WC):
                project(UNITS[("glu", j)], WEIGHTS[("glu", j)], ZH, ZL, WC, x_wait=zw if j == 0 else None)
                if j >= 1:
                    down_start(DOWNS + j - 1)
                    for tb in range(TB):
                        down_block(DOWNS + j - 1, (j - 1) % 2, tb)
            after = last_down(DOWNS + 3, UNITS["norm3"], 2)

            ffn("2", DOWN2, 2, after, None)
            d = DOWN2 + NF - 1
            down_start(d)
            for tb in range(TB):
                down_block(d, d % 2, tb)
            for s in range(S8 + 1):
                unit = UNITS[("out", s)]
                bank_wait(unit, 2)
                last_col = (s + 1) * NK if s < S8 else NT
                pe.wait_ge(down_free, TILES * d + DC * -(-last_col // TW))
                m = NK if s < S8 else DEC
                for c in range(DC):
                    last = pe.transpose(AB[unit.slot][c // 4][0:m, (c % 4) * P:(c % 4 + 1) * P],
                                        HT[:, c, s * NK:s * NK + m], IDENT[:, :])
                last.then_inc(banks_full[unit.slot], 3)

        @block.scalar
        def _(act):
            def split_hi(slot, n, k=DC, unit=None, down=None):
                act.wait_ge(raw_full[slot], (n + 1) * 16)
                if unit is not None:
                    act.wait_ge(banks_full[slot], unit.full(2))
                if down is not None:
                    act.wait_ge(down_full, last_tile(down))
                act.activation(WH[:, slot, 0:k * P], RAW[:, slot, 0:k * P], ACT.Copy).then_inc(w_hi[slot], 1)

            def h_hi(d, par, tb, wait):
                act.wait_ge(*wait)
                if not (isinstance(d, int) and d < 2):
                    act.wait_ge(down_full, TILES * (d - 1))
                act.activation(HH[:, par, cols(tb)], T[:, cols(tb)], ACT.Copy).then_inc(hi_done, 1)

            def upper(k, i):
                tb, c = divmod(i, DC)
                act.wait_ge(xn_tmp, XN * k + i + 1)
                act.activation(XH[:, c, cols(tb)], ring(i), ACT.Copy).then_inc(xn_hi, 1)

            def norm(unit, k, d, free_unit):
                def squares(tb, first, last):
                    for c in range(first, last):
                        i = DC * tb + c
                        act.wait_ge(down_free, TILES * d + DC * tb + c + 1)
                        if i >= 3:
                            block, q = divmod(i - 3, DC)
                            act.wait_ge(acc_done, (DC - 1) * (TB * (k - 1) + block) + max(q, 1))
                        act.activation(SQ[:, (i % 3) * TW:(i % 3 + 1) * TW], HT[:, c, cols(tb)], ACT.Square
                                       ).then_inc(sq_done, 1)

                def root(tb):
                    n = TB * (k - 1) + tb
                    act.wait_ge(sums_done, n + 1)
                    act.activation(RQ[:, n, :], AB[unit.slot][tb][0:QW, TW:TW + 4], ACT.Sqrt, bias=EPSC[0:QW, :],
                                   scale=1.0 / D).then_inc(rt_done, 1)

                def spread(tb):
                    act.wait_ge(banks_full[unit.slot], unit.full(tb))
                    take(act, unit, tb)
                    act.activation(R[:, cols(tb)], AB[unit.slot][tb][:, 0:TW], ACT.Copy).then_inc(banks_free[unit.slot], 1)

                def uppers(first, last):
                    for i in range(first, last):
                        upper(k, i)

                squares(0, 0, DC)
                squares(1, 0, 5)
                root(0)
                squares(1, 5, DC)
                squares(2, 0, 1)
                spread(0)
                squares(2, 1, 5)
                root(1)
                squares(2, 5, DC)
                spread(1)
                for u in free_unit:
                    act.wait_ge(banks_full[u.slot], u.full(2))
                uppers(0, 6)
                root(2)
                uppers(6, DC + 3)
                spread(2)
                uppers(DC + 3, XN)

            def ffn(which, down, last_next):
                ug, uu = UNITS["gate" + which], UNITS["up" + which]
                wg, wu = WEIGHTS["gate" + which], WEIGHTS["up" + which]

                def silu(f, d):
                    if isinstance(f, int) and f == 0:
                        take(act, ug)
                    for tb in range(TB):
                        act.wait_ge(banks_full[0], ug.at(f).full(tb))
                        if not (isinstance(f, int) and f == 0):
                            act.wait_ge(banks_free[1], uu.at(f - 1).full(tb))
                        else:
                            act.wait_ge(xn_ready, XN if down == 0 else 3 * XN)
                        act.activation(S[:, cols(tb)], AB[0][tb][:, 0:TW], ACT.Silu).then_inc(banks_free[0], 1)

                def uppers(f, par):
                    for tb in range(TB):
                        h_hi(f + down, par, tb, (banks_free[1], uu.at(f).full(tb)))

                def step(f, par):
                    split_hi(1, f + wu, unit=uu.at(f - 1))
                    if isinstance(f, int) and f == 1:
                        split_hi(2, down) if down == 0 else split_hi(2, down, down=down - 1)
                    else:
                        split_hi(2, f + (down - 1), down=f + (down - 2))
                    silu(f, f + down)
                    split_hi(0, f + (wg + 1), unit=ug.at(f))
                    uppers(f, par)

                silu(0, down)
                split_hi(0, wg + 1, unit=ug)
                uppers(0, 0)
                if down == 0:
                    act.wait_ge(lri_done, 3)
                    act.activation(TMP[:, 0, :], LRI[:, 2, :], ACT.Exp).then_inc(disc_a, 1)
                step(1, 1)
                if down == 0:
                    act.wait_ge(disc_p, 1)
                    act.activation(TMP[:, 3, :], TMP[:, 1, :], ACT.Exp).then_inc(disc_a, 1)
                    act.activation(TMP[:, 4, :], TMP[:, 2, :], ACT.Sin).then_inc(disc_a, 1)
                    act.activation(TMP[:, 5, :], TMP[:, 6, :], ACT.Sin).then_inc(disc_a, 1)
                step(2, 0)
                with act.Fori(1, (NF - 2) // 2) as i:
                    step(i * 2 + 1, 1)
                    step(i * 2 + 2, 0)
                f = NF - 1
                split_hi(1, f + wu, unit=uu.at(f - 1))
                split_hi(2, f + (down - 1), down=f + (down - 2))
                silu(f, f + down)
                if last_next is not None:
                    split_hi(0, last_next, unit=ug.at(f))
                uppers(f, 1)
                split_hi(2, f + down, down=f + down - 1)

            act.wait_ge(const_done, 3)

            def x_rms(s):
                src, m = (X[:, s, :], P) if s < S8 else (XD[:, :], DEC)
                act.wait_ge(x_in[s], 16)
                if s > 0:
                    act.wait_ge(sq_x, s)
                act.activation(JUNK[0:m, :], src, ACT.Square, accum_out=SS[0:m, s, 0:1]).then_inc(sq_x, 1)
                act.wait_ge(sq_x, s + 1)
                act.activation(RS[0:m, s:s + 1], SS[0:m, s, 0:1], ACT.Sqrt, bias=EPSC[0:m, :], scale=1.0 / D
                               ).then_inc(sqrt_x, 1)

            def x_spread(s):
                unit, b = UNITS[("rms", s // 3)], s % 3
                m = P if s < S8 else DEC
                act.wait_ge(banks_full[unit.slot], unit.full(b))
                act.activation(R[:, s * P:s * P + m], AB[unit.slot][b][:, 0:m], ACT.Copy).then_inc(banks_free[unit.slot], 1)

            x_rms(0)
            x_rms(1)
            x_spread(0)
            split_hi(0, 0)
            for s in range(2, 5):
                x_rms(s)
                x_spread(s - 1)
            for i in range(DC):
                upper(0, i)
            x_rms(5)
            x_rms(6)
            x_spread(4)
            x_spread(5)
            for i in range(DC, 2 * DC):
                upper(0, i)
            x_rms(7)
            x_rms(8)
            for s in range(6, S8 + 1):
                x_spread(s)
            for i in range(2 * DC, XN):
                upper(0, i)
            split_hi(1, 0)
            ffn("1", DOWN1, WEIGHTS[("u", 0)])
            split_hi(1, WEIGHTS[("u", 1)], unit=UNITS["up1"].at(NF - 1))

            act.wait_ge(disc_p, 4)
            norm(UNITS["norm2"], 1, NF - 1, [UNITS["gate1"].at(NF - 1), UNITS["up1"].at(NF - 1)])

            def evict(unit, tb, dst):
                act.wait_ge(banks_full[unit.slot], unit.full(tb))
                take(act, unit, tb)
                act.activation(dst[:, cols(tb)], AB[unit.slot][tb][:, 0:TW], ACT.Copy).then_inc(banks_free[unit.slot], 1)

            def next_split(name):
                i = WEIGHTED.index(name)
                slot = UNITS[name].slot
                before = [w for w in WEIGHTED[:i] if UNITS[w].slot == slot]
                k = WC if name[0] == "glu" else DC
                split_hi(slot, WEIGHTS[name], k, unit=UNITS[before[-1]])

            for j in range(WC):
                unit = UNITS[("u", j)]
                dst = (S, T)[j % 2]
                if j >= 2:
                    act.wait_ge(u_out[j - 2], 16)
                if j == 0:
                    act.wait_ge(xn_ready, 2 * XN)
                for tb in range(TB):
                    evict(unit, tb, dst)
                next_split(WEIGHTED[j + 2])
                if j == 0:
                    split_hi(2, DOWNC, down=DOWNC - 1)
            act.wait_ge(down_full, last_tile(DOWN1 + NF - 1))
            for n in range(12):
                unit, b = UNITS[("tab", n // 3)], n % 3
                act.wait_ge(banks_full[unit.slot], unit.full(b))
                take(act, unit, b)
                if n < 8:
                    act.activation(WT[:, 2 * n:2 * n + 2, :, :].rearrange("p g r n -> p (g r n)"), AB[unit.slot][b][:, :],
                                   ACT.Copy).then_inc(banks_free[unit.slot], 1)
                else:
                    if n == 8:
                        act.wait_ge(disc_p, 5)
                    src = AB[unit.slot][b][0:32, :].rearrange("p (g n) -> p g n", n=P)
                    act.activation(KT[:, 4 * (n - 8):4 * (n - 7), 7 * C16:], src, ACT.Copy
                                   ).then_inc(banks_free[unit.slot], 1)
            unit = UNITS["carried"]
            act.wait_ge(banks_full[unit.slot], unit.full(2))
            take(act, unit)
            act.wait_ge(xs_zero, 1)
            for ri in range(2):
                last = act.activation(XS[:, ri * GP:(ri + 1) * GP, 0:DEC].rearrange("p g t -> p t g"),
                                      AB[unit.slot][0][:, ri * P:(ri + 1) * P].rearrange("p (t g) -> p t g", g=GP), ACT.Copy)
            last.then_inc(banks_free[unit.slot], 3)
            unit = UNITS["buffer"]
            act.wait_ge(banks_full[unit.slot], unit.full(2))
            take(act, unit)
            act.activation(CBT[:, :, :].rearrange("p j n -> p (j n)"), AB[unit.slot][0][:, 0:64], ACT.Copy
                           ).then_inc(banks_free[unit.slot], 3)

            for c in range(WC):
                names = [("xc", c), ("gc", c), ("gb", c)]
                i = WEIGHTED.index(names[0])
                unit = UNITS[names[0]]
                if c == 0:
                    act.wait_ge(u_out[2], 16)
                    act.wait_ge(u_out[3], 16)
                else:
                    act.wait_ge(banks_free[UNITS[("gc", c - 1)].slot], UNITS[("gc", c - 1)].full(2))
                for tb in range(TB):
                    evict(unit, tb, S)
                next_split(WEIGHTED[i + 2])
                next_split(WEIGHTED[i + 3])
                unit = UNITS[("gb", c)]
                if c == 0:
                    for n, items in enumerate(V_BANKS):
                        vu, b = UNITS[("v", n // 3)], n % 3
                        act.wait_ge(banks_full[vu.slot], vu.full(b))
                        take(act, vu, b)
                        src = AB[vu.slot][b][:, 0:len(items) * YC].rearrange("p (q n) -> p q n", n=YC)
                        act.activation(XS[:, items[0]:items[-1] + 1, DEC + 1:XC], src, ACT.Copy
                                       ).then_inc(banks_free[vu.slot], 2 if n == len(V_BANKS) - 1 else 1)
                for tb in range(TB):
                    h_hi(DOWNC + c, c % 2, tb, (banks_free[unit.slot], unit.full(tb)))
                next_split(WEIGHTED[i + 4])
                if c >= 1:
                    split_hi(2, DOWNC + c, down=DOWNC + c - 1)
            for j in range(WC):
                unit = UNITS[("y", j)]
                if j >= 2:
                    act.wait_ge(z_out[j - 2], 16 * 9)
                for b, items in enumerate(Y_BANKS):
                    act.wait_ge(banks_full[unit.slot], unit.full(b))
                    take(act, unit, b)
                    act.activation(Z[:, j % 2, items[0]:items[-1] + 1, :].rearrange("p g n -> p (g n)"),
                                   AB[unit.slot][b][:, 0:len(items) * YC], ACT.Gelu_apprx_tanh
                                   ).then_inc(banks_free[unit.slot], 1)
            unit = UNITS["states"]
            act.wait_ge(banks_full[unit.slot], unit.full(2))
            take(act, unit)
            act.activation(STO[:, 0:2, :].rearrange("p r n -> p (r n)"), AB[unit.slot][0][:, 0:2 * P], ACT.Copy)
            act.activation(STO[0:GP, 2:4, :].rearrange("p r n -> p (r n)"), AB[unit.slot][0][0:GP, 2 * P:4 * P], ACT.Copy
                           ).then_inc(banks_free[unit.slot], 3)
            act.wait_ge(banks_free[unit.slot], unit.full(2))
            act.nop().then_inc(st_out, 1)
            unit = UNITS["vout"]
            act.wait_ge(banks_full[unit.slot], unit.full(2))
            take(act, unit)
            act.activation(VO[:, :], AB[unit.slot][0][0:16, :], ACT.Copy).then_inc(banks_free[unit.slot], 3)
            act.wait_ge(banks_free[unit.slot], unit.full(2))
            act.nop().then_inc(st_out, 1)
            y3 = UNITS[("y", 3)]
            for tb in range(TB):
                for j in range(WC):
                    if tb == 0:
                        act.wait_ge(zt_in[j], 16)
                        act.wait_ge(z_out[j], 16 * 9)
                    act.activation(ZH[:, j, cols(tb)], ZT[:, j, cols(tb)], ACT.Copy).then_inc(z_hi, 1)
            split_hi(2, DOWNS, down=DOWNS - 1)
            for j in range(WC):
                unit = UNITS[("glu", j)]
                for tb in range(TB):
                    act.wait_ge(banks_full[unit.slot], unit.full(tb))
                    if j > 0:
                        act.wait_ge(gate_done, 3 * (j - 1) + tb + 1)
                    take(act, unit, tb)
                    act.activation(S[:, cols(tb)], AB[unit.slot][tb][:, 0:TW], ACT.Sigmoid, bias=BG[:, j:j + 1]
                                   ).then_inc(banks_free[unit.slot], 1)
                for tb in range(TB):
                    h_hi(DOWNS + j, j % 2, tb, (gate_done, 3 * j + tb + 1))
                if j < 2:
                    next_split(("glu", j + 2))
                if j >= 1:
                    split_hi(2, DOWNS + j, down=DOWNS + j - 1)
                if j == 2:
                    split_hi(0, WEIGHTS["gate2"], unit=UNITS[("glu", 2)])
                if j == 3:
                    split_hi(1, WEIGHTS["up2"], unit=UNITS[("glu", 3)])
            norm(UNITS["norm3"], 2, DOWNS + 3, [UNITS[("glu", 3)]])
            ffn("2", DOWN2, None)

            act.wait_ge(h_ready, 3 * ND)
            for s in range(S8 + 1):
                unit = UNITS[("out", s)]
                m = NK if s < S8 else DEC
                act.wait_ge(banks_full[unit.slot], unit.full(2))
                for h in range(2):
                    if s > 0 or h > 0:
                        act.wait_ge(sq_x, 9 + 2 * s + h)
                    act.activation(S[0:m, 0:512], AB[unit.slot][h][0:m, :], ACT.Square, accum_out=SS[0:m, s, h:h + 1]
                                   ).then_inc(sq_x, 1)
                act.wait_ge(ss_sum, s + 1)
                act.activation(RS[0:m, s:s + 1], SS[0:m, s, 0:1], ACT.Sqrt, bias=EPSC[0:m, :], scale=1.0 / D
                               ).then_inc(sqrt_x, 1)

        @block.vector
        def _(dve):
            def f(t):
                return t.bitcast(F32)

            def split_lo(slot, n, k=DC):
                dve.wait_ge(w_hi[slot], n + 1)
                dve.tensor_tensor(WL[:, slot, 0:k * P], RAW[:, slot, 0:k * P], f(WH[:, slot, 0:k * P]), ALU.subtract
                                  ).then_inc(w_split[slot], 1)

            def h_lo(d, par, tb):
                dve.wait_ge(hi_done, 3 * d + tb + 1)
                dve.tensor_tensor(HL[:, par, cols(tb)], T[:, cols(tb)], f(HH[:, par, cols(tb)]), ALU.subtract
                                  ).then_inc(h_ready, 1)

            def add_tile(d, tb, j, scale):
                dve.wait_ge(down_full, TILES * d + DC * tb + j + 1)
                ht = HT[:, j, cols(tb)]
                if scale == 1.0:
                    ins = dve.tensor_tensor(ht, DB[(DC * tb + j) % 2][:, 0:TW], ht, ALU.add)
                else:
                    ins = dve.scalar_tensor_tensor(ht, DB[(DC * tb + j) % 2][:, 0:TW], scale, ht, ALU.mult, ALU.add)
                ins.then_inc(down_free, 1)

            def add_block(d, tb, scale=0.5):
                for j in range(DC):
                    add_tile(d, tb, j, scale)

            def scaled(k, i):
                tb, c = divmod(i, DC)
                if i >= 6:
                    dve.wait_ge(xn_ready, XN * k + i - 5)
                dve.scalar_tensor_tensor(ring(i), HT[:, c, cols(tb)], GAIN[:, k, c:c + 1], R[:, cols(tb)], ALU.mult,
                                         ALU.mult).then_inc(xn_tmp, 1)

            def norm(unit, k, d, scale):
                def diagonals(tb):
                    n = TB * (k - 1) + tb
                    dve.wait_ge(rt_done, n + 1)
                    dve.reciprocal(RQ[:, n, :], RQ[:, n, :]).then_inc(rcp_done, 1)
                    dve.wait_ge(rcp_done, n + 1)
                    for q in range(4):
                        at = tb * TW + q * QW
                        dve.tensor_scalar(R[0:QW, at:at + QW], IDENT[0:QW, 0:QW], RQ[:, n, q:q + 1], None, ALU.mult
                                          ).then_inc(diag_done, 1)

                for tb in range(TB):
                    for j in range(DC):
                        add_tile(d, tb, j, scale)
                        if tb > 0 and j == 5:
                            diagonals(tb - 1)
                dve.wait_ge(h_ready, 3 * d + 3)
                for tb in range(TB):
                    dve.wait_ge(banks_free[unit.slot], unit.full(tb))
                    for c in range(DC):
                        scaled(k, DC * tb + c)
                    if tb == 0:
                        diagonals(2)

            def ffn(which, down, last_next):
                ug, uu = UNITS["gate" + which], UNITS["up" + which]
                wg, wu = WEIGHTS["gate" + which], WEIGHTS["up" + which]

                def mul(n, tb):
                    if isinstance(n, int) and n == 0:
                        take(dve, uu, tb)
                    dve.wait_ge(banks_full[1], uu.at(n).full(tb))
                    dve.wait_ge(banks_free[0], ug.at(n).full(tb))
                    if not (isinstance(n, int) and n == 0):
                        dve.wait_ge(h_ready, 3 * (n + (down - 1)) + tb + 1)
                    else:
                        dve.wait_ge(xn_ready, XN if down == 0 else 3 * XN)
                    dve.tensor_tensor(T[:, cols(tb)], AB[1][tb][:, 0:TW], S[:, cols(tb)], ALU.mult
                                      ).then_inc(banks_free[1], 1)

                def step(n, par):
                    split_lo(1, n + wu)
                    split_lo(2, n + (down - 1))
                    for tb in range(TB):
                        add_block(n + (down - 1), tb)
                        mul(n, tb)
                        if tb == 0:
                            split_lo(0, n + (wg + 1))
                    for tb in range(TB):
                        h_lo(n + down, par, tb)

                split_lo(0, wg + 1)
                for tb in range(TB):
                    mul(0, tb)
                for tb in range(TB):
                    h_lo(down, 0, tb)
                if down == 0:
                    parameters()
                step(1, 1)
                if down == 0:
                    dve.wait_ge(disc_p, 2)
                    dve.reciprocal(TMP[:, 12, :], TMP[:, 7, :]).then_inc(den_inv, 1)
                step(2, 0)
                with dve.Fori(1, (NF - 2) // 2) as i:
                    step(i * 2 + 1, 1)
                    step(i * 2 + 2, 0)
                n = NF - 1
                split_lo(1, n + wu)
                split_lo(2, n + down - 1)
                for tb in range(TB):
                    add_block(n + down - 1, tb)
                    mul(n, tb)
                    if tb == 0 and last_next is not None:
                        split_lo(0, last_next)
                for tb in range(TB):
                    h_lo(n + down, 1, tb)
                split_lo(2, n + down)

            def parameters():
                dve.wait_ge(par_full, 1)
                for n in range(3):
                    last = dve.tensor_copy(LRI[:, n, :], DB[0][:, 32 * n:32 * n + GP])
                    last.then_inc(lri_done, 1)
                dve.wait_ge(lri_done, 3)
                dve.nop().then_inc(par_free, 1)
                for ri in range(2):
                    dve.wait_ge(par_full, 2 + ri)
                    for g2 in range(2):
                        half = slice(g2 * NS, (g2 + 1) * NS)
                        src = DB[1 - ri][half, :].rearrange("p (g e c) -> p g e c", e=2, c=C16)[:, :, g2, :]
                        dve.tensor_scalar(CA[half, :, ri, 0:C16], src, (1.0, -1.0)[ri], None, ALU.mult).then_inc(c_done, 1)
                    dve.wait_ge(c_done, 2 * ri + 2)
                    dve.nop().then_inc(par_free, 1)

            dve.wait_ge(const_done, 3)

            def x_tile(s):
                for h in range(2):
                    dve.wait_ge(xt_full, 2 * s + h + 1)
                    m = P if s < S8 else DEC
                    dve.tensor_copy(HT[:, 4 * h:4 * h + 4, s * P:s * P + m],
                                    DB[h][:, 0:4 * m].rearrange("p (c n) -> p c n", n=m)).then_inc(xt_free, 1)
                dve.wait_ge(sqrt_x, s + 1)
                dve.reciprocal(RS[0:m, s:s + 1], RS[0:m, s:s + 1]).then_inc(rcp_x, 1)
                dve.wait_ge(rcp_x, s + 1)
                dve.tensor_scalar(R[0:m, s * P:s * P + m], IDENT[0:m, 0:m], RS[0:m, s:s + 1], None, ALU.mult
                                  ).then_inc(diag_x, 1)

            def x_scaled(tb, last_tile):
                if tb == 0:
                    dve.wait_ge(gain_in, 48)
                unit = UNITS[("rms", last_tile // 3)]
                dve.wait_ge(banks_free[unit.slot], unit.full(last_tile % 3))
                dve.wait_ge(xt_free, 2 * last_tile + 2)
                for c in range(DC):
                    scaled(0, DC * tb + c)

            x_tile(0)
            x_tile(1)
            split_lo(0, 0)
            for s in range(2, 5):
                x_tile(s)
            x_scaled(0, 2)
            x_tile(5)
            x_tile(6)
            x_scaled(1, 5)
            x_tile(7)
            x_tile(8)
            x_scaled(2, 8)
            split_lo(1, 0)

            ffn("1", DOWN1, WEIGHTS[("u", 0)])
            split_lo(1, WEIGHTS[("u", 1)])
            norm(UNITS["norm2"], 1, DOWN1 + NF - 1, 0.5)

            def next_lo(name):
                split_lo(UNITS[name].slot, WEIGHTS[name], WC if name[0] == "glu" else DC)

            for j in range(WC):
                next_lo(WEIGHTED[j + 2])
                if j == 0:
                    split_lo(2, DOWNC)

            unit = UNITS[("tab", 3)]
            dve.wait_ge(banks_free[unit.slot], unit.full(2))
            for g in range(GP):
                dve.tensor_scalar(DTM[:, :], DM[:, :], DT[:, g:g + 1], None, ALU.mult).then_inc(kt_done, 1)
                dve.wait_ge(kt_done, 2 * g + 1)
                dve.tensor_tensor(KT[:, g, 7 * C16:8 * C16], KT[:, g, 7 * C16:8 * C16], DTM[:, :], ALU.add
                                  ).then_inc(kt_done, 1)
                dve.wait_ge(kt_done, 2 * g + 2)
            dve.nop().then_inc(dt_k, 2)

            vb = UNITS["buffer"]
            steps = [0]

            def step_done(ins):
                steps[0] += 1
                ins.then_inc(conv_step, 1)
                dve.wait_ge(conv_step, steps[0])

            def taps(k):
                return CW[:, k, c:c + 1]

            for c in range(WC):
                i = WEIGHTED.index(("xc", c))
                xu, gu, bu = UNITS[("xc", c)], UNITS[("gc", c)], UNITS[("gb", c)]
                if c == 0:
                    dve.wait_ge(banks_full[vb.slot], vb.full(2))
                for tb in range(TB):
                    if c > 0:
                        add_block(DOWNC + c - 1, tb, 1.0)
                    dve.wait_ge(banks_full[gu.slot], gu.full(tb))
                    dve.wait_ge(banks_free[xu.slot], xu.full(tb))
                    if c > 0:
                        dve.wait_ge(h_ready, 3 * (DOWNC + c - 1) + 3)
                    take(dve, gu, tb)
                    dve.tensor_tensor(V[:, cols(tb)], AB[gu.slot][tb][:, 0:TW], S[:, cols(tb)], ALU.mult
                                      ).then_inc(banks_free[gu.slot], 1)
                    if tb == 0:
                        next_lo(WEIGHTED[i + 2])
                next_lo(WEIGHTED[i + 3])
                dve.wait_ge(banks_free[gu.slot], gu.full(2))
                if c == 0:
                    dve.wait_ge(u_out[3], 16)
                    dve.wait_ge(banks_free[vb.slot], vb.full(2))
                    dve.wait_ge(xs_zero, 1)
                step_done(dve.tensor_copy(VPRE[:, :, 1:NK],
                                          V[:, 6 * NK:SEQ].rearrange("p (s k) -> p s k", k=NK)[:, :, 0:NK - 1]))
                step_done(dve.tensor_copy(VOUT[:, c, 0:DEC], V[:, SEQ:NT]))
                step_done(dve.tensor_copy(VOUT[:, c, DEC:DEC + 2],
                                          V[:, 6 * NK:SEQ].rearrange("p (s k) -> p s k", k=NK)[:, :, NK - 1]))
                step_done(dve.tensor_scalar(T[:, :], V[:, :], taps(2), None, ALU.mult))

                def tap(dst, src, k):
                    step_done(dve.scalar_tensor_tensor(dst, src, taps(k), dst, ALU.mult, ALU.add))
                tap(T[:, NK:SEQ], V[:, 0:SEQ - NK], 1)
                tap(T[:, 0:NK], VPRE[:, 1, :], 1)
                tap(T[:, 2 * NK:SEQ], V[:, 0:SEQ - 2 * NK], 0)
                tap(T[:, 0:2 * NK], VPRE[:, :, :].rearrange("p s k -> p (s k)"), 0)
                buf = CBT[:, c, :].rearrange("p (b r) -> p b r", r=2)
                tap(T[:, SEQ:NT], buf[:, :, 1], 1)
                tap(T[:, SEQ:NT], buf[:, :, 0], 0)
                for tb in range(TB):
                    dve.wait_ge(banks_full[bu.slot], bu.full(tb))
                    take(dve, bu, tb)
                    dve.tensor_tensor(T[:, cols(tb)], AB[bu.slot][tb][:, 0:TW], T[:, cols(tb)], ALU.mult
                                      ).then_inc(banks_free[bu.slot], 1)
                for tb in range(TB):
                    h_lo(DOWNC + c, c % 2, tb)
                next_lo(WEIGHTED[i + 4])
                if c >= 1:
                    split_lo(2, DOWNC + c)
            for tb in range(TB):
                add_block(DOWNC + 3, tb, 1.0)
            for tb in range(TB):
                for j in range(WC):
                    dve.wait_ge(z_hi, WC * tb + j + 1)
                    dve.tensor_tensor(ZL[:, j, cols(tb)], ZT[:, j, cols(tb)], f(ZH[:, j, cols(tb)]), ALU.subtract
                                      ).then_inc(z_ready, 1)
            split_lo(2, DOWNS)
            for j in range(WC):
                unit = UNITS[("glu", j)]
                for tb in range(TB):
                    dve.wait_ge(banks_free[unit.slot], unit.full(tb))
                    dve.wait_ge(h_ready, 3 * (DOWNS + j - 1) + tb + 1)
                    dve.tensor_tensor(T[:, cols(tb)], S[:, cols(tb)], ZT[:, j, cols(tb)], ALU.mult
                                      ).then_inc(gate_done, 1)
                for tb in range(TB):
                    h_lo(DOWNS + j, j % 2, tb)
                if j < 2:
                    next_lo(("glu", j + 2))
                if j >= 1:
                    for tb in range(TB):
                        add_block(DOWNS + j - 1, tb, 1.0)
                    split_lo(2, DOWNS + j)
                if j == 2:
                    split_lo(0, WEIGHTS["gate2"])
                if j == 3:
                    split_lo(1, WEIGHTS["up2"])
            norm(UNITS["norm3"], 2, DOWNS + 3, 1.0)
            ffn("2", DOWN2, None)
            for tb in range(TB):
                add_block(DOWN2 + NF - 1, tb)
            dve.wait_ge(gf_in, 16)
            for s in range(S8 + 1):
                unit = UNITS[("out", s)]
                m = NK if s < S8 else DEC
                dve.wait_ge(sq_x, 9 + 2 * s + 2)
                take(dve, unit)
                dve.tensor_tensor(SS[0:m, s, 0:1], SS[0:m, s, 0:1], SS[0:m, s, 1:2], ALU.add).then_inc(ss_sum, 1)
                dve.wait_ge(sqrt_x, 9 + s + 1)
                dve.reciprocal(RS[0:m, s:s + 1], RS[0:m, s:s + 1]).then_inc(rcp_x, 1)
                dve.wait_ge(rcp_x, 9 + s + 1)
                if s >= 2:
                    dve.wait_ge(y_out[s % 2], 16 * (s // 2))
                for h in range(2):
                    span = slice(512 * h, 512 * (h + 1))
                    dve.scalar_tensor_tensor(OUT[0:m, s % 2, span], AB[unit.slot][h][0:m, :], RS[0:m, s:s + 1],
                                             GF[0:m, span], ALU.mult, ALU.mult).then_inc(out_done, 1)
                dve.wait_ge(out_done, 2 * s + 2)
                dve.nop().then_inc(banks_free[unit.slot], 3)

        @block.gpsimd
        def _(pool):
            count = [0]

            def chain(ins):
                count[0] += 1
                ins.then_inc(pool_step, 1)
                pool.wait_ge(pool_step, count[0])

            chain(pool.memset(IDENT[:, :], 0.0))
            pool.affine_select(out=IDENT[:, :], in_=IDENT[:, :], compare_op=ALU.not_equal, fill=1.0, base=0,
                               pattern=[[-1, P]], channel_multiplier=1).then_inc(const_done, 1)
            pool.memset(ONES[:, :], 1.0).then_inc(const_done, 1)
            pool.memset(EPSC[:, :], EPS).then_inc(const_done, 1)
            pool.memset(VOUT[:, :, :], 0.0)
            with nc.allow_non_contiguous_dma(reason="small parameters, channels to partitions"):
                for n, name in enumerate(("ffn1_norm", "mix_norm", "ffn2_norm")):
                    pool.dma_start(GAIN[:, n, :], a[name][0].rearrange("(c p) -> p c", p=P)).then_inc(gain_in, 16)
            chain(pool.memset(PAR[:, :], 0.0))
            pool.dma_start(PAR[0:GP, :], a["ssm_lambda_re"][0].rearrange("(g e) p -> g (e p)", e=2)).then_inc(par_in, 16)
            pool.dma_start(PAR[32:32 + GP, :], a["ssm_lambda_im"][0].rearrange("(g e) p -> g (e p)", e=2)
                           ).then_inc(par_in, 16)
            pool.dma_start(TMP[64:64 + GP, 0, 0:2], a["ssm_log_dt"][0].rearrange("(g e) -> g e", e=2)).then_inc(dt_in, 16)

            def lower(k, first, last):
                for i in range(first, last):
                    tb, c = divmod(i, DC)
                    pool.wait_ge(xn_hi, XN * k + i + 1)
                    pool.tensor_tensor(XL[:, c, cols(tb)], ring(i), XH[:, c, cols(tb)].bitcast(F32), ALU.subtract
                                       ).then_inc(xn_ready, 1)
                pool.wait_ge(xn_ready, XN * k + last)

            def norm(k):
                for tb in range(TB):
                    for c in range(1, DC):
                        i, n = DC * tb + c, TB * (k - 1) + tb
                        pool.wait_ge(sq_done, XN * (k - 1) + i + 1)
                        square = lambda j: SQ[:, (j % 3) * TW:(j % 3 + 1) * TW]
                        if c == 1:
                            ins = pool.tensor_tensor(R[:, cols(tb)], square(i - 1), square(i), ALU.add)
                        else:
                            pool.wait_ge(acc_done, (DC - 1) * n + c - 1)
                            ins = pool.tensor_tensor(R[:, cols(tb)], R[:, cols(tb)], square(i), ALU.add)
                        ins.then_inc(acc_done, 1)
                lower(k, 0, XN)

            lower(0, 0, DC)
            lower(0, DC, 2 * DC)
            pool.wait_ge(xt_full, 2 * (S8 + 1))
            pool.wait_ge(sq_x, S8 + 1)
            for ri, name in enumerate(("ssm_c_re", "ssm_c_im")):
                src = a[name][0].rearrange("(q g) c p -> (g c) q p", q=4)
                for twice in range(2):
                    pool.dma_start(CL[:, ri, :, twice * NS:(twice + 1) * NS], src).then_inc(c_in, 16)
            lower(0, 2 * DC, XN)
            with nc.allow_non_contiguous_dma(reason="small parameters, channels to partitions"):
                pool.dma_start(CW[:, :, :], a["conv_w"][0].rearrange("k (c p) -> p k c", p=P)).then_inc(consts_in, 16)
                pool.dma_start(BG[:, :], a["ssm_b_glu"][0].rearrange("(c p) -> p c", p=P)).then_inc(consts_in, 16)
                pool.dma_start(DT[:, :], a["ssm_d"][0].rearrange("(g n) -> n g", n=32)).then_inc(consts_in, 16)
            for ri, name in enumerate(("ssm_b_re", "ssm_b_im")):
                pool.dma_start(BRAW[:, ri, :, :], a[name][0].rearrange("(g e) p c -> (e p) g c", e=2)).then_inc(b_in, 16)
            pool.wait_ge(par_in, 32)
            pool.nop().then_inc(par_set, 1)
            pool.wait_ge(dt_in, 16)
            for e in range(2):
                pool.tensor_copy(PAR[64:64 + GP, e * NS:(e + 1) * NS],
                                 TMP[64:64 + GP, 0, e:e + 1].broadcast_to([GP, NS])).then_inc(par_set, 1)

            t = lambda n: TMP[:, n, :]

            def tt(out, x, y, op):
                chain(pool.tensor_tensor(out, x, y, op))

            def ts(out, x, s1, op1, s2=None, op2=None):
                if op2 is None:
                    chain(pool.tensor_scalar(out, x, s1, None, op1))
                else:
                    chain(pool.tensor_scalar(out, x, s1, s2, op1, op2))

            lr, li = LRI[:, 0, :], LRI[:, 1, :]
            pool.wait_ge(disc_a, 1)
            tt(t(1), lr, t(0), ALU.mult)
            tt(t(2), li, t(0), ALU.mult)
            ts(t(7), t(2), 1.0 / TWO_PI, ALU.mult)
            ts(t(7), t(7), MAGIC, ALU.add)
            ts(t(7), t(7), MAGIC, ALU.subtract)
            for part in (PI_A, PI_B, PI_C):
                ts(t(8), t(7), part, ALU.mult)
                tt(t(2), t(2), t(8), ALU.subtract)
            ts(t(2), t(2), 3.1415925, ALU.min, -3.1415925, ALU.max)
            ts(t(8), t(2), -1.0, ALU.mult)
            chain(pool.tensor_scalar(t(9), t(2), 0.0, None, ALU.max))
            chain(pool.tensor_scalar(t(8), t(8), 0.0, None, ALU.max))
            tt(t(6), t(9), t(8), ALU.add)
            ts(t(6), t(6), -1.0, ALU.mult, float(np.pi / 2), ALU.add)
            pool.nop().then_inc(disc_p, 1)
            pool.wait_ge(disc_a, 4)
            ar, ai, nai = AP8[:, 7, 0, :], AP8[:, 7, 1, :], AP8[:, 7, 2, :]
            tt(ar, t(3), t(5), ALU.mult)
            tt(ai, t(3), t(4), ALU.mult)
            tt(t(7), lr, lr, ALU.mult)
            tt(t(8), li, li, ALU.mult)
            tt(t(7), t(7), t(8), ALU.add)
            pool.nop().then_inc(disc_p, 1)
            ts(t(8), ar, -1.0, ALU.add)
            tt(t(9), t(8), lr, ALU.mult)
            tt(t(10), ai, li, ALU.mult)
            tt(t(9), t(9), t(10), ALU.add)
            tt(t(10), ai, lr, ALU.mult)
            tt(t(11), t(8), li, ALU.mult)
            tt(t(10), t(10), t(11), ALU.subtract)
            pool.wait_ge(den_inv, 1)
            tt(t(9), t(9), t(12), ALU.mult)
            tt(t(10), t(10), t(12), ALU.mult)
            pool.wait_ge(b_in, 32)
            pool.wait_ge(c_done, 4)

            def over(x, n=C16):
                return x.rearrange("p (g o) -> p g o", o=1).broadcast_to([P, GP, n])

            D1 = PROD[:, 0]
            D2 = PROD[:, 1]
            br, bi = BRAW[:, 0], BRAW[:, 1]

            def bs(ri, s):
                return BS[:, :, ri, s * C16:(s + 1) * C16]

            def ca(ri, j):
                return CA[:, :, ri, j * C16:(j + 1) * C16]

            def rotate(out_r, out_i, in_r, in_i, cr, ci, sign):
                tt(D1, in_r, over(cr), ALU.mult)
                tt(D2, in_i, over(ci), ALU.mult)
                tt(out_r, D1, D2, ALU.subtract if sign == 1 else ALU.add)
                tt(D1, in_i, over(cr), ALU.mult)
                tt(D2, in_r, over(ci), ALU.mult)
                tt(out_i, D1, D2, ALU.add if sign == 1 else ALU.subtract)

            rotate(bs(0, 7), bs(1, 7), br, bi, t(9), t(10), 1)
            for s in range(6, -1, -1):
                rotate(bs(0, s), bs(1, s), bs(0, s + 1), bs(1, s + 1), ar, ai, 1)
            for j in range(1, 9):
                rotate(ca(0, j), ca(1, j), ca(0, j - 1), ca(1, j - 1), ar, ai, -1)
            chain(pool.memset(BD[:, :, :, :], 0.0))
            for ri in range(2):
                chain(pool.tensor_copy(BD[0:NS, :, ri, 0:C16], BS[0:NS, :, ri, 7 * C16:]))
                chain(pool.tensor_copy(BD[NS:P, :, ri, C16:], BS[NS:P, :, ri, 7 * C16:]))
            pool.dma_start(CAD, CA[:, :, :, :].rearrange("p g r n -> p (g r) n")).then_inc(ca_out, 16)

            def square_of(x, out_r, out_i):
                tt(t(0), x[0], x[0], ALU.mult)
                tt(t(1), x[1], x[1], ALU.mult)
                tt(t(2), x[0], x[1], ALU.mult)
                tt(out_r, t(0), t(1), ALU.subtract)
                tt(out_i, t(2), t(2), ALU.add)
            chain(pool.tensor_copy(t(12), ar))
            chain(pool.tensor_copy(t(13), ai))
            square_of((ar, ai), t(3), t(4))
            square_of((t(3), t(4)), t(5), t(6))
            square_of((t(5), t(6)), AP8[:, 0, 0, :], AP8[:, 0, 1, :])
            for i in range(1, 8):
                x, y = (AP8[:, i - 1, 0, :], AP8[:, i - 1, 1, :]), (AP8[:, 0, 0, :], AP8[:, 0, 1, :])
                tt(t(0), x[0], y[0], ALU.mult)
                tt(t(1), x[1], y[1], ALU.mult)
                tt(AP8[:, i, 0, :], t(0), t(1), ALU.subtract)
                tt(t(0), x[0], y[1], ALU.mult)
                tt(t(1), x[1], y[0], ALU.mult)
                tt(AP8[:, i, 1, :], t(0), t(1), ALU.add)
            chain(pool.tensor_scalar(AP8[:, :, 2, :], AP8[:, :, 1, :], -1.0, None, ALU.mult))
            ts(t(11), t(13), -1.0, ALU.mult)
            tt(DM[:, :], IDENT[0:32, 0:C16], IDENT[0:32, C16:32], ALU.add)
            pool.wait_ge(consts_in, 16 * 3)
            pool.nop().then_inc(disc_p, 2)
            norm(1)
            tab = UNITS[("tab", 2)]
            pool.wait_ge(banks_full[tab.slot], tab.full(1))
            pool.wait_ge(ca_out, 16)
            chain(pool.memset(KT[:, :, 0:7 * C16], 0.0))
            pool.nop().then_inc(disc_p, 1)
            tab = UNITS[("tab", 3)]
            pool.wait_ge(banks_full[tab.slot], tab.full(2))
            pool.wait_ge(t0_out, 16 * 16)
            pool.memset(XS[:, :, DEC:DEC + 1], 0.0)
            chain(pool.memset(VPRE[:, :, 0:1], 0.0))
            pool.nop().then_inc(xs_zero, 1)
            pool.memset(U[:, :, 0:DEC], 0.0)
            chain(pool.memset(U[:, :, DEC + NK:UC], 0.0))
            pool.nop().then_inc(u_zero, 1)

            v3 = UNITS[("v", 3)]
            pool.wait_ge(banks_free[v3.slot], v3.full(2))
            v2 = UNITS[("v", 2)]
            pool.wait_ge(banks_free[v2.slot], v2.full(2))
            main = XS[:, :, DEC + 1:DEC + 1 + NK].rearrange("p g (b i) -> p g b i", i=8)

            def power(i, what, n, both):
                x = (AP8[:, i, what, :] if i >= 0 else t({0: 12, 1: 13, 2: 11}[what]))
                x = x.rearrange("p (r g o) -> p r g o", r=1, o=1)
                return x.broadcast_to([P, 2, GP, n]) if both else x[:, 0].broadcast_to([P, GP, n])

            def advance(dst, src, i, n):
                t1, t2 = ST1[:, :, :, 0:n], ST2[:, :, :, 0:n]
                halves = (slice(0, GP), slice(GP, 2 * GP))
                src4 = src.rearrange("p (r g) n -> p r g n", r=2)
                dst4 = dst.rearrange("p (r g) n -> p r g n", r=2)
                pool.tensor_tensor(t1, src4, power(i, 0, n, True), ALU.mult).then_inc(pool_step, 1)
                pool.tensor_tensor(t2[:, 0], src[:, halves[1], :], power(i, 2, n, False), ALU.mult).then_inc(pool_step, 1)
                count[0] += 2
                tt(t2[:, 1], src[:, halves[0], :], power(i, 1, n, False), ALU.mult)
                tt(dst4, dst4, t1, ALU.add)
                tt(dst4, dst4, t2, ALU.add)

            for i in range(1, 8):
                advance(main[:, :, :, i], main[:, :, :, i - 1], 0, 16)
            for b in range(1, 16):
                advance(main[:, :, b, 7:8], main[:, :, b - 1, 7:8], 7, 1)
            for i in range(7):
                advance(main[:, :, 1:16, i], main[:, :, 0:15, 7], i, 15)
            advance(XS[:, :, XC - DEC:XC], XS[:, :, 0:DEC], -1, DEC)
            for ri in range(2):
                chain(pool.tensor_copy(DNEW[:, ri, :].rearrange("p (t g) -> p g t", g=GP),
                                       XS[:, ri * GP:(ri + 1) * GP, XC - DEC:XC]))
            pool.nop().then_inc(scanned, 1)
            last = UNITS[("gb", 3)]
            pool.wait_ge(banks_full[last.slot], last.full(2))
            for g2 in range(2):
                half = slice(g2 * NS, (g2 + 1) * NS)
                chain(pool.memset(CB[half, :, :, 1 - g2, :], 0.0))
            pool.nop().then_inc(cb_zero, 1)
            pool.wait_ge(conv_step, 10 * WC)
            norm(2)


_OUTS = [("y_prompt", (1, SEQ, D)), ("y_sample", (DEC, 1, D)), ("re_prompt", (1, 1, G, NS)), ("im_prompt", (1, 1, G, NS)),
         ("conv_prompt", (1, 1, 2, W)), ("re_sample", (1, DEC, G, NS)), ("im_sample", (1, DEC, G, NS)),
         ("conv_sample", (1, DEC, 2, W))]


def kernel(**inputs):
    import concourse.bacc as bacc
    from concourse.bass_utils import run_bass_kernel_spmd

    nc = bacc.Bacc("TRN2", target_bir_lowering=False, num_devices=1)
    arrays, ins, outs = {}, {}, {}
    for name, value in inputs.items():
        arrays["in_" + name] = np.ascontiguousarray(value)
        ins[name] = nc.dram_tensor("in_" + name, arrays["in_" + name].shape, F32, kind="ExternalInput").ap()
    for name, shape in _OUTS:
        outs[name] = nc.dram_tensor("out_" + name, shape, F32, kind="ExternalOutput").ap()
    hybrid_trunk(nc, ins, outs)
    result = run_bass_kernel_spmd(nc, [arrays], core_ids=[0]).results[0]
    return tuple(result["out_" + name] for name, _ in _OUTS)
```

```python
from contextlib import ExitStack

import numpy as np

import concourse.bass as bass
from concourse import mybir

F32 = mybir.dt.float32
F32R = mybir.dt.float32r
ALU = mybir.AluOpType
ACT = mybir.ActivationFunctionType

P = 128
D = 1024
DC = D // P
SEQ = 1024
DEC = 8
S8 = 8
NK = SEQ // S8
NT = SEQ + DEC
TB = 3
TW = NT // TB
QW = TW // 4
XN = TB * DC
FF = 2816
NF = FF // P
W = 512
WC = W // P
G = 32
GP = G // 2
C16 = 16
NS = 64
EPS = 1e-6
UC = DEC + NK + DEC
XC = DEC + 1 + NK + DEC
YC = DEC + NK
MAGIC = 12582912.0
TWO_PI = 2 * np.pi
PI_A = 6.28125
PI_B = round((TWO_PI - PI_A) * 2**19) / 2**19
PI_C = TWO_PI - PI_A - PI_B


class Unit:

    def __init__(self, slot, before):
        self.slot, self.before = slot, before

    def full(self, bank):
        return 3 * self.before + bank + 1

    def at(self, step):
        return Unit(self.slot, self.before + step)


def plan():
    units, used, weights, loaded = {}, [0, 0], {}, [0, 0, 0]

    def weigh(name, slot, times=1):
        weights[name] = (slot, loaded[slot])
        loaded[slot] += times

    def add(name, slot, weighted=False, times=1, weights_in=None):
        units[name] = Unit(slot, used[slot])
        used[slot] += times
        if weighted:
            weigh(name, slot if weights_in is None else weights_in, times)

    add("gate1", 0, True, NF)
    add("up1", 1, True, NF)
    weigh("down1", 2, NF - 1)
    weigh("last1", 0)
    for j, slot in enumerate((2, 1, 0, 1)):
        add(("u", j), j % 2, True, weights_in=slot)
    weigh("downc", 2, WC)
    weigh("downs", 2, WC - 1)
    for n in range(4):
        add(("tab", n), n % 2)
    add("carried", 0)
    add("buffer", 1)
    n = 0
    for c in range(WC):
        for what in ("xc", "gc", "gb"):
            add((what, c), n % 2, True)
            n += 1
        if c == 0:
            for v in range(4):
                add(("v", v), (n + v) % 2)
    for j in range(4):
        add(("y", j), j % 2)
    add("states", 0)
    add("vout", 1)
    for j in range(WC):
        add(("glu", j), j % 2, True)
    weigh("last_s", 1)
    weigh("up2_first", 2)
    weigh("down2", 2, NF - 1)
    add("gate2", 0, True, NF)
    add("up2", 1)
    weigh("up2_rest", 1, NF - 1)
    used[1] += NF - 1
    weigh("last2", 0)
    return units, weights


UNITS, WEIGHTS = plan()
FIRST_UP = {"1": WEIGHTS["up1"], "2": WEIGHTS["up2_first"]}
UP = {"1": WEIGHTS["up1"][1], "2": WEIGHTS["up2_rest"][1] - 1}
GATE = {"1": WEIGHTS["gate1"][1], "2": WEIGHTS["gate2"][1]}
WEIGHTED = [("u", j) for j in range(WC)]
for _c in range(WC):
    WEIGHTED += [("xc", _c), ("gc", _c), ("gb", _c)]
WEIGHTED += [("glu", j) for j in range(WC)]

DOWN1, DOWNC, DOWNS, DOWN2 = 0, NF, NF + WC, NF + 2 * WC
ND = 2 * NF + 2 * WC
TILES = TB * DC

def down_weights(d):
    special = {NF - 1: "last1", DOWNS + WC - 1: "last_s", ND - 1: "last2"}
    return WEIGHTS[special[d]] if isinstance(d, int) and d in special else (2, d)


V_ITEMS = 2 * GP
V_BANKS = [list(range(b, min(b + 3, V_ITEMS))) for b in range(0, V_ITEMS, 3)]
Y_BANKS = [[0, 1, 2], [3, 4, 5], [6, 7]]


def hybrid_trunk(nc, a, o):
    ctx = ExitStack()

    def sb(name, shape, dt=F32, stack=ctx):
        return stack.enter_context(nc.sbuf_tensor(name, shape, dt))

    def sem(name):
        return ctx.enter_context(nc.semaphore(name))

    def dram(name, shape):
        return nc.dram_tensor(name, shape, F32, kind="Internal").ap()

    with ctx:
        HT = sb("HT", [P, DC, NT])
        RAW = sb("RAW", [P, 3, D])
        WH = sb("WH", [P, 3, D], F32R)
        WL = sb("WL", [P, 3, D], F32R)
        IDENT = sb("IDENT", [P, P])
        ONES = sb("ONES", [P, P])
        S = sb("S", [P, NT])
        T = sb("T", [P, NT])
        GAIN = sb("GAIN", [P, 3, DC])
        EPSC = sb("EPSC", [P, 1])
        CW = sb("CW", [P, 3, WC])
        BG = sb("BG", [P, WC])
        CBT = sb("CBT", [P, WC, 2 * DEC])
        VOUT = sb("VOUT", [P, WC, 16])
        SS = sb("SS", [P, S8 + 1, 2])
        RS = sb("RS", [P, S8 + 1])
        RQ = sb("RQ", [QW, 2 * TB, 4])
        LRI = sb("LRI", [P, 3, GP])
        TMP = sb("TMP", [P, 14, GP])
        AP8 = sb("AP8", [P, S8, 3, GP])
        DT = sb("DT", [32, GP])
        DM = sb("DM", [32, C16])
        st = ExitStack()
        XD = sb("XD", [DEC, D], F32, st)
        JUNK = sb("JUNK", [P, D], F32, st)
        st.close()
        WT = sb("WT", [P, GP, 2, P], F32, st)
        st.close()
        HH = sb("HH", [P, 2, NT], F32R)
        HL = sb("HL", [P, 2, NT], F32R)
        st = ExitStack()
        PROD = sb("PROD", [P, 2, GP, C16], F32, st)
        st.close()
        CARR = sb("CARR", [P, 2, P], F32, st)
        CBUF = sb("CBUF", [16, W], F32, st)
        st.close()
        R = sb("R", [P, NT])
        V = R
        st = ExitStack()
        BRAW = sb("BRAW", [P, 2, GP, C16], F32, st)
        PAR = sb("PAR", [96, P], F32, st)
        st.close()
        CS = sb("CS", [P, 2, P], F32, st)
        st.close()
        ST1 = sb("ST1", [P, 2, GP, GP], F32, st)
        ST2 = sb("ST2", [P, 2, GP, GP], F32, st)
        st.close()
        SQ = sb("SQ", [P, NT])
        st = ExitStack()
        T0 = sb("T0", [P, GP, 2, P], F32, st)
        CB = sb("CB", [P, GP, 2, 2, P], F32, st)
        Z = sb("Z", [P, 2, 8, YC], F32, st)
        st.close()
        ZH = sb("ZH", [P, WC, NT], F32R, st)
        ZL = sb("ZL", [P, WC, NT], F32R, st)
        st.close()
        XH = sb("XH", [P, DC, NT], F32R)
        XL = sb("XL", [P, DC, NT], F32R)
        st = ExitStack()
        X = sb("X", [P, S8, D], F32, st)
        st.close()
        CA = sb("CA", [P, GP, 2, 9 * C16], F32, st)
        BD = sb("BD", [P, GP, 2, 2 * C16], F32, st)
        st2 = ExitStack()
        CL = sb("CL", [P, 2, 4, P], F32, st2)
        st2.close()
        BS = sb("BS", [P, GP, 2, P], F32, st)
        st.close()
        sb("over_CA", [P, GP, 2, 9 * C16], F32, st)
        sb("over_BD", [P, GP, 2, 2 * C16], F32, st)
        KT = sb("KT", [32, GP, 15 * C16], F32, st)
        DTM = sb("DTM", [32, GP, C16], F32, st)
        st.close()
        U = sb("U", [P, G, UC], F32, st)
        XS = sb("XS", [P, 2 * GP, XC], F32, st)
        VPRE = sb("VPRE", [P, 2, NK], F32, st)
        DNEW = sb("DNEW", [P, 2, P], F32, st)
        st.close()
        ZT = sb("ZT", [P, WC, NT], F32, st)
        STO = sb("STO", [P, 4, P], F32, st)
        VO = sb("VO", [16, W], F32, st)
        st.close()
        OUT = sb("OUT", [P, 4, D], F32, st)
        GF = sb("GF", [P, D], F32, st)
        st.close()

        AB = [[ctx.enter_context(nc.psum_tensor(f"bank{s}{b}", [P, 512], F32)) for b in range(3)] for s in range(2)]
        DB = [ctx.enter_context(nc.psum_tensor(f"bank_down{b}", [P, 512], F32)) for b in range(2)]

        UD = dram("u_scratch", [W, NT])
        ZD = dram("z_scratch", [W, NT])
        CAD = dram("ca_scratch", [P, GP * 2, 9 * C16])
        T0D = dram("t0_scratch", [P, GP, 2, P])

        banks_full = [sem("banks_full_0"), sem("banks_full_1")]
        banks_free = [sem("banks_free_0"), sem("banks_free_1")]
        raw_full = [sem(f"raw_full_{s}") for s in range(3)]
        w_hi = [sem(f"w_hi_{s}") for s in range(3)]
        w_split = [sem(f"w_split_{s}") for s in range(3)]
        hi_done = sem("hi_done")
        h_ready = sem("h_ready")
        down_full = sem("down_full")
        down_free = sem("down_free")
        gate_done = sem("gate_done")
        x_in = [sem(f"x_in_{s}") for s in range(S8 + 1)]
        sq_x = sem("sq_x")
        sqrt_x = sem("sqrt_x")
        ss_sum = sem("ss_sum")
        rcp_x = sem("rcp_x")
        diag_x = sem("diag_x")
        xt_full = sem("xt_full")
        xt_free = sem("xt_free")
        par_full = sem("par_full")
        par_free = sem("par_free")
        xn_hi = sem("xn_hi")
        xn_low = [sem("xn_low_pool"), sem("xn_low_dve")]
        xn_tmp = sem("xn_tmp")
        sq_done = sem("sq_done")
        acc_done = sem("acc_done")
        sums_done = sem("sums_done")
        rt_done = sem("rt_done")
        rcp_done = sem("rcp_done")
        diag_done = sem("diag_done")
        const_done = sem("const_done")
        spread_full = sem("spread_full")
        spread_free = sem("spread_free")
        gain_in = sem("gain_in")
        gains_in = sem("gains_in")
        consts_in = sem("consts_in")
        c_in = sem("c_in")
        b_in = sem("b_in")
        par_in = sem("par_in")
        dt_in = sem("dt_in")
        par_set = sem("par_set")
        lri_done = sem("lri_done")
        c_done = sem("c_done")
        disc_a = sem("disc_a")
        disc_p = sem("disc_p")
        den_inv = sem("den_inv")
        pool_step = sem("pool_step")
        ca_out = sem("ca_out")
        kt_done = sem("kt_done")
        dt_k = sem("dt_k")
        t0_out = sem("t0_out")
        u_out = [sem(f"u_out_{j}") for j in range(WC)]
        u_zero = sem("u_zero")
        u_in = sem("u_in")
        carr_in = sem("carr_in")
        cbt_done = sem("cbt_done")
        xs_zero = sem("xs_zero")
        scanned = sem("scanned")
        conv_step = sem("conv_step")
        cb_zero = sem("cb_zero")
        y_tab = [sem(f"y_tab_{j}") for j in range(WC)]
        z_out = [sem(f"z_out_{j}") for j in range(WC)]
        zt_in = [sem(f"zt_in_{j}") for j in range(WC)]
        z_hi = sem("z_hi")
        z_ready = sem("z_ready")
        small_out = sem("small_out")
        st_out = sem("st_out")
        gf_in = sem("gf_in")
        out_done = sem("out_done")
        y_out = [sem(f"y_out_{n}") for n in range(4)]
        out_full = sem("out_full")
        out_free = sem("out_free")

        block = ctx.enter_context(nc.Block())

        def cols(tb):
            return slice(tb * TW, (tb + 1) * TW)

        def ring(i):
            return (S, T)[i % 6 // 3][:, (i % 3) * TW:(i % 3 + 1) * TW]

        OB = [(AB[0][0], AB[0][1]), (AB[1][0], AB[1][1]), (AB[0][2], AB[1][2])]

        alone = {
            DOWN1 + NF - 1: ((AB[0][1], UNITS["gate1"].at(NF - 1)), (AB[0][2], UNITS["gate1"].at(NF - 1))),
            DOWNC + WC - 1: ((AB[0][1], UNITS[("gc", 3)]), (AB[0][2], UNITS[("gc", 3)])),
            DOWNS + WC - 1: ((AB[0][1], UNITS[("glu", 2)]), (AB[0][2], UNITS[("glu", 2)])),
            ND - 1: ((AB[0][2], UNITS["gate2"].at(NF - 1)), (AB[1][2], UNITS["up2"].at(NF - 1))),
        }
        for j in range(WC - 1):
            alone[DOWNS + j] = ((AB[j % 2][1], UNITS[("glu", j)]), (AB[j % 2][2], UNITS[("glu", j)]))
        alone_order = [0, 1, 2, 3] * 5 + [0, 1, 0, 1]

        def down_bank(d, t):
            if not (isinstance(d, int) and d in alone):
                return DB[t % 2], TILES * d + t - 1
            n = alone_order[t]
            if n in alone_order[:t]:
                last = max(i for i in range(t) if alone_order[i] == n)
                return (DB[n] if n < 2 else alone[d][n - 2][0]), TILES * d + last + 1
            return (DB[n], TILES * d + t - 1) if n < 2 else alone[d][n - 2]

        def x_bank(s):
            if s < 6:
                return AB[1][1 + s % 2], s - 2 if s >= 2 else None
            return AB[1][2], s - 1

        def by_dve(i):
            return i < 5 or i % 3 == 2

        vector_blocks = sum(map(by_dve, range(XN)))

        def low_count(k, i):
            mine = sum(map(by_dve, range(i + 1)))
            if by_dve(i):
                return xn_low[1], vector_blocks * k + mine
            return xn_low[0], (XN - vector_blocks) * k + i + 1 - mine

        def wait_xn(eng, k):
            eng.wait_ge(*low_count(k, XN - 2))
            eng.wait_ge(*low_count(k, XN - 1))

        def take(eng, unit, bank=0):
            if isinstance(unit.before, int) and 3 * unit.before + bank == 0:
                return
            eng.wait_ge(banks_free[unit.slot], 3 * unit.before + bank)

        def last_tile(d):
            return TILES * (d + 1)

        x_rows = a["x_prompt"].rearrange("b (k s) d -> (b k) s d", s=S8)
        xs_rows = a["x_sample"].rearrange("b t d -> (b t) d")
        w_in = a["w_in"][0]

        def columns(w, n, k=DC):
            return w.rearrange("(c p) m -> p c m", p=P)[:, 0:k, n * P:(n + 1) * P] if isinstance(n, int) \
                else w.rearrange("(c p) m -> p c m", p=P)[:, 0:k, bass.ds(n * P, P)]

        def weights_of(name):
            what, j = name
            if what == "glu":
                return columns(a["ssm_w_glu"][0], j, WC)
            first = {"u": 0, "xc": W, "gb": 2 * W, "gc": 3 * W}[what] // P
            return columns(w_in, first + j)

        def down_rows(w, f):
            return w[f * P:(f + 1) * P, :] if isinstance(f, int) else w[bass.ds(f * P, P), :]

        @block.sync
        def _(sp):
            def load(slot, n, src):
                if not (isinstance(n, int) and n == 0):
                    sp.wait_ge(w_split[slot], n)
                dst = RAW[:, slot, :]
                if len(src.shape) == 3:
                    dst = dst.rearrange("p (c m) -> p c m", m=P)[:, 0:src.shape[1]]
                sp.dma_start(dst, src).then_inc(raw_full[slot], 16)

            def load_named(name):
                load(*WEIGHTS[name], weights_of(name))

            for s in range(2):
                sp.dma_start(X[:, s, :], x_rows[:, s, :]).then_inc(x_in[s], 16)
            load(0, 0, columns(a["ffn1_w_gate"][0], 0))
            for s in range(2, S8):
                sp.dma_start(X[:, s, :], x_rows[:, s, :]).then_inc(x_in[s], 16)
                if s == 3:
                    load(1, 0, columns(a["ffn1_w_up"][0], 0))
            sp.dma_start(XD[:, :], xs_rows).then_inc(x_in[S8], 16)
            sp.dma_start(o["conv_sample"][0, :, 0, :], a["state_conv"][0, :, 1, :]).then_inc(small_out, 16)
            load(2, 0, down_rows(a["ffn1_w_down"][0], 0))

            def ffn_rest(which, wg, wu, wd, down):
                with sp.Fori(1, NF - 1) as f:
                    load(0, f + GATE[which], columns(wg, f))
                    load(1, f + UP[which], columns(wu, f))
                    load(2, f + down, down_rows(wd, f))
                f = NF - 1
                load(0, f + GATE[which], columns(wg, f))
                load(1, f + UP[which], columns(wu, f))
                load(*WEIGHTS["last" + which], down_rows(wd, f))

            ffn_rest("1", a["ffn1_w_gate"][0], a["ffn1_w_up"][0], a["ffn1_w_down"][0], DOWN1)

            for j in range(3):
                load_named(("u", j))
            load(2, DOWNC, down_rows(a["w_out"][0], WC))
            load_named(("u", 3))
            wait_xn(sp, 1)
            for ri, name in enumerate(("state_ssm_re", "state_ssm_im")):
                sp.dma_start(CARR[:, ri, :], a[name][0].rearrange("b (g e) p -> (b g) (e p)", e=2)).then_inc(carr_in, 16)
            sp.dma_start(CBUF[:, :], a["state_conv"][0].rearrange("b r c -> (b r) c")).then_inc(carr_in, 16)

            def store_u(j):
                unit = UNITS[("u", j)]
                sp.wait_ge(banks_free[unit.slot], unit.full(2))
                sp.dma_start(UD[j * P:(j + 1) * P, :], (S, T)[j % 2][:, :]).then_inc(u_out[j], 16)

            store_u(0)
            load_named(("xc", 0))
            store_u(1)
            load_named(("gc", 0))
            store_u(2)
            load_named(("gb", 0))
            store_u(3)
            for j in range(WC):
                sp.wait_ge(u_out[j], 16)
            sp.wait_ge(u_zero, 1)
            ug = UD.rearrange("(g c) n -> c g n", c=C16)
            for s in range(S8):
                sp.dma_start(U[s * C16:(s + 1) * C16, :, DEC:DEC + NK], ug[:, :, s * NK:(s + 1) * NK]).then_inc(u_in, 16)
            with nc.allow_non_contiguous_dma(reason="32 bytes a row, small"):
                sp.dma_start(U[0:C16, :, 0:DEC], ug[:, :, SEQ:NT]).then_inc(u_in, 16)
                sp.dma_start(U[P - C16:P, :, DEC + NK:UC], ug[:, :, SEQ:NT]).then_inc(u_in, 16)
            sp.wait_ge(dt_k, 1)
            for s in range(S8):
                for g2 in range(2):
                    sp.dma_start(T0D[s * C16:(s + 1) * C16, :, g2, :],
                                 KT[g2 * C16:(g2 + 1) * C16, :, (7 - s) * C16:(7 - s) * C16 + P]).then_inc(t0_out, 16)

            for c in range(1, WC):
                for what in ("xc", "gc", "gb"):
                    load_named((what, c))
                load(2, DOWNC + c, down_rows(a["w_out"][0], WC + c))
            load_named(("glu", 0))
            load_named(("glu", 1))
            last = UNITS[("gb", 3)]
            sp.wait_ge(banks_full[last.slot], last.full(2))
            sp.wait_ge(t0_out, 16 * 16)
            sp.wait_ge(ca_out, 16)
            for j in range(WC):
                q = slice(4 * j, 4 * j + 4)
                sp.dma_start(T0[:, q], T0D[:, q]).then_inc(y_tab[j], 16)
                for g2 in range(2):
                    half = slice(g2 * NS, (g2 + 1) * NS)
                    sp.dma_start(CB[half, q, :, g2, :].rearrange("p g r n -> p (g r) n"),
                                 CAD[half, 8 * j:8 * j + 8, C16:]).then_inc(y_tab[j], 16)
            def load_z(j):
                sp.wait_ge(z_out[j], 16 * 9)
                sp.dma_start(ZT[:, j, :], ZD[j * P:(j + 1) * P, :]).then_inc(zt_in[j], 16)

            for j in range(WC):
                if j == WC - 1:
                    states = UNITS["states"]
                    sp.wait_ge(banks_full[states.slot], states.full(2))
                    load_z(0)
                    load_z(1)
                unit = UNITS[("y", j)]
                sp.wait_ge(banks_free[unit.slot], unit.full(2))
                zg = ZD[j * P:(j + 1) * P, :].rearrange("(g c) n -> c g n", c=C16)
                for t in range(S8):
                    sp.dma_start(zg[:, :, t * NK:(t + 1) * NK],
                                 Z[t * C16:(t + 1) * C16, j % 2, :, DEC:YC]).then_inc(z_out[j], 16)
                with nc.allow_non_contiguous_dma(reason="32 bytes a row, small"):
                    sp.dma_start(zg[:, :, SEQ:NT], Z[0:C16, j % 2, :, 0:DEC]).then_inc(z_out[j], 16)
            load_z(2)
            load_z(3)
            load(2, DOWNS, down_rows(a["w_out"][0], 0))
            sp.wait_ge(st_out, 2)
            for ri, (ps, ss) in enumerate((("re_prompt", "re_sample"), ("im_prompt", "im_sample"))):
                sp.dma_start(o[ps][0, 0].rearrange("(g e) p -> g (e p)", e=2), STO[0:GP, 2 + ri, :]).then_inc(small_out, 16)
                sp.dma_start(o[ss][0].rearrange("b (g e) p -> (b g) (e p)", e=2), STO[:, ri, :]).then_inc(small_out, 16)
            sp.dma_start(o["conv_sample"][0, :, 1, :], VO[0:DEC, :]).then_inc(small_out, 16)
            sp.dma_start(o["conv_prompt"][0, 0], VO[DEC:DEC + 2, :]).then_inc(small_out, 16)
            for j in range(2, WC):
                load_named(("glu", j))
                load(2, DOWNS + j - 1, down_rows(a["w_out"][0], j - 1))
            load(*WEIGHTS["gate2"], columns(a["ffn2_w_gate"][0], 0))
            load(*WEIGHTS["last_s"], down_rows(a["w_out"][0], 3))
            load(*WEIGHTS["up2_first"], columns(a["ffn2_w_up"][0], 0))
            load(2, DOWN2, down_rows(a["ffn2_w_down"][0], 0))
            ffn_rest("2", a["ffn2_w_gate"][0], a["ffn2_w_up"][0], a["ffn2_w_down"][0], DOWN2)
            sp.wait_ge(small_out, 16 * 7)
            sp.dma_start(GF[:, :], a["final_norm"].rearrange("(o d) -> o d", o=1).to_broadcast([P, D])).then_inc(gf_in, 16)
            y_rows = o["y_prompt"].rearrange("b (k s) d -> (b k) s d", s=S8)
            for s in range(S8 + 1):
                sp.wait_ge(out_done, 2 * s + 2)
                if s < S8:
                    sp.dma_start(y_rows[:, s, :], OUT[:, s % 4, :]).then_inc(y_out[s % 4], 16)
                else:
                    sp.dma_start(o["y_sample"].rearrange("b t d -> (b t) d"), OUT[0:DEC, s % 4, :]).then_inc(y_out[s % 4], 16)
            for n in range(4):
                sp.wait_ge(y_out[n], 16 * (3 if n == 0 else 2))

        @block.tensor
        def _(pe):
            def product3(out, wh, wl, xh, xl, first, last):
                pe.matmul(out, wh, xh, start=first, stop=False)
                pe.matmul(out, wh, xl, start=False, stop=False)
                return pe.matmul(out, wl, xh, start=False, stop=last)

            def bank_wait(unit, b):
                if isinstance(unit.before, int) and unit.before == 0:
                    return
                pe.wait_ge(banks_free[unit.slot], 3 * unit.before + b - 2)

            def down_tile(d, par, tb, j):
                slot = down_weights(d)[0]
                out, free = down_bank(d, DC * tb + j)
                if isinstance(d, int) and d == 0 and tb == 0 and j < 2:
                    pe.wait_ge(par_free, 3)
                elif isinstance(free, Unit):
                    pe.wait_ge(banks_free[free.slot], free.full(2))
                else:
                    pe.wait_ge(down_free, free)
                out = out[:, 0:TW]
                m = slice(j * P, (j + 1) * P)
                product3(out, WH[:, slot, m], WL[:, slot, m], HH[:, par, cols(tb)], HL[:, par, cols(tb)], True, True
                         ).then_inc(down_full, 1)

            def down_start(d):
                slot, n = down_weights(d)
                pe.wait_ge(w_split[slot], n + 1)

            def down_block(d, par, tb):
                pe.wait_ge(h_ready, 3 * d + tb + 1)
                for j in range(DC):
                    down_tile(d, par, tb, j)

            def project(unit, weight, xh=XH, xl=XL, k=DC, x_wait=None, down=None):
                slot, number = weight
                pe.wait_ge(w_split[slot], number + 1)
                if down is not None:
                    down_start(down[0])
                for tb in range(TB):
                    if x_wait is not None:
                        pe.wait_ge(*x_wait[tb])
                    bank_wait(unit, tb)
                    if down is not None:
                        pe.wait_ge(h_ready, 3 * down[0] + tb + 1)
                    out = AB[unit.slot][tb][:, 0:TW]
                    for c in range(k):
                        m = slice(c * P, (c + 1) * P)
                        last = product3(out, WH[:, slot, m], WL[:, slot, m], xh[:, c, cols(tb)],
                                        xl[:, c, cols(tb)], c == 0, c == k - 1)
                        if c == k - 1:
                            last.then_inc(banks_full[unit.slot], 1)
                        if down is not None:
                            down_tile(down[0], down[1], tb, c)

            def project_two(units, weights, k, after):
                for tb in range(TB):
                    for unit in units:
                        bank_wait(unit, tb)
                    for group in (((0, 1),) if k > 0 and tb < TB - 1 else ((0,), (1,))):
                        if tb == 0:
                            for n in group:
                                slot, number = weights[n]
                                pe.wait_ge(w_split[slot], number + 1)
                        for c in range(DC):
                            m = slice(c * P, (c + 1) * P)
                            if group[0] == 0:
                                pe.wait_ge(*low_count(k, DC * tb + c))
                            for n in group:
                                slot = weights[n][0]
                                last = product3(AB[units[n].slot][tb][:, 0:TW], WH[:, slot, m], WL[:, slot, m],
                                                XH[:, c, cols(tb)], XL[:, c, cols(tb)], c == 0, c == DC - 1)
                                if c == DC - 1:
                                    last.then_inc(banks_full[units[n].slot], 1)
                            if (tb, group[-1], c) in after:
                                after[tb, group[-1], c]()

            def norm_sums(free, k, tb):
                pe.wait_ge(banks_free[free.slot], free.full(tb))
                pe.wait_ge(acc_done, (DC - 1) * (TB * (k - 1) + tb + 1))
                for q in range(4):
                    at = tb * TW + q * QW
                    last = pe.matmul(AB[1][tb][0:QW, TW + q:TW + q + 1], R[:, at:at + QW], ONES[:, 0:1],
                                     start=True, stop=True)
                last.then_inc(sums_done, 1)

            def norm_spread(k, tb):
                for q in range(4):
                    at = tb * TW + q * QW
                    pe.wait_ge(diag_done, 4 * (TB * (k - 1) + tb) + q + 1)
                    last = pe.matmul(AB[1][tb][:, q * QW:(q + 1) * QW], ONES[0:QW, :], R[0:QW, at:at + QW],
                                     start=True, stop=True)
                last.then_inc(spread_full, 1)

            def last_down(d, free, k):
                down_start(d)
                for tb in range(TB):
                    pe.wait_ge(h_ready, 3 * d + tb + 1)
                    for j in range(DC):
                        down_tile(d, d % 2, tb, j)
                        if tb > 0 and j == 4:
                            norm_sums(free, k, tb - 1)
                        if tb == 1 and j == DC - 1:
                            norm_spread(k, 0)
                return {(0, 1, 5): lambda: norm_spread(k, 1), (0, 1, 6): lambda: norm_sums(free, k, 2),
                        (1, 1, 2): lambda: norm_spread(k, 2)}

            def ffn(which, down, k, after, between):
                ug, uu = UNITS["gate" + which], UNITS["up" + which]
                project_two((ug, uu), (WEIGHTS["gate" + which], FIRST_UP[which]), k, after)
                if between is not None:
                    between()

                def step(f, par):
                    project(ug.at(f), (0, f + GATE[which]))
                    project(uu.at(f), (1, f + UP[which]), down=(f + (down - 1), par))
                step(1, 0)
                step(2, 1)
                with pe.Fori(1, (NF - 2) // 2) as i:
                    step(i * 2 + 1, 0)
                    step(i * 2 + 2, 1)
                step(NF - 1, 0)

            pe.wait_ge(const_done, 3)

            def x_transpose(s):
                pe.wait_ge(x_in[s], 16)
                for h in range(2):
                    if s > 0:
                        pe.wait_ge(xt_free, 2 * s + h - 1)
                    for c in range(4 * h, 4 * h + 4):
                        m = slice(c * P, (c + 1) * P)
                        if s < S8:
                            last = pe.transpose(DB[h][:, (c % 4) * P:(c % 4 + 1) * P], X[:, s, m], IDENT[:, :])
                        else:
                            last = pe.transpose(DB[h][:, (c % 4) * DEC:(c % 4 + 1) * DEC], XD[:, m], IDENT[0:DEC, 0:DEC])
                    last.then_inc(xt_full, 1)

            def x_spread(s):
                m = P if s < S8 else DEC
                bank, earlier = x_bank(s)
                if earlier is not None:
                    pe.wait_ge(spread_free, earlier + 1)
                pe.wait_ge(diag_x, s + 1)
                pe.matmul(bank[:, 0:m], ONES[0:m, :], R[0:m, s * P:s * P + m], start=True, stop=True
                          ).then_inc(spread_full, 1)

            def x_next(transposes, spreads):
                for s in transposes:
                    x_transpose(s)
                for s in spreads:
                    x_spread(s)

            def parameters():
                pe.wait_ge(par_set, 3)
                pe.wait_ge(xt_free, 2 * (S8 + 1))
                pe.transpose(DB[0][:, 0:96], PAR[:, :], IDENT[0:96, 0:96]).then_inc(par_full, 1)
                pe.wait_ge(c_in, 64)
                for ri in range(2):
                    if ri == 1:
                        pe.wait_ge(par_free, 1)
                    for q in range(4):
                        last = pe.transpose(DB[1 - ri][:, q * P:(q + 1) * P], CL[:, ri, q, :], IDENT[:, :])
                    last.then_inc(par_full, 1)

            x_next((0, 1), (0,))
            x_next((2,), (1,))
            x_next((3,), (2,))
            ffn("1", DOWN1, 0, {(0, 0, DC - 1): lambda: x_next((4, 5), (3, 4)), (0, 1, 0): lambda: x_next((), (5,)),
                                (0, 1, DC - 1): lambda: x_next((6,), ()), (1, 0, 4): lambda: x_next((7,), (6,)),
                                (1, 0, 6): lambda: x_next((8,), (7,)), (1, 1, 0): lambda: x_next((), (8,))}, parameters)

            after = last_down(DOWN1 + NF - 1, UNITS["up1"].at(NF - 1), 1)
            project_two((UNITS[("u", 0)], UNITS[("u", 1)]), (WEIGHTS[("u", 0)], WEIGHTS[("u", 1)]), 1, after)
            for j in range(2, WC):
                project(UNITS[("u", j)], WEIGHTS[("u", j)])
            pe.wait_ge(disc_p, 4)
            for n in range(8):
                unit, b = UNITS[("tab", n // 3)], n % 3
                bank_wait(unit, b)
                for q in range(4):
                    i = 4 * n + q
                    last = pe.transpose(AB[unit.slot][b][:, q * P:(q + 1) * P], BS[:, i // 2, i % 2, :], IDENT[:, :])
                last.then_inc(banks_full[unit.slot], 1)
            for n in range(8, 12):
                unit, b = UNITS[("tab", n // 3)], n % 3
                bank_wait(unit, b)
                for q in range(4):
                    i = 4 * (n - 8) + q
                    for ri in range(2):
                        last = pe.matmul(AB[unit.slot][b][0:32, q * P:(q + 1) * P], BD[:, i, ri, :], CA[:, i, ri, 0:P],
                                         start=ri == 0, stop=ri == 1)
                last.then_inc(banks_full[unit.slot], 1)
            unit = UNITS["carried"]
            pe.wait_ge(carr_in, 48)
            bank_wait(unit, 2)
            for ri in range(2):
                last = pe.transpose(AB[unit.slot][0][:, ri * P:(ri + 1) * P], CARR[:, ri, :], IDENT[:, :])
            last.then_inc(banks_full[unit.slot], 3)
            unit = UNITS["buffer"]
            bank_wait(unit, 2)
            for j in range(WC):
                last = pe.transpose(AB[unit.slot][0][:, j * 16:(j + 1) * 16], CBUF[:, j * P:(j + 1) * P],
                                    IDENT[0:16, 0:16])
            last.then_inc(banks_full[unit.slot], 3)

            for c in range(WC):
                project(UNITS[("xc", c)], WEIGHTS[("xc", c)])
                project(UNITS[("gc", c)], WEIGHTS[("gc", c)], down=None if c == 0 else (DOWNC + c - 1, (c - 1) % 2))
                project(UNITS[("gb", c)], WEIGHTS[("gb", c)])
                if c == 0:
                    pe.wait_ge(u_in, 16 * 10)
                    for n, items in enumerate(V_BANKS):
                        unit, b = UNITS[("v", n // 3)], n % 3
                        bank_wait(unit, b)
                        for q, i in enumerate(items):
                            ri, g = divmod(i, GP)
                            for g2 in range(2):
                                half = slice(g2 * NS, (g2 + 1) * NS)
                                last = pe.matmul(AB[unit.slot][b][half, q * YC:(q + 1) * YC], WT[:, g, ri, half],
                                                 U[:, 2 * g + g2, DEC:UC], start=True, stop=True)
                        last.then_inc(banks_full[unit.slot], 2 if n == len(V_BANKS) - 1 else 1)

            d = DOWNC + 3
            down_start(d)
            down_block(d, d % 2, 0)
            pe.wait_ge(scanned, 1)
            pe.wait_ge(down_free, TILES * d + DC)
            for j in range(WC):
                unit = UNITS[("y", j)]
                pe.wait_ge(y_tab[j], 48)
                pe.wait_ge(cb_zero, 2 * j + 2)
                for b, items in enumerate(Y_BANKS):
                    bank_wait(unit, b)
                    for q, i in enumerate(items):
                        g = 8 * j + i
                        out = AB[unit.slot][b][:, q * YC:(q + 1) * YC]
                        pe.matmul(out, T0[:, g // 2, g % 2, :], U[:, g, 0:YC], start=True, stop=False)
                        pe.matmul(out, CB[:, g // 2, 0, g % 2, :], XS[:, g // 2, 0:YC], start=False, stop=False)
                        last = pe.matmul(out, CB[:, g // 2, 1, g % 2, :], XS[:, GP + g // 2, 0:YC], start=False, stop=True)
                    last.then_inc(banks_full[unit.slot], 1)
            unit = UNITS["states"]
            bank_wait(unit, 2)
            for ri in range(2):
                pe.transpose(AB[unit.slot][0][:, ri * P:(ri + 1) * P], DNEW[:, ri, :], IDENT[:, :])
                last = pe.transpose(AB[unit.slot][0][0:GP, (2 + ri) * P:(3 + ri) * P],
                                    XS[:, ri * GP:(ri + 1) * GP, DEC + NK], IDENT[:, :])
            last.then_inc(banks_full[unit.slot], 3)
            unit = UNITS["vout"]
            bank_wait(unit, 2)
            pe.wait_ge(conv_step, 10 * WC)
            for j in range(WC):
                last = pe.transpose(AB[unit.slot][0][0:16, j * P:(j + 1) * P], VOUT[:, j, :], IDENT[:, :])
            last.then_inc(banks_full[unit.slot], 3)
            for tb in range(1, TB):
                down_block(d, d % 2, tb)

            zw = [(z_ready, 4), (z_ready, 8), (z_ready, 12)]
            for j in range(WC):
                if j >= 2:
                    pe.wait_ge(down_free, TILES * (DOWNS + j - 2) + 20)
                project(UNITS[("glu", j)], WEIGHTS[("glu", j)], ZH, ZL, WC, x_wait=zw if j == 0 else None)
                if j >= 1:
                    down_start(DOWNS + j - 1)
                    for tb in range(TB):
                        down_block(DOWNS + j - 1, (j - 1) % 2, tb)
            after = last_down(DOWNS + 3, UNITS[("glu", 3)], 2)

            ffn("2", DOWN2, 2, after, None)
            d = DOWN2 + NF - 1
            down_start(d)
            def out_tile(s):
                if s >= 3:
                    pe.wait_ge(out_free, s - 2)
                last_col = (s + 1) * NK if s < S8 else NT
                pe.wait_ge(down_free, TILES * d + DC * -(-last_col // TW))
                m = NK if s < S8 else DEC
                for c in range(DC):
                    last = pe.transpose(OB[s % 3][c // 4][0:m, (c % 4) * P:(c % 4 + 1) * P],
                                        HT[:, c, s * NK:s * NK + m], IDENT[:, :])
                last.then_inc(out_full, 1)

            down_block(d, d % 2, 0)
            down_block(d, d % 2, 1)
            out_tile(0)
            out_tile(1)
            down_block(d, d % 2, 2)
            pe.wait_ge(down_free, TILES * d + 20)
            for s in range(2, S8 + 1):
                out_tile(s)

        @block.scalar
        def _(act):
            def split_hi(slot, n, k=DC, unit=None, down=None):
                act.wait_ge(raw_full[slot], (n + 1) * 16)
                if unit is not None:
                    act.wait_ge(banks_full[unit.slot], unit.full(2))
                if down is not None:
                    act.wait_ge(down_full, last_tile(down))
                act.activation(WH[:, slot, 0:k * P], RAW[:, slot, 0:k * P], ACT.Copy).then_inc(w_hi[slot], 1)

            def h_hi(d, par, tb, wait):
                act.wait_ge(*wait)
                if not (isinstance(d, int) and d < 2):
                    act.wait_ge(down_full, TILES * (d - 1))
                act.activation(HH[:, par, cols(tb)], T[:, cols(tb)], ACT.Copy).then_inc(hi_done, 1)

            def upper(k, i):
                tb, c = divmod(i, DC)
                act.wait_ge(xn_tmp, XN * k + i + 1)
                act.activation(XH[:, c, cols(tb)], ring(i), ACT.Copy).then_inc(xn_hi, 1)

            def spread(n, columns, src):
                act.wait_ge(spread_full, n + 1)
                act.activation(R[:, columns], src, ACT.Copy).then_inc(spread_free, 1)

            def norm(k, d, free_unit):
                def squares(tb, first, last):
                    for c in range(first, last):
                        i = DC * tb + c
                        act.wait_ge(down_free, TILES * d + DC * tb + c + 1)
                        if i >= 3:
                            block, q = divmod(i - 3, DC)
                            act.wait_ge(acc_done, (DC - 1) * (TB * (k - 1) + block) + max(q, 1))
                        act.activation(SQ[:, (i % 3) * TW:(i % 3 + 1) * TW], HT[:, c, cols(tb)], ACT.Square
                                       ).then_inc(sq_done, 1)

                def root(tb):
                    n = TB * (k - 1) + tb
                    act.wait_ge(sums_done, n + 1)
                    act.activation(RQ[:, n, :], AB[1][tb][0:QW, TW:TW + 4], ACT.Sqrt, bias=EPSC[0:QW, :],
                                   scale=1.0 / D).then_inc(rt_done, 1)

                def spread_block(tb):
                    spread(S8 + 1 + TB * (k - 1) + tb, cols(tb), AB[1][tb][:, 0:TW])

                def uppers(first, last):
                    for i in range(first, last):
                        upper(k, i)

                squares(0, 0, DC)
                squares(1, 0, 5)
                root(0)
                squares(1, 5, DC)
                squares(2, 0, 1)
                spread_block(0)
                squares(2, 1, 5)
                root(1)
                squares(2, 5, DC)
                for u in free_unit:
                    act.wait_ge(banks_full[u.slot], u.full(2))
                uppers(0, 7)
                spread_block(1)
                uppers(7, DC)
                root(2)
                uppers(DC, DC + 5)
                spread_block(2)
                uppers(DC + 5, XN)

            def ffn(which, down):
                ug, uu = UNITS["gate" + which], UNITS["up" + which]
                wg, wu = GATE[which], UP[which]

                def silu(f, blocks=range(TB)):
                    for tb in blocks:
                        act.wait_ge(banks_full[0], ug.at(f).full(tb))
                        if not (isinstance(f, int) and f == 0):
                            act.wait_ge(banks_free[1], uu.at(f - 1).full(tb))
                        else:
                            take(act, ug, tb)
                            wait_xn(act, 0 if down == 0 else 2)
                        act.activation(S[:, cols(tb)], AB[0][tb][:, 0:TW], ACT.Silu).then_inc(banks_free[0], 1)

                def uppers(f, par):
                    for tb in range(TB):
                        h_hi(f + down, par, tb, (banks_free[1], uu.at(f).full(tb)))

                def step(f, par):
                    split_hi(1, f + wu, unit=uu.at(f - 1))
                    if isinstance(f, int) and f == 1:
                        split_hi(2, down) if down == 0 else split_hi(2, down, down=down - 1)
                    else:
                        split_hi(2, f + (down - 1), down=f + (down - 2))
                    silu(f)
                    split_hi(0, f + (wg + 1), unit=ug.at(f))
                    uppers(f, par)

                silu(0, (0, 1))
                split_hi(0, wg + 1, unit=ug)
                silu(0, (2,))
                uppers(0, 0)
                if down == 0:
                    act.wait_ge(lri_done, 3)
                    act.activation(TMP[:, 0, :], LRI[:, 2, :], ACT.Exp).then_inc(disc_a, 1)
                step(1, 1)
                if down == 0:
                    act.wait_ge(disc_p, 1)
                    act.activation(TMP[:, 3, :], TMP[:, 1, :], ACT.Exp).then_inc(disc_a, 1)
                    act.activation(TMP[:, 4, :], TMP[:, 2, :], ACT.Sin).then_inc(disc_a, 1)
                    act.activation(TMP[:, 5, :], TMP[:, 6, :], ACT.Sin).then_inc(disc_a, 1)
                step(2, 0)
                with act.Fori(1, (NF - 2) // 2) as i:
                    step(i * 2 + 1, 1)
                    step(i * 2 + 2, 0)
                f = NF - 1
                split_hi(1, f + wu, unit=uu.at(f - 1))
                split_hi(2, f + (down - 1), down=f + (down - 2))
                silu(f)
                split_hi(0, WEIGHTS["last" + which][1], unit=ug.at(f))
                uppers(f, 1)

            act.wait_ge(const_done, 3)

            def x_rms(s):
                src, m = (X[:, s, :], P) if s < S8 else (XD[:, :], DEC)
                act.wait_ge(x_in[s], 16)
                if s > 0:
                    act.wait_ge(sq_x, s)
                act.activation(JUNK[0:m, :], src, ACT.Square, accum_out=SS[0:m, s, 0:1]).then_inc(sq_x, 1)
                act.wait_ge(sq_x, s + 1)
                act.activation(RS[0:m, s:s + 1], SS[0:m, s, 0:1], ACT.Sqrt, bias=EPSC[0:m, :], scale=1.0 / D
                               ).then_inc(sqrt_x, 1)

            def x_spread(s):
                m = P if s < S8 else DEC
                spread(s, slice(s * P, s * P + m), x_bank(s)[0][:, 0:m])

            x_rms(0)
            x_rms(1)
            x_spread(0)
            split_hi(0, 0)
            for s in range(2, 4):
                x_rms(s)
                x_spread(s - 1)
            split_hi(1, 0)
            for i in range(DC):
                upper(0, i)
            x_rms(4)
            x_rms(5)
            x_spread(3)
            x_spread(4)
            x_spread(5)
            for i in range(DC, 2 * DC):
                upper(0, i)
            x_rms(6)
            x_rms(7)
            x_rms(8)
            for s in range(6, S8 + 1):
                x_spread(s)
            for i in range(2 * DC, XN):
                upper(0, i)
            ffn("1", DOWN1)
            split_hi(*WEIGHTS[("u", 0)], down=DOWN1 + NF - 2)
            split_hi(*WEIGHTS[("u", 1)], unit=UNITS["up1"].at(NF - 1))

            act.wait_ge(disc_p, 4)
            norm(1, NF - 1, [UNITS["gate1"].at(NF - 1), UNITS["up1"].at(NF - 1)])

            def evict(unit, tb, dst):
                act.wait_ge(banks_full[unit.slot], unit.full(tb))
                take(act, unit, tb)
                act.activation(dst[:, cols(tb)], AB[unit.slot][tb][:, 0:TW], ACT.Copy).then_inc(banks_free[unit.slot], 1)

            def next_split(name):
                i = WEIGHTED.index(name)
                slot, number = WEIGHTS[name]
                before = [w for w in WEIGHTED[:i] if WEIGHTS[w][0] == slot]
                k = WC if name[0] == "glu" else DC
                split_hi(slot, number, k, unit=UNITS[before[-1]])

            for j in range(WC):
                unit = UNITS[("u", j)]
                dst = (S, T)[j % 2]
                if j >= 2:
                    act.wait_ge(u_out[j - 2], 16)
                if j == 0:
                    split_hi(*WEIGHTS[("u", 2)], down=DOWN1 + NF - 1)
                    wait_xn(act, 1)
                for tb in range(TB):
                    evict(unit, tb, dst)
                if j == 0:
                    split_hi(2, DOWNC, unit=unit)
                else:
                    next_split(WEIGHTED[j + 2])
            act.wait_ge(down_full, last_tile(DOWN1 + NF - 1))
            for n in range(12):
                unit, b = UNITS[("tab", n // 3)], n % 3
                act.wait_ge(banks_full[unit.slot], unit.full(b))
                take(act, unit, b)
                if n < 8:
                    act.activation(WT[:, 2 * n:2 * n + 2, :, :].rearrange("p g r n -> p (g r n)"), AB[unit.slot][b][:, :],
                                   ACT.Copy).then_inc(banks_free[unit.slot], 1)
                else:
                    if n == 8:
                        act.wait_ge(disc_p, 5)
                    src = AB[unit.slot][b][0:32, :].rearrange("p (g n) -> p g n", n=P)
                    act.activation(KT[:, 4 * (n - 8):4 * (n - 7), 7 * C16:], src, ACT.Copy
                                   ).then_inc(banks_free[unit.slot], 1)
            unit = UNITS["carried"]
            act.wait_ge(banks_full[unit.slot], unit.full(2))
            take(act, unit)
            act.activation(CS[:, :, :].rearrange("p r n -> p (r n)"), AB[unit.slot][0][:, 0:2 * P], ACT.Copy
                           ).then_inc(banks_free[unit.slot], 3)
            unit = UNITS["buffer"]
            act.wait_ge(banks_full[unit.slot], unit.full(2))
            take(act, unit)
            act.activation(CBT[:, :, :].rearrange("p j n -> p (j n)"), AB[unit.slot][0][:, 0:64], ACT.Copy
                           ).then_inc(banks_free[unit.slot], 3)

            for c in range(WC):
                names = [("xc", c), ("gc", c), ("gb", c)]
                i = WEIGHTED.index(names[0])
                unit = UNITS[names[0]]
                if c == 0:
                    act.wait_ge(u_out[2], 16)
                    act.wait_ge(u_out[3], 16)
                else:
                    act.wait_ge(banks_free[UNITS[("gc", c - 1)].slot], UNITS[("gc", c - 1)].full(2))
                for tb in range(TB):
                    evict(unit, tb, S)
                next_split(WEIGHTED[i + 2])
                next_split(WEIGHTED[i + 3])
                unit = UNITS[("gb", c)]
                if c == 0:
                    act.wait_ge(xs_zero, 1)
                    for n, items in enumerate(V_BANKS):
                        vu, b = UNITS[("v", n // 3)], n % 3
                        act.wait_ge(banks_full[vu.slot], vu.full(b))
                        take(act, vu, b)
                        src = AB[vu.slot][b][:, 0:len(items) * YC].rearrange("p (q n) -> p q n", n=YC)
                        act.activation(XS[:, items[0]:items[-1] + 1, DEC + 1:XC], src, ACT.Copy
                                       ).then_inc(banks_free[vu.slot], 2 if n == len(V_BANKS) - 1 else 1)
                for tb in range(TB):
                    h_hi(DOWNC + c, c % 2, tb, (banks_free[unit.slot], unit.full(tb)))
                    if tb == 0 and c >= 1:
                        split_hi(2, DOWNC + c, down=DOWNC + c - 1)
                next_split(WEIGHTED[i + 4])
            for j in range(WC):
                unit = UNITS[("y", j)]
                if j >= 2:
                    act.wait_ge(z_out[j - 2], 16 * 9)
                for b, items in enumerate(Y_BANKS):
                    act.wait_ge(banks_full[unit.slot], unit.full(b))
                    take(act, unit, b)
                    act.activation(Z[:, j % 2, items[0]:items[-1] + 1, :].rearrange("p g n -> p (g n)"),
                                   AB[unit.slot][b][:, 0:len(items) * YC], ACT.Gelu_apprx_tanh
                                   ).then_inc(banks_free[unit.slot], 1)
            unit = UNITS["states"]
            act.wait_ge(banks_full[unit.slot], unit.full(2))
            take(act, unit)
            act.activation(STO[:, 0:2, :].rearrange("p r n -> p (r n)"), AB[unit.slot][0][:, 0:2 * P], ACT.Copy)
            act.activation(STO[0:GP, 2:4, :].rearrange("p r n -> p (r n)"), AB[unit.slot][0][0:GP, 2 * P:4 * P], ACT.Copy
                           ).then_inc(banks_free[unit.slot], 3)
            act.wait_ge(banks_free[unit.slot], unit.full(2))
            act.nop().then_inc(st_out, 1)
            unit = UNITS["vout"]
            act.wait_ge(banks_full[unit.slot], unit.full(2))
            take(act, unit)
            act.activation(VO[:, :], AB[unit.slot][0][0:16, :], ACT.Copy).then_inc(banks_free[unit.slot], 3)
            act.wait_ge(banks_free[unit.slot], unit.full(2))
            act.nop().then_inc(st_out, 1)
            y3 = UNITS[("y", 3)]
            for tb in range(TB):
                for j in range(WC):
                    if tb == 0:
                        act.wait_ge(zt_in[j], 16)
                        act.wait_ge(z_out[j], 16 * 9)
                    act.activation(ZH[:, j, cols(tb)], ZT[:, j, cols(tb)], ACT.Copy).then_inc(z_hi, 1)
            split_hi(2, DOWNS, down=DOWNS - 1)
            for j in range(WC):
                unit = UNITS[("glu", j)]
                for tb in range(TB):
                    act.wait_ge(banks_full[unit.slot], unit.full(tb))
                    if j > 0:
                        act.wait_ge(gate_done, 3 * (j - 1) + tb + 1)
                    take(act, unit, tb)
                    act.activation(S[:, cols(tb)], AB[unit.slot][tb][:, 0:TW], ACT.Sigmoid, bias=BG[:, j:j + 1]
                                   ).then_inc(banks_free[unit.slot], 1)
                for tb in range(TB):
                    h_hi(DOWNS + j, j % 2, tb, (gate_done, 3 * j + tb + 1))
                if j < 2:
                    next_split(("glu", j + 2))
                if j == 3:
                    split_hi(*WEIGHTS["last_s"], unit=UNITS[("glu", 3)])
                if j >= 1:
                    split_hi(2, DOWNS + j, down=DOWNS + j - 1)
                if j == 2:
                    split_hi(*WEIGHTS["gate2"], unit=UNITS[("glu", 2)])
            norm(2, DOWNS + 3, [UNITS[("glu", 3)]])
            ffn("2", DOWN2)

            act.wait_ge(h_ready, 3 * ND)
            for s in range(S8 + 1):
                m = NK if s < S8 else DEC
                act.wait_ge(out_full, s + 1)
                for h in range(2):
                    if s > 0 or h > 0:
                        act.wait_ge(sq_x, 9 + 2 * s + h)
                    act.activation(S[0:m, 0:512], OB[s % 3][h][0:m, :], ACT.Square, accum_out=SS[0:m, s, h:h + 1]
                                   ).then_inc(sq_x, 1)
                act.wait_ge(ss_sum, s + 1)
                act.activation(RS[0:m, s:s + 1], SS[0:m, s, 0:1], ACT.Sqrt, bias=EPSC[0:m, :], scale=1.0 / D
                               ).then_inc(sqrt_x, 1)

        @block.vector
        def _(dve):
            def f(t):
                return t.bitcast(F32)

            def split_lo(slot, n, k=DC, half=None):
                if half is not None:
                    span = slice(half * (D // 2), (half + 1) * (D // 2))
                    dve.wait_ge(w_hi[slot], n + 1)
                    ins = dve.tensor_tensor(WL[:, slot, span], RAW[:, slot, span], f(WH[:, slot, span]), ALU.subtract)
                    if half == 1:
                        ins.then_inc(w_split[slot], 1)
                    return
                dve.wait_ge(w_hi[slot], n + 1)
                dve.tensor_tensor(WL[:, slot, 0:k * P], RAW[:, slot, 0:k * P], f(WH[:, slot, 0:k * P]), ALU.subtract
                                  ).then_inc(w_split[slot], 1)

            def h_lo(d, par, tb):
                dve.wait_ge(hi_done, 3 * d + tb + 1)
                dve.tensor_tensor(HL[:, par, cols(tb)], T[:, cols(tb)], f(HH[:, par, cols(tb)]), ALU.subtract
                                  ).then_inc(h_ready, 1)

            def add_tile(d, tb, j, scale):
                dve.wait_ge(down_full, TILES * d + DC * tb + j + 1)
                ht = HT[:, j, cols(tb)]
                tile = down_bank(d, DC * tb + j)[0][:, 0:TW]
                if scale == 1.0:
                    ins = dve.tensor_tensor(ht, tile, ht, ALU.add)
                else:
                    ins = dve.scalar_tensor_tensor(ht, tile, scale, ht, ALU.mult, ALU.add)
                ins.then_inc(down_free, 1)

            def add_block(d, tb, scale=0.5, weights=None):
                for j in range(DC):
                    add_tile(d, tb, j, scale)
                    if weights is not None and j in (2, 6):
                        split_lo(*weights, half=0 if j == 2 else 1)

            def scaled(k, i):
                tb, c = divmod(i, DC)
                if i >= 6:
                    dve.wait_ge(*low_count(k, i - 6))
                dve.scalar_tensor_tensor(ring(i), HT[:, c, cols(tb)], GAIN[:, k, c:c + 1], R[:, cols(tb)], ALU.mult,
                                         ALU.mult).then_inc(xn_tmp, 1)

            def lower(k, i):
                tb, c = divmod(i, DC)
                dve.wait_ge(xn_hi, XN * k + i + 1)
                dve.tensor_tensor(XL[:, c, cols(tb)], ring(i), f(XH[:, c, cols(tb)]), ALU.subtract
                                  ).then_inc(xn_low[1], 1)

            def normalised(k, tb, after={}):
                for i in range(DC * tb, DC * (tb + 1) + 1):
                    if i < DC * (tb + 1):
                        scaled(k, i)
                    if i > DC * tb and by_dve(i - 1):
                        lower(k, i - 1)
                    if i in after:
                        after[i]()

            def norm(k, d, scale, splits=()):
                def diagonals(tb):
                    n = TB * (k - 1) + tb
                    dve.wait_ge(rt_done, n + 1)
                    dve.reciprocal(RQ[:, n, :], RQ[:, n, :]).then_inc(rcp_done, 1)
                    dve.wait_ge(rcp_done, n + 1)
                    for q in range(4):
                        at = tb * TW + q * QW
                        dve.tensor_scalar(R[0:QW, at:at + QW], IDENT[0:QW, 0:QW], RQ[:, n, q:q + 1], None, ALU.mult
                                          ).then_inc(diag_done, 1)

                for tb in range(TB):
                    for j in range(DC):
                        add_tile(d, tb, j, scale)
                        if tb == 0 and j in (1, 3) and k == 1:
                            h_lo(d, 1, (j + 1) // 2)
                        if tb == 1 and j == 5:
                            diagonals(0)
                    if tb == 0:
                        for name in splits:
                            split_lo(*WEIGHTS[name])
                dve.wait_ge(h_ready, 3 * d + 3)
                dve.wait_ge(gains_in, 32)
                for tb in range(TB):
                    dve.wait_ge(spread_free, S8 + 1 + TB * (k - 1) + tb + 1)
                    normalised(k, tb, {5: lambda: diagonals(1)} if tb == 0 else {})
                    if tb == 0:
                        diagonals(2)

            def ffn(which, down):
                ug, uu = UNITS["gate" + which], UNITS["up" + which]
                wg, wu = GATE[which], UP[which]

                def mul(n, tb):
                    if isinstance(n, int) and n == 0:
                        take(dve, uu, tb)
                    dve.wait_ge(banks_full[1], uu.at(n).full(tb))
                    dve.wait_ge(banks_free[0], ug.at(n).full(tb))
                    if not (isinstance(n, int) and n == 0):
                        dve.wait_ge(h_ready, 3 * (n + (down - 1)) + tb + 1)
                    else:
                        wait_xn(dve, 0 if down == 0 else 2)
                    dve.tensor_tensor(T[:, cols(tb)], AB[1][tb][:, 0:TW], S[:, cols(tb)], ALU.mult
                                      ).then_inc(banks_free[1], 1)

                def step(n, par):
                    split_lo(1, n + wu)
                    split_lo(2, n + (down - 1))
                    for tb in range(TB):
                        add_block(n + (down - 1), tb, weights=(0, n + (wg + 1)) if tb == 1 else None)
                        mul(n, tb)
                    for tb in range(TB):
                        h_lo(n + down, par, tb)

                for tb in range(TB):
                    if tb == 2:
                        split_lo(0, wg + 1)
                    mul(0, tb)
                for tb in range(TB):
                    h_lo(down, 0, tb)
                if down == 0:
                    parameters()
                step(1, 1)
                if down == 0:
                    dve.wait_ge(disc_p, 2)
                    dve.reciprocal(TMP[:, 12, :], TMP[:, 7, :]).then_inc(den_inv, 1)
                step(2, 0)
                with dve.Fori(1, (NF - 2) // 2) as i:
                    step(i * 2 + 1, 1)
                    step(i * 2 + 2, 0)
                n = NF - 1
                split_lo(1, n + wu)
                split_lo(2, n + down - 1)
                for tb in range(TB):
                    add_block(n + down - 1, tb, weights=WEIGHTS["last" + which] if tb == 1 else None)
                    mul(n, tb)
                    if tb == 1:
                        h_lo(n + down, 1, 0)

            def parameters():
                dve.wait_ge(par_full, 1)
                for n in range(3):
                    last = dve.tensor_copy(LRI[:, n, :], DB[0][:, 32 * n:32 * n + GP])
                    last.then_inc(lri_done, 1)
                dve.wait_ge(lri_done, 3)
                dve.nop().then_inc(par_free, 1)
                for ri in range(2):
                    dve.wait_ge(par_full, 2 + ri)
                    for g2 in range(2):
                        half = slice(g2 * NS, (g2 + 1) * NS)
                        src = DB[1 - ri][half, :].rearrange("p (g e c) -> p g e c", e=2, c=C16)[:, :, g2, :]
                        dve.tensor_scalar(CA[half, :, ri, 0:C16], src, (1.0, -1.0)[ri], None, ALU.mult).then_inc(c_done, 1)
                    dve.wait_ge(c_done, 2 * ri + 2)
                    dve.nop().then_inc(par_free, 1)

            dve.wait_ge(const_done, 3)

            def x_tile(s):
                for h in range(2):
                    dve.wait_ge(xt_full, 2 * s + h + 1)
                    m = P if s < S8 else DEC
                    dve.tensor_copy(HT[:, 4 * h:4 * h + 4, s * P:s * P + m],
                                    DB[h][:, 0:4 * m].rearrange("p (c n) -> p c n", n=m)).then_inc(xt_free, 1)
                dve.wait_ge(sqrt_x, s + 1)
                dve.reciprocal(RS[0:m, s:s + 1], RS[0:m, s:s + 1]).then_inc(rcp_x, 1)
                dve.wait_ge(rcp_x, s + 1)
                dve.tensor_scalar(R[0:m, s * P:s * P + m], IDENT[0:m, 0:m], RS[0:m, s:s + 1], None, ALU.mult
                                  ).then_inc(diag_x, 1)

            def x_scaled(tb, last_tile):
                if tb == 0:
                    dve.wait_ge(gain_in, 16)
                dve.wait_ge(spread_free, last_tile + 1)
                dve.wait_ge(xt_free, 2 * last_tile + 2)
                normalised(0, tb)

            x_tile(0)
            x_tile(1)
            split_lo(0, 0)
            for s in range(2, 4):
                x_tile(s)
            x_scaled(0, 2)
            x_tile(4)
            x_tile(5)
            x_scaled(1, 5)
            x_tile(6)
            x_tile(7)
            x_tile(8)
            x_scaled(2, 8)

            ffn("1", DOWN1)
            norm(1, DOWN1 + NF - 1, 0.5, [("u", 0), ("u", 1)])

            def next_lo(name):
                split_lo(*WEIGHTS[name], WC if name[0] == "glu" else DC)

            for j in range(WC):
                next_lo(WEIGHTED[j + 2])
                if j == 0:
                    split_lo(2, DOWNC)

            unit = UNITS[("tab", 3)]
            dve.wait_ge(banks_free[unit.slot], unit.full(2))
            dve.tensor_tensor(DTM[:, :, :], DM[:, :].rearrange("p (o c) -> p o c", o=1).broadcast_to([32, GP, C16]),
                              DT[:, :].rearrange("p (g o) -> p g o", o=1).broadcast_to([32, GP, C16]), ALU.mult
                              ).then_inc(kt_done, 1)
            dve.wait_ge(kt_done, 1)
            skip = KT[:, :, 7 * C16:8 * C16]
            dve.tensor_tensor(skip, skip, DTM[:, :, :], ALU.add).then_inc(dt_k, 1)

            vb = UNITS["buffer"]
            steps = [0]

            def step_done(ins):
                steps[0] += 1
                ins.then_inc(conv_step, 1)
                dve.wait_ge(conv_step, steps[0])

            def taps(k):
                return CW[:, k, c:c + 1]

            for c in range(WC):
                i = WEIGHTED.index(("xc", c))
                xu, gu, bu = UNITS[("xc", c)], UNITS[("gc", c)], UNITS[("gb", c)]
                if c == 0:
                    dve.wait_ge(banks_full[vb.slot], vb.full(2))
                for tb in range(TB):
                    if c > 0:
                        add_block(DOWNC + c - 1, tb, 1.0, WEIGHTS[WEIGHTED[i + 2]] if tb == 1 else None)
                    dve.wait_ge(banks_full[gu.slot], gu.full(tb))
                    dve.wait_ge(banks_free[xu.slot], xu.full(tb))
                    if c > 0:
                        dve.wait_ge(h_ready, 3 * (DOWNC + c - 1) + 3)
                    take(dve, gu, tb)
                    dve.tensor_tensor(V[:, cols(tb)], AB[gu.slot][tb][:, 0:TW], S[:, cols(tb)], ALU.mult
                                      ).then_inc(banks_free[gu.slot], 1)
                    if tb == 0 and c == 0:
                        next_lo(WEIGHTED[i + 2])
                next_lo(WEIGHTED[i + 3])
                dve.wait_ge(banks_free[gu.slot], gu.full(2))
                if c == 0:
                    dve.wait_ge(u_out[3], 16)
                    dve.wait_ge(banks_free[vb.slot], vb.full(2))
                    dve.wait_ge(xs_zero, 1)
                step_done(dve.tensor_copy(VPRE[:, :, 1:NK],
                                          V[:, 6 * NK:SEQ].rearrange("p (s k) -> p s k", k=NK)[:, :, 0:NK - 1]))
                step_done(dve.tensor_copy(VOUT[:, c, 0:DEC], V[:, SEQ:NT]))
                step_done(dve.tensor_copy(VOUT[:, c, DEC:DEC + 2],
                                          V[:, 6 * NK:SEQ].rearrange("p (s k) -> p s k", k=NK)[:, :, NK - 1]))
                step_done(dve.tensor_scalar(T[:, :], V[:, :], taps(2), None, ALU.mult))

                def tap(dst, src, k):
                    step_done(dve.scalar_tensor_tensor(dst, src, taps(k), dst, ALU.mult, ALU.add))
                tap(T[:, NK:SEQ], V[:, 0:SEQ - NK], 1)
                tap(T[:, 0:NK], VPRE[:, 1, :], 1)
                tap(T[:, 2 * NK:SEQ], V[:, 0:SEQ - 2 * NK], 0)
                tap(T[:, 0:2 * NK], VPRE[:, :, :].rearrange("p s k -> p (s k)"), 0)
                buf = CBT[:, c, :].rearrange("p (b r) -> p b r", r=2)
                tap(T[:, SEQ:NT], buf[:, :, 1], 1)
                tap(T[:, SEQ:NT], buf[:, :, 0], 0)
                for tb in range(TB):
                    dve.wait_ge(banks_full[bu.slot], bu.full(tb))
                    take(dve, bu, tb)
                    dve.tensor_tensor(T[:, cols(tb)], AB[bu.slot][tb][:, 0:TW], T[:, cols(tb)], ALU.mult
                                      ).then_inc(banks_free[bu.slot], 1)
                    if tb == 1 and c >= 1:
                        split_lo(2, DOWNC + c)
                    if tb >= 1 and c >= 1:
                        h_lo(DOWNC + c, c % 2, tb - 1)
                for tb in range(TB) if c == 0 else (TB - 1,):
                    h_lo(DOWNC + c, c % 2, tb)
                if c < WC - 1:
                    next_lo(WEIGHTED[i + 4])
            def z_lo(tb, j):
                dve.wait_ge(z_hi, WC * tb + j + 1)
                dve.tensor_tensor(ZL[:, j, cols(tb)], ZT[:, j, cols(tb)], f(ZH[:, j, cols(tb)]), ALU.subtract
                                  ).then_inc(z_ready, 1)

            add_block(DOWNC + 3, 0, 1.0)
            next_lo(("glu", 1))
            add_block(DOWNC + 3, 1, 1.0)
            for j in range(DC):
                add_tile(DOWNC + 3, 2, j, 1.0)
                if j in (5, 6, 7):
                    z_lo(0, j - 5)
            for tb in range(TB):
                for j in range(3 if tb == 0 else 0, WC):
                    z_lo(tb, j)
            split_lo(2, DOWNS)
            for j in range(WC):
                unit = UNITS[("glu", j)]
                for tb in range(TB):
                    dve.wait_ge(banks_free[unit.slot], unit.full(tb))
                    dve.wait_ge(h_ready, 3 * (DOWNS + j - 1) + tb + 1)
                    dve.tensor_tensor(T[:, cols(tb)], S[:, cols(tb)], ZT[:, j, cols(tb)], ALU.mult
                                      ).then_inc(gate_done, 1)
                if j >= 1:
                    add_block(DOWNS + j - 1, 0, 1.0)
                for tb in range(TB):
                    h_lo(DOWNS + j, j % 2, tb)
                if j < 2:
                    next_lo(("glu", j + 2))
                if j >= 1:
                    add_block(DOWNS + j - 1, 1, 1.0)
                    if j == 3:
                        split_lo(*WEIGHTS["last_s"])
                    add_block(DOWNS + j - 1, 2, 1.0)
                    split_lo(2, DOWNS + j)
                if j == 2:
                    split_lo(*WEIGHTS["gate2"])
            norm(2, DOWNS + 3, 1.0)
            ffn("2", DOWN2)
            def out_sum(s):
                m = NK if s < S8 else DEC
                dve.wait_ge(sq_x, 9 + 2 * s + 2)
                dve.tensor_tensor(SS[0:m, s, 0:1], SS[0:m, s, 0:1], SS[0:m, s, 1:2], ALU.add).then_inc(ss_sum, 1)

            def out_tile(s):
                m = NK if s < S8 else DEC
                dve.wait_ge(sqrt_x, 9 + s + 1)
                dve.reciprocal(RS[0:m, s:s + 1], RS[0:m, s:s + 1]).then_inc(rcp_x, 1)
                dve.wait_ge(rcp_x, 9 + s + 1)
                if s >= 4:
                    dve.wait_ge(y_out[s % 4], 16 * (s // 4))
                for h in range(2):
                    span = slice(512 * h, 512 * (h + 1))
                    dve.scalar_tensor_tensor(OUT[0:m, s % 4, span], OB[s % 3][h][0:m, :], RS[0:m, s:s + 1],
                                             GF[0:m, span], ALU.mult, ALU.mult).then_inc(out_done, 1)
                dve.wait_ge(out_done, 2 * s + 2)
                dve.nop().then_inc(out_free, 1)

            d = DOWN2 + NF - 1
            for tb in range(TB):
                for j in range(DC):
                    add_tile(d, tb, j, 0.5)
                    if tb == 0 and j in (1, 3):
                        h_lo(d, 1, (j + 1) // 2)
                    if tb == 2 and j == 3:
                        out_sum(0)
                    if tb == 2 and j == 6:
                        out_sum(1)
            dve.wait_ge(gf_in, 16)
            out_tile(0)
            out_tile(1)
            for s in range(2, S8 + 1):
                out_sum(s)
                out_tile(s)

        @block.gpsimd
        def _(pool):
            count = [0]

            def chain(ins):
                count[0] += 1
                ins.then_inc(pool_step, 1)
                pool.wait_ge(pool_step, count[0])

            chain(pool.memset(IDENT[:, :], 0.0))
            pool.affine_select(out=IDENT[:, :], in_=IDENT[:, :], compare_op=ALU.not_equal, fill=1.0, base=0,
                               pattern=[[-1, P]], channel_multiplier=1).then_inc(const_done, 1)
            pool.memset(ONES[:, :], 1.0).then_inc(const_done, 1)
            pool.memset(EPSC[:, :], EPS).then_inc(const_done, 1)
            pool.memset(VOUT[:, :, :], 0.0)
            with nc.allow_non_contiguous_dma(reason="small parameters, channels to partitions"):
                pool.dma_start(GAIN[:, 0, :], a["ffn1_norm"][0].rearrange("(c p) -> p c", p=P)).then_inc(gain_in, 16)
            chain(pool.memset(PAR[:, :], 0.0))
            pool.dma_start(PAR[0:GP, :], a["ssm_lambda_re"][0].rearrange("(g e) p -> g (e p)", e=2)).then_inc(par_in, 16)
            pool.dma_start(PAR[32:32 + GP, :], a["ssm_lambda_im"][0].rearrange("(g e) p -> g (e p)", e=2)
                           ).then_inc(par_in, 16)
            pool.dma_start(TMP[64:64 + GP, 0, 0:2], a["ssm_log_dt"][0].rearrange("(g e) -> g e", e=2)).then_inc(dt_in, 16)

            def lower(k, first, last):
                for i in range(first, last):
                    if by_dve(i):
                        continue
                    tb, c = divmod(i, DC)
                    pool.wait_ge(xn_hi, XN * k + i + 1)
                    pool.tensor_tensor(XL[:, c, cols(tb)], ring(i), XH[:, c, cols(tb)].bitcast(F32), ALU.subtract
                                       ).then_inc(xn_low[0], 1)
                pool.wait_ge(*low_count(k, last - 1 if not by_dve(last - 1) else last - 2))

            def norm(k):
                for tb in range(TB):
                    for c in range(1, DC):
                        i, n = DC * tb + c, TB * (k - 1) + tb
                        pool.wait_ge(sq_done, XN * (k - 1) + i + 1)
                        square = lambda j: SQ[:, (j % 3) * TW:(j % 3 + 1) * TW]
                        if c == 1:
                            ins = pool.tensor_tensor(R[:, cols(tb)], square(i - 1), square(i), ALU.add)
                        else:
                            pool.wait_ge(acc_done, (DC - 1) * n + c - 1)
                            ins = pool.tensor_tensor(R[:, cols(tb)], R[:, cols(tb)], square(i), ALU.add)
                        ins.then_inc(acc_done, 1)
                lower(k, 0, XN)

            pool.wait_ge(w_hi[1], 1)
            pool.tensor_tensor(WL[:, 1, :], RAW[:, 1, :], WH[:, 1, :].bitcast(F32), ALU.subtract).then_inc(w_split[1], 1)
            pool.wait_ge(w_split[1], 1)
            lower(0, 0, 2 * DC)
            pool.wait_ge(par_in, 32)
            pool.nop().then_inc(par_set, 1)
            pool.wait_ge(dt_in, 16)
            for e in range(2):
                pool.tensor_copy(PAR[64:64 + GP, e * NS:(e + 1) * NS],
                                 TMP[64:64 + GP, 0, e:e + 1].broadcast_to([GP, NS])).then_inc(par_set, 1)
            pool.wait_ge(par_set, 3)
            pool.wait_ge(xt_full, 2 * (S8 + 1))
            pool.wait_ge(sq_x, S8 + 1)
            for ri, name in enumerate(("ssm_c_re", "ssm_c_im")):
                src = a[name][0].rearrange("(q g) c p -> (g c) q p", q=4)
                for twice in range(2):
                    pool.dma_start(CL[:, ri, :, twice * NS:(twice + 1) * NS], src).then_inc(c_in, 16)
            lower(0, 2 * DC, XN)
            with nc.allow_non_contiguous_dma(reason="small parameters, channels to partitions"):
                for n, name in ((1, "mix_norm"), (2, "ffn2_norm")):
                    pool.dma_start(GAIN[:, n, :], a[name][0].rearrange("(c p) -> p c", p=P)).then_inc(gains_in, 16)
                pool.dma_start(CW[:, :, :], a["conv_w"][0].rearrange("k (c p) -> p k c", p=P)).then_inc(consts_in, 16)
                pool.dma_start(BG[:, :], a["ssm_b_glu"][0].rearrange("(c p) -> p c", p=P)).then_inc(consts_in, 16)
                pool.dma_start(DT[:, :], a["ssm_d"][0].rearrange("(g n) -> n g", n=32)).then_inc(consts_in, 16)
            for ri, name in enumerate(("ssm_b_re", "ssm_b_im")):
                pool.dma_start(BRAW[:, ri, :, :], a[name][0].rearrange("(g e) p c -> (e p) g c", e=2)).then_inc(b_in, 16)
            t = lambda n: TMP[:, n, :]

            def tt(out, x, y, op):
                chain(pool.tensor_tensor(out, x, y, op))

            def ts(out, x, s1, op1, s2=None, op2=None):
                if op2 is None:
                    chain(pool.tensor_scalar(out, x, s1, None, op1))
                else:
                    chain(pool.tensor_scalar(out, x, s1, s2, op1, op2))

            lr, li = LRI[:, 0, :], LRI[:, 1, :]
            pool.wait_ge(disc_a, 1)
            tt(t(1), lr, t(0), ALU.mult)
            tt(t(2), li, t(0), ALU.mult)
            ts(t(7), t(2), 1.0 / TWO_PI, ALU.mult)
            ts(t(7), t(7), MAGIC, ALU.add)
            ts(t(7), t(7), MAGIC, ALU.subtract)
            for part in (PI_A, PI_B, PI_C):
                ts(t(8), t(7), part, ALU.mult)
                tt(t(2), t(2), t(8), ALU.subtract)
            ts(t(2), t(2), 3.1415925, ALU.min, -3.1415925, ALU.max)
            ts(t(8), t(2), -1.0, ALU.mult)
            chain(pool.tensor_scalar(t(9), t(2), 0.0, None, ALU.max))
            chain(pool.tensor_scalar(t(8), t(8), 0.0, None, ALU.max))
            tt(t(6), t(9), t(8), ALU.add)
            ts(t(6), t(6), -1.0, ALU.mult, float(np.pi / 2), ALU.add)
            pool.nop().then_inc(disc_p, 1)
            pool.wait_ge(disc_a, 4)
            ar, ai, nai = AP8[:, 7, 0, :], AP8[:, 7, 1, :], AP8[:, 7, 2, :]
            tt(ar, t(3), t(5), ALU.mult)
            tt(ai, t(3), t(4), ALU.mult)
            tt(t(7), lr, lr, ALU.mult)
            tt(t(8), li, li, ALU.mult)
            tt(t(7), t(7), t(8), ALU.add)
            pool.nop().then_inc(disc_p, 1)
            ts(t(8), ar, -1.0, ALU.add)
            tt(t(9), t(8), lr, ALU.mult)
            tt(t(10), ai, li, ALU.mult)
            tt(t(9), t(9), t(10), ALU.add)
            tt(t(10), ai, lr, ALU.mult)
            tt(t(11), t(8), li, ALU.mult)
            tt(t(10), t(10), t(11), ALU.subtract)
            pool.wait_ge(den_inv, 1)
            tt(t(9), t(9), t(12), ALU.mult)
            tt(t(10), t(10), t(12), ALU.mult)
            pool.wait_ge(b_in, 32)
            pool.wait_ge(c_done, 4)

            def over(x, n=C16):
                return x.rearrange("p (g o) -> p g o", o=1).broadcast_to([P, GP, n])

            D1 = PROD[:, 0]
            D2 = PROD[:, 1]
            br, bi = BRAW[:, 0], BRAW[:, 1]

            def bs(ri, s):
                return BS[:, :, ri, s * C16:(s + 1) * C16]

            def ca(ri, j):
                return CA[:, :, ri, j * C16:(j + 1) * C16]

            def rotate(out_r, out_i, in_r, in_i, cr, ci, sign):
                tt(D1, in_r, over(cr), ALU.mult)
                tt(D2, in_i, over(ci), ALU.mult)
                tt(out_r, D1, D2, ALU.subtract if sign == 1 else ALU.add)
                tt(D1, in_i, over(cr), ALU.mult)
                tt(D2, in_r, over(ci), ALU.mult)
                tt(out_i, D1, D2, ALU.add if sign == 1 else ALU.subtract)

            rotate(bs(0, 7), bs(1, 7), br, bi, t(9), t(10), 1)
            for s in range(6, -1, -1):
                rotate(bs(0, s), bs(1, s), bs(0, s + 1), bs(1, s + 1), ar, ai, 1)
            for j in range(1, 9):
                rotate(ca(0, j), ca(1, j), ca(0, j - 1), ca(1, j - 1), ar, ai, -1)
            chain(pool.memset(BD[:, :, :, :], 0.0))
            for ri in range(2):
                chain(pool.tensor_copy(BD[0:NS, :, ri, 0:C16], BS[0:NS, :, ri, 7 * C16:]))
                chain(pool.tensor_copy(BD[NS:P, :, ri, C16:], BS[NS:P, :, ri, 7 * C16:]))
            pool.dma_start(CAD, CA[:, :, :, :].rearrange("p g r n -> p (g r) n")).then_inc(ca_out, 16)

            def square_of(x, out_r, out_i):
                tt(t(0), x[0], x[0], ALU.mult)
                tt(t(1), x[1], x[1], ALU.mult)
                tt(t(2), x[0], x[1], ALU.mult)
                tt(out_r, t(0), t(1), ALU.subtract)
                tt(out_i, t(2), t(2), ALU.add)
            chain(pool.tensor_copy(t(12), ar))
            chain(pool.tensor_copy(t(13), ai))
            square_of((ar, ai), t(3), t(4))
            square_of((t(3), t(4)), t(5), t(6))
            square_of((t(5), t(6)), AP8[:, 0, 0, :], AP8[:, 0, 1, :])
            for i in range(1, 8):
                x, y = (AP8[:, i - 1, 0, :], AP8[:, i - 1, 1, :]), (AP8[:, 0, 0, :], AP8[:, 0, 1, :])
                tt(t(0), x[0], y[0], ALU.mult)
                tt(t(1), x[1], y[1], ALU.mult)
                tt(AP8[:, i, 0, :], t(0), t(1), ALU.subtract)
                tt(t(0), x[0], y[1], ALU.mult)
                tt(t(1), x[1], y[0], ALU.mult)
                tt(AP8[:, i, 1, :], t(0), t(1), ALU.add)
            chain(pool.tensor_scalar(AP8[:, :, 2, :], AP8[:, :, 1, :], -1.0, None, ALU.mult))
            ts(t(11), t(13), -1.0, ALU.mult)
            tt(DM[:, :], IDENT[0:32, 0:C16], IDENT[0:32, C16:32], ALU.add)
            pool.wait_ge(consts_in, 16 * 3)
            pool.nop().then_inc(disc_p, 2)
            norm(1)
            tab = UNITS[("tab", 2)]
            pool.wait_ge(banks_full[tab.slot], tab.full(1))
            pool.wait_ge(ca_out, 16)
            chain(pool.memset(KT[:, :, 0:7 * C16], 0.0))
            pool.nop().then_inc(disc_p, 1)
            tab = UNITS[("tab", 3)]
            pool.wait_ge(banks_full[tab.slot], tab.full(2))
            pool.memset(U[:, :, 0:DEC], 0.0)
            chain(pool.memset(U[:, :, DEC + NK:UC], 0.0))
            pool.nop().then_inc(u_zero, 1)
            pool.wait_ge(t0_out, 16 * 16)
            pool.memset(XS[:, :, DEC:DEC + 1], 0.0)
            chain(pool.memset(VPRE[:, :, 0:1], 0.0))
            carried = UNITS["carried"]
            pool.wait_ge(banks_free[carried.slot], carried.full(2))
            for ri in range(2):
                chain(pool.tensor_copy(XS[:, ri * GP:(ri + 1) * GP, 0:DEC],
                                       CS[:, ri, :].rearrange("p (t g) -> p g t", g=GP)))
            pool.nop().then_inc(xs_zero, 1)

            v3 = UNITS[("v", 3)]
            pool.wait_ge(banks_free[v3.slot], v3.full(2))
            v2 = UNITS[("v", 2)]
            pool.wait_ge(banks_free[v2.slot], v2.full(2))
            main = XS[:, :, DEC + 1:DEC + 1 + NK].rearrange("p g (b i) -> p g b i", i=8)

            def power(i, what, n, both):
                x = (AP8[:, i, what, :] if i >= 0 else t({0: 12, 1: 13, 2: 11}[what]))
                x = x.rearrange("p (r g o) -> p r g o", r=1, o=1)
                return x.broadcast_to([P, 2, GP, n]) if both else x[:, 0].broadcast_to([P, GP, n])

            def advance(dst, src, i, n):
                t1, t2 = ST1[:, :, :, 0:n], ST2[:, :, :, 0:n]
                halves = (slice(0, GP), slice(GP, 2 * GP))
                src4 = src.rearrange("p (r g) n -> p r g n", r=2)
                dst4 = dst.rearrange("p (r g) n -> p r g n", r=2)
                pool.tensor_tensor(t1, src4, power(i, 0, n, True), ALU.mult).then_inc(pool_step, 1)
                pool.tensor_tensor(t2[:, 0], src[:, halves[1], :], power(i, 2, n, False), ALU.mult).then_inc(pool_step, 1)
                count[0] += 2
                tt(t2[:, 1], src[:, halves[0], :], power(i, 1, n, False), ALU.mult)
                tt(dst4, dst4, t1, ALU.add)
                tt(dst4, dst4, t2, ALU.add)

            for i in range(1, 8):
                advance(main[:, :, :, i], main[:, :, :, i - 1], 0, 16)
            for b in range(1, 16):
                advance(main[:, :, b, 7:8], main[:, :, b - 1, 7:8], 7, 1)
            for i in range(7):
                advance(main[:, :, 1:16, i], main[:, :, 0:15, 7], i, 15)
            advance(XS[:, :, XC - DEC:XC], XS[:, :, 0:DEC], -1, DEC)
            for ri in range(2):
                chain(pool.tensor_copy(DNEW[:, ri, :].rearrange("p (t g) -> p g t", g=GP),
                                       XS[:, ri * GP:(ri + 1) * GP, XC - DEC:XC]))
            pool.nop().then_inc(scanned, 1)
            last = UNITS[("gb", 3)]
            pool.wait_ge(banks_full[last.slot], last.full(2))
            for j in range(WC):
                for g2 in range(2):
                    pool.memset(CB[g2 * NS:(g2 + 1) * NS, 4 * j:4 * j + 4, :, 1 - g2, :], 0.0).then_inc(cb_zero, 1)
            pool.wait_ge(cb_zero, 2 * WC)
            pool.wait_ge(conv_step, 10 * WC)
            norm(2)


_OUTS = [("y_prompt", (1, SEQ, D)), ("y_sample", (DEC, 1, D)), ("re_prompt", (1, 1, G, NS)), ("im_prompt", (1, 1, G, NS)),
         ("conv_prompt", (1, 1, 2, W)), ("re_sample", (1, DEC, G, NS)), ("im_sample", (1, DEC, G, NS)),
         ("conv_sample", (1, DEC, 2, W))]


def kernel(**inputs):
    import concourse.bacc as bacc
    from concourse.bass_utils import run_bass_kernel_spmd

    nc = bacc.Bacc("TRN2", target_bir_lowering=False, num_devices=1)
    arrays, ins, outs = {}, {}, {}
    for name, value in inputs.items():
        arrays["in_" + name] = np.ascontiguousarray(value)
        ins[name] = nc.dram_tensor("in_" + name, arrays["in_" + name].shape, F32, kind="ExternalInput").ap()
    for name, shape in _OUTS:
        outs[name] = nc.dram_tensor("out_" + name, shape, F32, kind="ExternalOutput").ap()
    hybrid_trunk(nc, ins, outs)
    result = run_bass_kernel_spmd(nc, [arrays], core_ids=[0]).results[0]
    return tuple(result["out_" + name] for name, _ in _OUTS)
```
